# Optimizing a Trainium2 kernel written in Bass

```python
import math
import jax, jax.numpy as jnp
from jax import lax
import numpy as np

D_MODEL = 1024
BATCH = 1
SEQ = 256
DEPTH = 2

N_MEM = 256
HEAD_DIM = 64
MIX_WIDTH = 3 * D_MODEL // 4
MIX_HEADS = MIX_WIDTH // HEAD_DIM
MEM_HEADS = 4
MEM_WIDTH = MEM_HEADS * HEAD_DIM
NSA_KV_GROUPS = 4
NSA_GROUP_SIZE = MIX_HEADS // NSA_KV_GROUPS
KV_WIDTH = NSA_KV_GROUPS * HEAD_DIM
CMP_BLOCK = 32
CMP_STRIDE = 16
CMP_HIDDEN = 2 * HEAD_DIM
SEL_BLOCK = 64
SEL_TOPN = 16
WINDOW = 512
NSA_Q_BLOCK = 64
FORCE_SCORE = 1.0e4
NSA_IN = MIX_WIDTH + 6 * KV_WIDTH + 3 * MIX_HEADS + MEM_WIDTH
DECAY_LORA = 64
ICLR_LORA = 64
GATE_LORA = 160
RW_SHIFT = 3 * MIX_WIDTH + DECAY_LORA + ICLR_LORA + GATE_LORA
RW_IN = RW_SHIFT + MEM_WIDTH
GN_EPS = 64e-5
FFN_HIDDEN = -(-8 * D_MODEL // (3 * 256)) * 256
N_NSA = (DEPTH + 1) // 2
N_RWKV = DEPTH // 2
RMS_EPS = 1e-6
NEG_INF = -1e30


def _rmsnorm(x, g):
    xf = x.astype(jnp.float32)
    y = xf * lax.rsqrt(jnp.mean(xf * xf, axis=-1, keepdims=True) + RMS_EPS)
    return (y * g.astype(jnp.float32)).astype(x.dtype)

def _split(x, sizes):
    idx = [int(i) for i in np.cumsum(sizes)[:-1]]
    return jnp.split(x, idx, axis=-1)

def _alibi_slopes(n):
    def pow2(m):
        start = 2.0 ** (-8.0 / m)
        return [start ** (i + 1) for i in range(m)]
    c = 2 ** int(math.floor(math.log2(n)))
    s = pow2(c)
    if c < n:
        s = s + pow2(2 * c)[0::2][: n - c]
    return np.asarray(s, dtype=np.float32)

def _masked_softmax(s, mask):
    p = jax.nn.softmax(jnp.where(mask, s, NEG_INF), axis=-1)
    return p * mask

def _compress(kv, pos, w1, w2):
    S = kv.shape[1]
    n_cmp = (S - CMP_BLOCK) // CMP_STRIDE + 1
    idx = jnp.arange(n_cmp)[:, None] * CMP_STRIDE + jnp.arange(CMP_BLOCK)[None, :]
    blocks = kv[:, idx] + pos[None, None, :, None, :]
    hid = jax.nn.gelu(jnp.einsum('bnlgd,lde->bnge', blocks, w1))
    return jnp.einsum('bnge,ed->bngd', hid, w2)

def _nsa_mixer(h, w_in, gate_b, cmp_pos, cmp_w1, cmp_w2):
    B, S, _ = h.shape
    G, R, Dh, QB = NSA_KV_GROUPS, NSA_GROUP_SIZE, HEAD_DIM, NSA_Q_BLOCK
    proj = h @ w_in
    q, kc, vc, ks, vs, kw, vw, gl, q_mem = _split(
        proj, [MIX_WIDTH] + [KV_WIDTH] * 6 + [3 * MIX_HEADS, MEM_WIDTH])
    q = q.reshape(B, S, G, R, Dh)
    kc, vc, ks, vs, kw, vw = (t.reshape(B, S, G, Dh) for t in (kc, vc, ks, vs, kw, vw))
    gates = jax.nn.sigmoid(gl + gate_b).reshape(B, S, 3, G, R)

    kc_b = _compress(kc, cmp_pos[0], cmp_w1[0], cmp_w2[0])
    vc_b = _compress(vc, cmp_pos[1], cmp_w1[1], cmp_w2[1])
    n_cmp = kc_b.shape[1]
    n_blk = S // SEL_BLOCK
    n_sel = min(SEL_TOPN, n_blk)
    ks_blk = ks.reshape(B, n_blk, SEL_BLOCK, G, Dh).transpose(0, 3, 1, 2, 4)
    vs_blk = vs.reshape(B, n_blk, SEL_BLOCK, G, Dh).transpose(0, 3, 1, 2, 4)
    kw_pad = jnp.pad(kw, ((0, 0), (WINDOW, 0), (0, 0), (0, 0)))
    vw_pad = jnp.pad(vw, ((0, 0), (WINDOW, 0), (0, 0), (0, 0)))

    slopes = jnp.asarray(_alibi_slopes(MIX_HEADS).reshape(G, R))[None, :, :, None, None]
    cmp_start = jnp.arange(n_cmp) * CMP_STRIDE
    cmp_end = cmp_start + CMP_BLOCK - 1
    sel_start = jnp.arange(n_blk) * SEL_BLOCK
    overlap = ((cmp_start[:, None] <= sel_start[None, :] + SEL_BLOCK - 1)
               & (cmp_end[:, None] >= sel_start[None, :])).astype(jnp.float32)
    blk_ids = jnp.arange(n_blk)
    b_idx = jnp.arange(B)[:, None, None, None]
    g_idx = jnp.arange(G)[None, :, None, None]
    scale = HEAD_DIM ** -0.5

    def chunk(c0):
        t = c0 + jnp.arange(QB)
        qc = lax.dynamic_slice_in_dim(q, c0, QB, axis=1)
        dist_c = t[:, None] - cmp_end[None, :]
        s_c = jnp.einsum('bqgrd,bngd->bgrqn', qc, kc_b).astype(jnp.float32) * scale \
            - slopes * dist_c.astype(jnp.float32)
        p_c = _masked_softmax(s_c, dist_c >= 0)
        o_c = jnp.einsum('bgrqn,bngd->bqgrd', p_c.astype(vc_b.dtype), vc_b)
        imp = jnp.einsum('bgrqn,nj->bgqj', p_c, overlap)
        tb = (t // SEL_BLOCK)[:, None]
        valid = blk_ids[None, :] <= tb
        forced = (blk_ids[None, :] == 0) | (blk_ids[None, :] == tb) | (blk_ids[None, :] == tb - 1)
        score = jnp.where(valid, jnp.where(forced, FORCE_SCORE, imp), -jnp.inf)
        top_s, top_i = lax.top_k(score, n_sel)
        kg = ks_blk[b_idx, g_idx, top_i].reshape(B, G, QB, n_sel * SEL_BLOCK, Dh)
        vg = vs_blk[b_idx, g_idx, top_i].reshape(B, G, QB, n_sel * SEL_BLOCK, Dh)
        pos = (top_i[..., None] * SEL_BLOCK + jnp.arange(SEL_BLOCK)).reshape(B, G, QB, -1)
        ok = jnp.broadcast_to(jnp.isfinite(top_s)[..., None],
                              (B, G, QB, n_sel, SEL_BLOCK)).reshape(B, G, QB, -1)
        dist_s = t[None, None, :, None] - pos
        mask_s = ok & (dist_s >= 0)
        s_s = jnp.einsum('bqgrd,bgqkd->bgrqk', qc, kg).astype(jnp.float32) * scale \
            - slopes * dist_s[:, :, None].astype(jnp.float32)
        p_s = _masked_softmax(s_s, mask_s[:, :, None])
        o_s = jnp.einsum('bgrqk,bgqkd->bqgrd', p_s.astype(vg.dtype), vg)
        kwc = lax.dynamic_slice_in_dim(kw_pad, c0, WINDOW + QB, axis=1)
        vwc = lax.dynamic_slice_in_dim(vw_pad, c0, WINDOW + QB, axis=1)
        kp = c0 - WINDOW + jnp.arange(WINDOW + QB)
        dist_w = t[:, None] - kp[None, :]
        mask_w = (kp[None, :] >= 0) & (dist_w >= 0) & (dist_w < WINDOW)
        s_w = jnp.einsum('bqgrd,bkgd->bgrqk', qc, kwc).astype(jnp.float32) * scale \
            - slopes * dist_w.astype(jnp.float32)
        p_w = _masked_softmax(s_w, mask_w)
        o_w = jnp.einsum('bgrqk,bkgd->bqgrd', p_w.astype(vwc.dtype), vwc)
        gc = lax.dynamic_slice_in_dim(gates, c0, QB, axis=1)[..., None]
        return gc[:, :, 0] * o_c + gc[:, :, 1] * o_s + gc[:, :, 2] * o_w

    starts = jnp.arange(S // QB) * QB
    o = lax.map(chunk, starts)
    o = jnp.moveaxis(o, 0, 1).reshape(B, S, MIX_WIDTH)
    return o, q_mem

def _wkv7_scan(r, w, k, v, a, b):
    B, S, H, N = r.shape

    def step(state, inp):
        r_t, w_t, k_t, v_t, a_t, b_t = inp
        sa = jnp.einsum('bhvk,bhk->bhv', state, a_t)
        state = state * w_t[:, :, None, :] + sa[..., None] * b_t[:, :, None, :] \
            + v_t[..., None] * k_t[:, :, None, :]
        return state, jnp.einsum('bhvk,bhk->bhv', state, r_t)

    xs = tuple(jnp.moveaxis(t, 1, 0) for t in (r, w, k, v, a, b))
    s0 = jnp.zeros((B, H, N, N), jnp.float32)
    _, y = lax.scan(step, s0, xs)
    return jnp.moveaxis(y, 0, 1)

def _rwkv7_mixer(h, w_in, mu, w0, w2, a0, a2, g2, k_k, k_a, r_k, lnx_w, lnx_b):
    B, S, _ = h.shape
    H, N = MIX_HEADS, HEAD_DIM
    proj = h @ w_in
    z, q_mem = proj[..., :RW_SHIFT], proj[..., RW_SHIFT:]
    z_prev = jnp.pad(z, ((0, 0), (1, 0), (0, 0)))[:, :-1]
    z = z + (z_prev - z) * mu
    r, k, v, zw, za, zg = _split(z, [MIX_WIDTH] * 3 + [DECAY_LORA, ICLR_LORA, GATE_LORA])
    w_log = -jax.nn.softplus(-(w0 + jnp.tanh(zw) @ w2)) - 0.5
    decay = jnp.exp(-jnp.exp(w_log.astype(jnp.float32)))
    a = jax.nn.sigmoid(a0 + za @ a2)
    g = jax.nn.sigmoid(zg) @ g2
    kk = (k * k_k).astype(jnp.float32).reshape(B, S, H, N)
    kk = kk / jnp.maximum(jnp.sqrt(jnp.sum(kk * kk, axis=-1, keepdims=True)), 1e-12)
    k = k * (1 + (a - 1) * k_a)

    def heads(t):
        return t.astype(jnp.float32).reshape(B, S, H, N)

    rh, wh, kh, vh, ah = heads(r), heads(decay), heads(k), heads(v), heads(a)
    y = _wkv7_scan(rh, wh, kh, vh, -kk, kk * ah)
    mean = jnp.mean(y, axis=-1, keepdims=True)
    var = jnp.mean(jnp.square(y - mean), axis=-1, keepdims=True)
    y = ((y - mean) * lax.rsqrt(var + GN_EPS)).reshape(B, S, MIX_WIDTH)
    y = y * lnx_w.astype(jnp.float32) + lnx_b.astype(jnp.float32)
    bonus = jnp.sum(rh * kh * r_k.astype(jnp.float32), axis=-1, keepdims=True) * vh
    out = (y + bonus.reshape(B, S, MIX_WIDTH)) * g.astype(jnp.float32)
    return out.astype(h.dtype), q_mem

def _mem_attention(q_mem, mem_n, w_kv):
    B, S, _ = q_mem.shape
    M = mem_n.shape[1]
    k, v = jnp.split(mem_n @ w_kv, 2, axis=-1)
    q = q_mem.reshape(B, S, MEM_HEADS, HEAD_DIM)
    k = k.reshape(B, M, MEM_HEADS, HEAD_DIM)
    v = v.reshape(B, M, MEM_HEADS, HEAD_DIM)
    s = jnp.einsum('bshd,bmhd->bhsm', q, k).astype(jnp.float32) * (HEAD_DIM ** -0.5)
    p = jax.nn.softmax(s, axis=-1).astype(v.dtype)
    return jnp.einsum('bhsm,bmhd->bshd', p, v).reshape(B, S, MEM_WIDTH)

def _swiglu(h, w_in, w_out):
    gate, up = jnp.split(h @ w_in, 2, axis=-1)
    return (jax.nn.silu(gate) * up) @ w_out

def first_inputs(seed: int = 0) -> dict:
    key = jax.random.key(seed)
    ks = jax.random.split(key, 32)
    f32 = jnp.float32

    def nrm(k, shape, scale):
        return jax.random.normal(k, shape, f32) * scale

    D = D_MODEL
    return {
        'x': nrm(ks[0], (BATCH, SEQ, D), 1.0),
        'mem': nrm(ks[1], (BATCH, N_MEM, D), 1.0),
        'norm1': 1.0 + nrm(ks[2], (DEPTH, D), 0.05),
        'norm_mem': 1.0 + nrm(ks[3], (DEPTH, D), 0.05),
        'w_mem_kv': nrm(ks[4], (DEPTH, D, 2 * MEM_WIDTH), D ** -0.5),
        'w_o': nrm(ks[5], (DEPTH, MIX_WIDTH + MEM_WIDTH, D), (MIX_WIDTH + MEM_WIDTH) ** -0.5),
        'norm2': 1.0 + nrm(ks[6], (DEPTH, D), 0.05),
        'w_ffn_in': nrm(ks[7], (DEPTH, D, 2 * FFN_HIDDEN), D ** -0.5),
        'w_ffn_out': nrm(ks[8], (DEPTH, FFN_HIDDEN, D), FFN_HIDDEN ** -0.5),
        'nsa_w_in': nrm(ks[9], (N_NSA, D, NSA_IN), D ** -0.5),
        'nsa_gate_b': nrm(ks[10], (N_NSA, 3 * MIX_HEADS), 0.1),
        'nsa_cmp_pos': nrm(ks[11], (N_NSA, 2, CMP_BLOCK, HEAD_DIM), 0.1),
        'nsa_cmp_w1': nrm(ks[12], (N_NSA, 2, CMP_BLOCK, HEAD_DIM, CMP_HIDDEN), (CMP_BLOCK * HEAD_DIM) ** -0.5),
        'nsa_cmp_w2': nrm(ks[13], (N_NSA, 2, CMP_HIDDEN, HEAD_DIM), CMP_HIDDEN ** -0.5),
        'rw_w_in': nrm(ks[14], (N_RWKV, D, RW_IN), D ** -0.5),
        'rw_mu': jax.random.uniform(ks[15], (N_RWKV, RW_SHIFT), f32),
        'rw_w0': jax.random.uniform(ks[16], (N_RWKV, MIX_WIDTH), f32, -5.0, 1.0),
        'rw_w2': nrm(ks[17], (N_RWKV, DECAY_LORA, MIX_WIDTH), 0.1 * DECAY_LORA ** -0.5),
        'rw_a0': nrm(ks[18], (N_RWKV, MIX_WIDTH), 0.5),
        'rw_a2': nrm(ks[19], (N_RWKV, ICLR_LORA, MIX_WIDTH), 0.3 * ICLR_LORA ** -0.5),
        'rw_g2': nrm(ks[20], (N_RWKV, GATE_LORA, MIX_WIDTH), GATE_LORA ** -0.5),
        'rw_k_k': 0.85 + nrm(ks[21], (N_RWKV, MIX_WIDTH), 0.05),
        'rw_k_a': 1.0 + nrm(ks[22], (N_RWKV, MIX_WIDTH), 0.05),
        'rw_r_k': nrm(ks[23], (N_RWKV, MIX_HEADS, HEAD_DIM), 0.1),
        'rw_lnx_w': 1.0 + nrm(ks[24], (N_RWKV, MIX_WIDTH), 0.05),
        'rw_lnx_b': nrm(ks[25], (N_RWKV, MIX_WIDTH), 0.02),
        'final_norm': 1.0 + nrm(ks[26], (D,), 0.05),
    }

def first_block(x, mem, norm1, norm_mem, w_mem_kv, w_o, norm2, w_ffn_in, w_ffn_out,
              nsa_w_in, nsa_gate_b, nsa_cmp_pos, nsa_cmp_w1, nsa_cmp_w2,
              rw_w_in, rw_mu, rw_w0, rw_w2, rw_a0, rw_a2, rw_g2, rw_k_k, rw_k_a, rw_r_k,
              rw_lnx_w, rw_lnx_b, final_norm):
    for i in range(DEPTH):
        j = i // 2
        hn = _rmsnorm(x, norm1[i])
        mn = _rmsnorm(mem, norm_mem[i])
        if i % 2 == 0:
            mix, q_mem = _nsa_mixer(hn, nsa_w_in[j], nsa_gate_b[j], nsa_cmp_pos[j],
                                    nsa_cmp_w1[j], nsa_cmp_w2[j])
        else:
            mix, q_mem = _rwkv7_mixer(hn, rw_w_in[j], rw_mu[j], rw_w0[j], rw_w2[j], rw_a0[j],
                                      rw_a2[j], rw_g2[j], rw_k_k[j], rw_k_a[j], rw_r_k[j],
                                      rw_lnx_w[j], rw_lnx_b[j])
        cross = _mem_attention(q_mem, mn, w_mem_kv[i])
        x = x + jnp.concatenate([mix, cross], axis=-1) @ w_o[i]
        x = x + _swiglu(_rmsnorm(x, norm2[i]), w_ffn_in[i], w_ffn_out[i])
    return _rmsnorm(x, final_norm)


DEPTH_2 = 1

CHUNK = 128
N_SGU_GROUPS = 8
SGU_WIDTH = D_MODEL
SGU_GROUP_DIM = SGU_WIDTH // N_SGU_GROUPS
N_HEADS = 8
HEAD_DIM_2 = 128
ATTN_WIDTH = N_HEADS * HEAD_DIM_2
Q_BLOCK = 128
D_FF = -(-8 * D_MODEL // (3 * 256)) * 256
EPS = 1e-6

_IN_SIZES = (SGU_WIDTH, SGU_WIDTH, ATTN_WIDTH, ATTN_WIDTH, ATTN_WIDTH, D_MODEL, D_MODEL, N_HEADS)
IN_WIDTH = sum(_IN_SIZES)
IN_SPLITS = tuple(int(s) for s in np.cumsum(_IN_SIZES)[:-1])


def rmsnorm(x, g):
    xf = x.astype(jnp.float32)
    r = lax.rsqrt(jnp.mean(xf * xf, axis=-1, keepdims=True) + EPS)
    return (xf * r * g.astype(jnp.float32)).astype(x.dtype)

def layernorm(x, g):
    xf = x.astype(jnp.float32)
    mu = jnp.mean(xf, axis=-1, keepdims=True)
    xc = xf - mu
    r = lax.rsqrt(jnp.mean(xc * xc, axis=-1, keepdims=True) + EPS)
    return (xc * r * g.astype(jnp.float32)).astype(x.dtype)

def spatial_gating(u, v, w_s, b_s, g_v):
    bsz, seq = v.shape[0], v.shape[1]
    v = layernorm(v, g_v)
    vc = v.reshape(bsz, seq // CHUNK, CHUNK, N_SGU_GROUPS, SGU_GROUP_DIM)
    causal = jnp.tril(jnp.ones((CHUNK, CHUNK), dtype=bool))
    w = jnp.where(causal[None], w_s, jnp.zeros_like(w_s))
    mixed = jnp.einsum('gts,bcsgd->bctgd', w, vc) + b_s.T[None, None, :, :, None]
    return u * mixed.reshape(bsz, seq, SGU_WIDTH)

def forgetting_attention(q, k, v, f_logit, b_f):
    bsz, seq = q.shape[0], q.shape[1]

    def heads(t):
        return t.reshape(bsz, seq, N_HEADS, HEAD_DIM_2).transpose(0, 2, 1, 3)

    q = heads(q) * (HEAD_DIM_2 ** -0.5)
    k = heads(k)
    v = heads(v)
    log_f = jax.nn.log_sigmoid((f_logit + b_f).astype(jnp.float32))
    c = jnp.cumsum(log_f, axis=1).transpose(0, 2, 1)
    k_pos = jnp.arange(seq)

    def block(i):
        start = i * Q_BLOCK
        qi = lax.dynamic_slice_in_dim(q, start, Q_BLOCK, axis=2)
        ci = lax.dynamic_slice_in_dim(c, start, Q_BLOCK, axis=2)
        s = jnp.einsum('bhqd,bhkd->bhqk', qi, k).astype(jnp.float32)
        s = s + ci[..., None] - c[:, :, None, :]
        q_pos = start + jnp.arange(Q_BLOCK)
        s = jnp.where(k_pos[None, :] <= q_pos[:, None], s, -jnp.inf)
        p = jax.nn.softmax(s, axis=-1).astype(v.dtype)
        return jnp.einsum('bhqk,bhkd->bhqd', p, v)

    out = lax.map(block, jnp.arange(seq // Q_BLOCK))
    return out.transpose(1, 0, 3, 2, 4).reshape(bsz, seq, ATTN_WIDTH)

def swiglu(h, w_gate, w_up, w_down):
    return (jax.nn.silu(h @ w_gate) * (h @ w_up)) @ w_down

def second_inputs(seed: int = 0) -> dict:
    key = jax.random.key(seed)
    ks = jax.random.split(key, 15)
    f32 = jnp.float32

    def nrm(k, shape, scale):
        return jax.random.normal(k, shape, f32) * scale

    def gain(k, shape):
        return 1.0 + 0.1 * jax.random.normal(k, shape, f32)

    x = jax.random.normal(ks[0], (BATCH, SEQ, D_MODEL), f32)
    mix_pre_g = gain(ks[1], (DEPTH_2, D_MODEL))
    w_in = nrm(ks[2], (DEPTH_2, D_MODEL, IN_WIDTH), D_MODEL ** -0.5)
    b_forget = jnp.linspace(1.0, 6.0, N_HEADS, dtype=f32)[None, :] + 0.1 * jax.random.normal(ks[3], (DEPTH_2, N_HEADS), f32)
    sgu_norm_g = gain(ks[4], (DEPTH_2, SGU_WIDTH))
    w_spatial = nrm(ks[5], (DEPTH_2, N_SGU_GROUPS, CHUNK, CHUNK), CHUNK ** -0.5)
    b_spatial = 1.0 + 0.1 * jax.random.normal(ks[6], (DEPTH_2, N_SGU_GROUPS, CHUNK), f32)
    w_out = nrm(ks[7], (DEPTH_2, D_MODEL, D_MODEL), D_MODEL ** -0.5)
    mix_post_g = gain(ks[8], (DEPTH_2, D_MODEL))
    ffn_pre_g = gain(ks[9], (DEPTH_2, D_MODEL))
    w_gate = nrm(ks[10], (DEPTH_2, D_MODEL, D_FF), D_MODEL ** -0.5)
    w_up = nrm(ks[11], (DEPTH_2, D_MODEL, D_FF), D_MODEL ** -0.5)
    w_down = nrm(ks[12], (DEPTH_2, D_FF, D_MODEL), D_FF ** -0.5)
    ffn_post_g = gain(ks[13], (DEPTH_2, D_MODEL))
    return {"x": x, "mix_pre_g": mix_pre_g, "w_in": w_in, "b_forget": b_forget,
            "sgu_norm_g": sgu_norm_g, "w_spatial": w_spatial, "b_spatial": b_spatial,
            "w_out": w_out, "mix_post_g": mix_post_g, "ffn_pre_g": ffn_pre_g,
            "w_gate": w_gate, "w_up": w_up, "w_down": w_down, "ffn_post_g": ffn_post_g}

def second_block(x, mix_pre_g, w_in, b_forget, sgu_norm_g, w_spatial, b_spatial, w_out,
              mix_post_g, ffn_pre_g, w_gate, w_up, w_down, ffn_post_g):
    for l in range(DEPTH_2):
        h = rmsnorm(x, mix_pre_g[l])
        proj = h @ w_in[l]
        u, v_s, q, k, v_a, g_a, g_b, f_logit = jnp.split(proj, IN_SPLITS, axis=-1)
        y_a = spatial_gating(jax.nn.gelu(u), jax.nn.gelu(v_s), w_spatial[l], b_spatial[l], sgu_norm_g[l])
        y_b = forgetting_attention(q, k, v_a, f_logit, b_forget[l])
        merged = jax.nn.sigmoid(g_a) * y_a + jax.nn.sigmoid(g_b) * y_b
        x = x + rmsnorm(merged @ w_out[l], mix_post_g[l])
        h = rmsnorm(x, ffn_pre_g[l])
        x = x + rmsnorm(swiglu(h, w_gate[l], w_up[l], w_down[l]), ffn_post_g[l])
    return x


def setup_inputs(seed=0):
    out = dict(first_inputs(seed))
    for name, value in second_inputs(seed + 1).items():
        if name != "x":
            out[name + "_2"] = value
    return out


def reference(
    x, mem, norm1, norm_mem, w_mem_kv, w_o, norm2, w_ffn_in, w_ffn_out, nsa_w_in, nsa_gate_b,
    nsa_cmp_pos, nsa_cmp_w1, nsa_cmp_w2, rw_w_in, rw_mu, rw_w0, rw_w2, rw_a0, rw_a2, rw_g2,
    rw_k_k, rw_k_a, rw_r_k, rw_lnx_w, rw_lnx_b, final_norm, mix_pre_g_2, w_in_2, b_forget_2,
    sgu_norm_g_2, w_spatial_2, b_spatial_2, w_out_2, mix_post_g_2, ffn_pre_g_2, w_gate_2,
    w_up_2, w_down_2, ffn_post_g_2,
):
    x = first_block(
        x, mem, norm1, norm_mem, w_mem_kv, w_o, norm2, w_ffn_in, w_ffn_out, nsa_w_in,
        nsa_gate_b, nsa_cmp_pos, nsa_cmp_w1, nsa_cmp_w2, rw_w_in, rw_mu, rw_w0, rw_w2, rw_a0,
        rw_a2, rw_g2, rw_k_k, rw_k_a, rw_r_k, rw_lnx_w, rw_lnx_b, final_norm,
    )
    return second_block(
        x, mix_pre_g_2, w_in_2, b_forget_2, sgu_norm_g_2, w_spatial_2, b_spatial_2, w_out_2,
        mix_post_g_2, ffn_pre_g_2, w_gate_2, w_up_2, w_down_2, ffn_post_g_2,
    )


_drawn_inputs = setup_inputs


def setup_inputs(seed=0):
    import zlib

    import numpy as np

    out = dict(_drawn_inputs(seed))
    spreads = {}
    factors = {'norm_mem': 7.099,
     'rw_w2': 50.981,
     'rw_k_k': 24.576,
     'rw_lnx_b': 14.573,
     'nsa_gate_b': 3.416,
     'rw_a2': 3.084,
     'rw_k_a': 6.412,
     'rw_lnx_w': 7.101}
    for name, (base, spread) in spreads.items():
        noise = np.random.default_rng([zlib.crc32(name.encode()), seed]).standard_normal(out[name].shape)
        drawn = base * np.exp(spread * noise) if base else spread * noise
        out[name] = __import__('jax').numpy.asarray(drawn.astype(out[name].dtype))
    for name, factor in factors.items():
        out[name] = (out[name] * factor).astype(out[name].dtype)
    return out
```

```python
import math
from contextlib import ExitStack

import numpy as np

import concourse.bass as bass
from concourse import mybir

F32 = mybir.dt.float32
ALU = mybir.AluOpType
ACT = mybir.ActivationFunctionType
AX = mybir.AxisListType

P = 128
D = 1024
S = 256
QT = S // P
KT = D // P
DH = 64
H = 12
G = 4
R = H // G
MH = 4
FFN = 2816
FT = FFN // P
CMP_BLOCK, CMP_STRIDE = 32, 16
NCMP = (S - CMP_BLOCK) // CMP_STRIDE + 1
CH = 64
NT = H * DH // P
EPS = 1e-6
GN_EPS = 64e-5
MERGES = (2, 4, 8, 16, 32)
NEG = -1e30
C0 = math.exp(-0.5)
NFH = 8
RING = 4
SLOT = 2048


def alibi_slopes(n):
    def pow2(m):
        start = 2.0 ** (-8.0 / m)
        return [start ** (i + 1) for i in range(m)]
    c = 2 ** int(math.floor(math.log2(n)))
    s = pow2(c)
    if c < n:
        s = s + pow2(2 * c)[0::2][: n - c]
    return [float(np.float32(v)) for v in s]


SLOPES = alibi_slopes(H)


def head_of(p, i):
    gp, r = divmod(i, R)
    return (2 * gp + p) * R + r


def shape_constants():
    i = np.arange(P)[:, None]
    t = np.arange(P)[None, :]
    parts = {}
    parts["ident"] = (i == t)
    same = (i // CH) == (t // CH)
    parts["wkv_mask"] = np.concatenate([same & (i < t), same & (i <= t)], 1)
    for s in (1, 2, 4, 8, 16, 32):
        parts[f"merge{s}"] = (i // (2 * s) == t // (2 * s)) & (i % (2 * s) < s) & (t % (2 * s) >= s)
    parts["head_ones"] = (i // DH) == (t // DH)
    parts["tri"] = i <= t
    parts["ones"] = np.ones((P, P))
    dist, causal = [], []
    for qt in range(QT):
        k = np.arange((qt + 1) * P)[None, :]
        d = (qt * P + i) - k
        dist.append(np.where(d >= 0, -d, NEG))
        causal.append(np.where(d >= 0, 0.0, NEG))
    parts["dist"] = np.concatenate(dist, 1)
    parts["causal"] = np.concatenate(causal, 1)
    parts["chunk_keep"] = np.broadcast_to((np.arange(S)[None, :] % CH) != 0, (P, S))
    end = np.arange(16)[None, :] * CMP_STRIDE + CMP_BLOCK - 1
    bias = np.zeros((P, 2, QT, NT, 16))
    mask = np.zeros((P, QT, 16))
    for qt in range(QT):
        d = qt * P + i - end
        mask[:, qt] = (d >= 0) & (np.arange(16)[None, :] < NCMP)
        for p in range(2):
            for j in range(NT):
                bias[:, p, qt, j] = np.where(d >= 0, -SLOPES[head_of(p, j)] * d, NEG)
    parts["cmp_bias"] = bias.reshape(P, -1)
    parts["cmp_mask"] = mask.reshape(P, -1)
    at, cols = {}, 0
    for name, a in parts.items():
        at[name] = (cols, a.shape[1])
        cols += a.shape[1]
    return at, np.ascontiguousarray(np.concatenate([np.asarray(a, np.float32) for a in parts.values()], 1))


VEC = {}
for _n, _k in (("norm1", 16), ("norm_mem", 16), ("norm2", 16), ("mix_pre_g_2", 8), ("ffn_pre_g_2", 8),
               ("rw_w0", 6), ("rw_a0", 6), ("rw_k_k", 6), ("rw_k_a", 6), ("rw_r_k", 6),
               ("rw_lnx_w", 6), ("rw_lnx_b", 6), ("rw_mu", 20)):
    VEC[_n] = (sum(k for _, k in VEC.values()), _k)
MU_LAST = sum(k for _, k in VEC.values())
MU_TAIL = 32


def kernel_program(nc, T, out):
    ctx = ExitStack()
    with ctx:
        build(nc, T, out, ctx)


def build(nc, T, out, ctx):
    def sb(name, n):
        return ctx.enter_context(nc.sbuf_tensor(name, [P, n], F32))

    sems = {}

    def sem(name):
        if name not in sems:
            sems[name] = ctx.enter_context(nc.semaphore(name))
        return sems[name]

    CAT, cst_np = shape_constants()

    ring = sb("ring", RING * SLOT)
    x_res = sb("x_res", QT * D)
    act_fm = sb("act_fm", KT * S)
    rows_tm = sb("rows_tm", QT * D)
    cst = sb("cst", cst_np.shape[1])
    vec = sb("vec", P)
    rw_wa2 = sb("rw_wa2", H * DH)
    rw_g2 = sb("rw_g2", 2 * H * DH)
    cmp_w2 = sb("cmp_w2", 2 * DH)
    kmem1 = sb("kmem1", 2 * S)
    vmem1 = sb("vmem1", QT * 256)
    qmem = sb("qmem", 2 * S)
    sbuf_s = sb("sbuf_s", 2 * 512)
    sbuf_p = sb("sbuf_p", 2 * 512)
    sbuf_pt = sb("sbuf_pt", 2 * 512)
    scratch = sb("scratch", D)
    zshift = sb("zshift", 2 * 2 * (S + 1))
    zdelta = sb("zdelta", 2 * S)
    small = sb("small", 512)
    ARENA = 24300
    arena = sb("arena", ARENA)

    x_tm = x_res[:, :].rearrange("p (q c) -> p q c", q=QT)
    tm = rows_tm[:, :].rearrange("p (q c) -> p q c", q=QT)
    fm = act_fm[:, :].rearrange("p (k t) -> p k t", k=KT)

    def C(name, rows=P):
        o, n = CAT[name]
        return cst[0:rows, o:o + n]

    ident = C("ident")

    def V(name, i, j=0):
        o, _ = VEC[name]
        return vec[:, o + i:o + i + 1]

    arena_at = [0]

    def take(n):
        a = arena[:, arena_at[0]:arena_at[0] + n]
        arena_at[0] += n
        assert arena_at[0] <= ARENA
        return a

    small_at = [0]

    def tiny(n):
        a = small[:, small_at[0]:small_at[0] + n]
        small_at[0] += n
        assert small_at[0] <= 512
        return a

    hT = take(FT * S).rearrange("p (k t) -> p k t", k=FT)
    silu = take(2 * S).rearrange("p (b t) -> p b t", b=2)
    L2_START = arena_at[0]
    arena_at[0] = 0
    qT = take(NT * S).rearrange("p (i t) -> p i t", i=NT)
    kcvT = take(2 * 2 * S).rearrange("p (v g t) -> p v g t", v=2, g=2)
    kselT = take(2 * S).rearrange("p (g t) -> p g t", g=2)
    kwinT = take(2 * S).rearrange("p (g t) -> p g t", g=2)
    vsel = take(QT * 256).rearrange("p (q c) -> p q c", q=QT)
    vwin = take(QT * 256).rearrange("p (q c) -> p q c", q=QT)
    kmem0 = take(2 * S)
    vmem0 = take(QT * 256)
    blocks = take(2 * CMP_BLOCK * 2 * NCMP).rearrange("p (v l n) -> p v l n", v=2, l=CMP_BLOCK)
    hid = take(2 * 4 * NCMP).rearrange("p (v n) -> p v n", v=2)
    kcb = take(2 * NCMP)
    vcb = take(256)
    s_cmp = take(2 * QT * NT * 16).rearrange("p (h q i n) -> p h q i n", h=2, q=QT, i=NT)
    p_cmpT = take(8 * 384).rearrange("p (u c) -> p u c", u=8)
    alibi = take(H * 384).rearrange("p (h c) -> p h c", h=H)
    posT = take(64)
    pos_rows = take(P)
    vec_rows = take(P)
    gate_b = take(3 * H)
    mem_tm = take(QT * D).rearrange("p (q c) -> p q c", q=QT)
    gates = tiny(QT * 3 * H).rearrange("p (q c) -> p q c", q=QT)
    rsum = tiny(2 * 40).rearrange("p (u q) -> p u q", q=QT)
    nmax = tiny(2 * 40).rearrange("p (u q) -> p u q", q=QT)
    coef = tiny(2 * 40).rearrange("p (u q) -> p u q", q=QT)
    ssq = tiny(2 * 10).rearrange("p (r q) -> p r q", q=QT)
    rms = tiny(2 * 10).rearrange("p (r q) -> p r q", q=QT)
    c_cmp = tiny(24)
    m_cmp = tiny(24)
    vecs2 = tiny(8)
    mem1_fm = p_cmpT.rearrange("p u c -> p (u c)")[:, 0:KT * S].rearrange("p (k t) -> p k t", k=KT)

    arena_at[0] = 0
    ar = take(NT * 2 * 2 * P).rearrange("p (i c b t) -> p i c b t", i=NT, c=2, b=2)
    b_fm = take(NT * S).rearrange("p (i t) -> p i t", i=NT)
    k_fm = take(NT * S).rearrange("p (i t) -> p i t", i=NT)
    g_fm = take(NT * S).rearrange("p (i t) -> p i t", i=NT)
    bonus = take(NT * S).rearrange("p (i t) -> p i t", i=NT)
    v_fm = take(NT * S).rearrange("p (i t) -> p i t", i=NT)
    AFTER = arena_at[0]
    r_fm = take(NT * S).rearrange("p (i t) -> p i t", i=NT)
    kraw = take(NT * S).rearrange("p (i t) -> p i t", i=NT)
    lora = take(3 * S).rearrange("p (i t) -> p i t", i=3)
    iclr = take(NT * S).rearrange("p (i t) -> p i t", i=NT)
    sg = take(NT * S).rearrange("p (i t) -> p i t", i=NT)
    csum = take(NT * S).rearrange("p (i t) -> p i t", i=NT)
    e_in = take(NT * S).rearrange("p (i t) -> p i t", i=NT)
    kk = take(NT * S).rearrange("p (i t) -> p i t", i=NT)
    e_neg = rows_tm[:, 0:NT * S].rearrange("p (i t) -> p i t", i=NT)
    arena_at[0] = AFTER
    sc = take(H * 512).rearrange("p (u b t) -> p u b t", u=H, b=4)
    tt = take(H * P).rearrange("p (u t) -> p u t", u=H)
    tmat = take(2 * 512).rearrange("p (b u t) -> p b u t", b=2, u=4)
    emat = take(2 * 512).rearrange("p (b u t) -> p b u t", b=2, u=4)
    cmat = take(2 * 512).rearrange("p (b u t) -> p b u t", b=2, u=4)
    kbv_tm = take(3 * H * DH).rearrange("p (w c) -> p w c", w=3)
    p_end = tiny(NT * 4).rearrange("p (i c) -> p i c", i=NT)
    y_fm = rows_tm[:, 0:NT * S].rearrange("p (i t) -> p i t", i=NT)
    y0 = sbuf_s[:, 0:H * DH]
    u_tm = sbuf_p[:, 0:H * DH]
    state = sbuf_pt[:, 0:2 * NT * DH].rearrange("p (b i v) -> p b i v", b=2, i=NT)
    cross = scratch[:, 0:QT * 256].rearrange("p (q c) -> p q c", q=QT)
    zt = arena[:, AFTER:AFTER + NT * S].rearrange("p (i t) -> p i t", i=NT)
    kk_sq = b_fm
    tms = [tmat[:, 0], tmat[:, 1], zshift[:, 0:512].rearrange("p (u t) -> p u t", u=4)]
    ems = [emat[:, 0], emat[:, 1], zshift[:, 512:1024].rearrange("p (u t) -> p u t", u=4)]
    cms = [cmat[:, 0], cmat[:, 1], zdelta[:, :].rearrange("p (u t) -> p u t", u=4)]
    VEC_DMAS, SMALL_DMAS = len(VEC) + 1, 8

    arena_at[0] = L2_START
    gains = take(4 * D).rearrange("p (g c) -> p g c", g=4)
    GAIN = {"final_norm": 0, "sgu_norm_g_2": 1, "mix_post_g_2": 2, "ffn_post_g_2": 3}
    q2 = arena[:, 0:2048].rearrange("p (k t) -> p k t", k=KT)
    k2 = arena[:, 2048:4096].rearrange("p (k t) -> p k t", k=KT)
    logf = arena[:, 4096:4112].rearrange("p (q h) -> p q h", q=QT)
    tmpf = arena[:, 4112:4160].rearrange("p (a q h) -> p a q h", a=3, q=QT)
    ccum = arena[:, 4160:4416]
    sel = arena[:, 4416:5440].rearrange("p (h t) -> p h t", h=NFH)
    u_g = take(QT * D).rearrange("p (q c) -> p q c", q=QT)
    v_n = take(QT * D).rearrange("p (q c) -> p q c", q=QT)
    v_a = take(QT * D).rearrange("p (q c) -> p q c", q=QT)
    sga = take(QT * D).rearrange("p (q c) -> p q c", q=QT)
    sgb = take(QT * D).rearrange("p (q c) -> p q c", q=QT)
    wsT = take(NFH * P).rearrange("p (g t) -> p g t", g=NFH)
    ws_raw = take(NFH * P).rearrange("p (g t) -> p g t", g=NFH)
    bn = tiny(24)
    mv = tiny(8)
    b_forget = tiny(8)

    bank = [ctx.enter_context(nc.psum_tensor(f"bank{i}", [P, 512], F32)) for i in range(8)]

    number, uses, slots = {}, {}, []
    turn_of, fills = [0, 0], [0] * 8

    def unit(name, banks=1, slot=None, upper=False):
        number[name] = len(number)
        uses[name] = []
        for _ in range(banks):
            b = 4 + turn_of[1] % 4 if upper else turn_of[0] % 4
            turn_of[upper] += 1
            uses[name].append((b, fills[b]))
            fills[b] += 1
        if slot:
            slots.append((name, slot))

    def align():
        turn_of[0] += -turn_of[0] % 4


    def cols(w, a, b):
        return w[:, a:b].rearrange("(k p) n -> p k n", p=P)

    def slot_cols(w, a, b):
        return lambda dst: [(dst[:, 0:KT * (b - a)].rearrange("p (k n) -> p k n", k=KT), cols(w, a, b))]

    def slot_rows(w, j):
        return lambda dst: [(dst.rearrange("p (k n) -> p k n", k=2),
                             w[2 * j * P:(2 * j + 2) * P, :].rearrange("(k p) n -> p k n", p=P))]

    def slot_pair(wa, a, wb, b):
        return lambda dst: [
            (dst.rearrange("p (k n) -> p k n", k=KT)[:, :, 0:P], cols(wa, a, a + P)),
            (dst.rearrange("p (k n) -> p k n", k=KT)[:, :, P:2 * P], cols(wb, b, b + P))]

    def slot_q(w, j):
        def loads(dst):
            d = dst.rearrange("p (k n) -> p k n", k=KT)
            for a in range(2):
                for p in range(2):
                    h = head_of(p, 2 * j + a)
                    yield (d[:, :, a * P + p * DH:a * P + (p + 1) * DH], cols(w, h * DH, (h + 1) * DH))
        return loads

    def slot_cmp(v, half):
        def loads(dst):
            w = T["nsa_cmp_w1"][0, v, half * 16:half * 16 + 16].rearrange("l d e -> d l e")
            for p in range(2):
                yield (dst[p * DH:(p + 1) * DH, :].rearrange("p (l e) -> p l e", l=16), w)
        return loads

    def ffn_units(tag, wa, a0, wb, b0, wo):
        for j in range(FT):
            unit(f"{tag}_in{j}", 1, slot_pair(wa, a0 + j * P, wb, b0 + j * P))
        align()
        for j in range(FT // 2):
            unit(f"{tag}_out{j}", 4 if j == 0 else 0, slot_rows(wo, j))

    nsa = T["nsa_w_in"][0]
    MW = H * DH
    for l in range(2):
        unit(f"kmem{l}", 1, slot_cols(T["w_mem_kv"][l], 0, 256))
        unit(f"vmem{l}", 1, slot_cols(T["w_mem_kv"][l], 256, 512))
    for j in range(3):
        unit(f"q{j}", 1, slot_q(nsa, j))
    for j, name in enumerate(("kc", "vc", "ks", "vs", "kw", "vw")):
        unit(name, 1, slot_cols(nsa, MW + j * 256, MW + (j + 1) * 256))
    GL = MW + 6 * 256
    unit("gl", 1, slot_cols(nsa, GL, GL + 3 * H))
    unit("qm0", 1, slot_cols(nsa, GL + 3 * H, GL + 3 * H + 256))
    for v in range(2):
        unit(f"hid{v}_0", 2, slot_cmp(v, 0))
        unit(f"hid{v}_1", 0, slot_cmp(v, 1))
    unit("kcb"), unit("vcb")
    unit("cs0"), unit("cs1")
    for j in range(8):
        unit(f"pct{j}")
    for j in range(4):
        unit(f"oc{j}")
    align()
    for j in range(4):
        unit(f"wo0_{j}", 4 if j == 0 else 0, slot_rows(T["w_o"][0], j))
    ffn_units("f0", T["w_ffn_in"][0], 0, T["w_ffn_in"][0], FFN, T["w_ffn_out"][0])
    rw = T["rw_w_in"][0]
    for j in range(10):
        unit(f"z{j}", 1, slot_cols(rw, j * 256, (j + 1) * 256))
    unit("z10", 1, slot_cols(rw, 2560, 2592))
    unit("qm1", 1, slot_cols(rw, 2592, 2848))
    for n in ("w2", "a2", "g2", "kn", "bs"):
        for j in range(3):
            unit(f"{n}_{j}")
    unit("crT")
    for pr in range(2):
        for w in range(3):
            for h in range(2):
                unit(f"tr{pr}_{w}_{h}", 1, upper=True)
        for u in range(H):
            unit(f"sc{pr}_{u}", 1, upper=True)
        for p in range(2):
            unit(f"y0{pr}_{p}", 1)
        for gi in range(3):
            unit(f"ti{pr}_{gi}", 1)
        for s in MERGES:
            for gi in range(3):
                unit(f"e{pr}_{s}_{gi}", 1, upper=True)
            for gi in range(3):
                unit(f"t{pr}_{s}_{gi}", 1 if s == 32 else 2)
        for c in (2 * pr, 2 * pr + 1):
            if c:
                unit(f"z{c}c", 2, upper=True)
            unit(f"u{c}c", 2)
            if c < 3:
                unit(f"h{c}c", 1, upper=True)
            if c:
                unit(f"oi{c}c", 2, upper=True)
        unit(f"oo{pr}", 2)
    for n in ("gm", "gv"):
        for j in range(3):
            unit(f"{n}_{j}")
    align()
    for j in range(4):
        unit(f"wo1_{j}", 4 if j == 0 else 0, slot_rows(T["w_o"][1], j))
    ffn_units("f1", T["w_ffn_in"][1], 0, T["w_ffn_in"][1], FFN, T["w_ffn_out"][1])
    w2in = T["w_in_2"][0]
    unit("wsT0"), unit("wsT1")
    for name, base in (("sv", 1024), ("su", 0)):
        for j in range(4):
            unit(f"{name}{j}", 1, slot_cols(w2in, base + j * 256, base + (j + 1) * 256))
    unit("sf", 1, slot_cols(w2in, 7168, 7176))
    for name, base in (("fq", 2048), ("fk", 3072), ("fv", 4096), ("ga", 5120), ("gb", 6144)):
        for j in range(4):
            unit(f"{name}{j}", 1, slot_cols(w2in, base + j * 256, base + (j + 1) * 256))
    unit("cc")
    for j in range(4):
        unit(f"sgu{j}")
    align()
    for j in range(4):
        unit(f"wo2_{j}", 4 if j == 0 else 0, slot_rows(T["w_out_2"][0], j))
    ffn_units("f2", T["w_gate_2"][0], 0, T["w_up_2"][0], 0, T["w_down_2"][0])

    slot_no = {name: n for n, (name, _) in enumerate(slots)}
    landed, total = {}, [0] * RING
    for n, (name, loads) in enumerate(slots):
        k = len(list(loads(ring[:, 0:SLOT])))
        total[n % RING] += 16 * k
        landed[name] = (n % RING, total[n % RING])

    unit_done = sem("unit_done")
    slot_landed = [sem(f"slot_landed{r}") for r in range(RING)]
    bank_free = [sem(f"bank_free{b}") for b in range(8)]

    def bank_of(name, i=0):
        return bank[uses[name][i][0]]

    def filled(name):
        return unit_done, number[name] + 1

    def evacuated(name, i=0):
        b, before = uses[name][i]
        return bank_free[b], before + 1

    def counter(name):
        return {"step": name, "counts": {}, "last": None}

    def tick(own, name=None):
        name = name or own["step"]
        own["counts"][name] = own["counts"].get(name, 0) + 1
        own["last"] = (sem(name), own["counts"][name])
        return sem(name)

    def freed(own, name, i=0):
        b, before = uses[name][i]
        own["last"] = (bank_free[b], before + 1)
        return bank_free[b]

    def last(own):
        return own["last"]

    heads = [("mem0", i) for i in range(MH)]
    for h in range(H):
        heads += [("sel", h), ("win", h)]
    heads += [("mem1", i) for i in range(MH)]
    heads += [("fox", i) for i in range(NFH)]
    first = {}
    for n, (kind, _) in enumerate(heads):
        first.setdefault(kind, n)
    AFTER_STAGE = {"mem0": "wo0_0", "mem1": "crT", "fox": "wo2_0"}
    STAGES = {"mem0": range(0, 28), "mem1": range(28, 32), "fox": range(32, 40)}

    def head_parts(n):
        kind, i = heads[n]
        if kind in ("mem0", "mem1"):
            k = (kmem0 if kind == "mem0" else kmem1[:, :]).rearrange("p (g t) -> p g t", g=2)
            v = (vmem0 if kind == "mem0" else vmem1[:, :]).rearrange("p (q c) -> p q c", q=QT)
            q = qmem[:, :].rearrange("p (g t) -> p g t", g=2)
            r = slice((i % 2) * DH, (i % 2) * DH + DH)
            return q[r, i // 2, :], k[r, i // 2, :], v[:, :, i * DH:(i + 1) * DH], DH, [(0, 0, S), (1, S, S)]
        causal = [(0, 0, P), (1, P, S)]
        if kind == "fox":
            return q2[:, i, :], k2[:, i, :], v_a[:, :, i * P:(i + 1) * P], P, causal
        g, r = divmod(i, R)
        p, gp = g % 2, g // 2
        rows = slice(p * DH, (p + 1) * DH)
        k = kselT if kind == "sel" else kwinT
        v = vsel if kind == "sel" else vwin
        return qT[rows, gp * R + r, :], k[rows, gp, :], v[:, :, g * DH:(g + 1) * DH], DH, causal

    def blocks_of(n):
        *_, segs = head_parts(n)
        return [(qt, kt, c + kt * P) for qt, c, nk in segs for kt in range(nk // P)]

    score_bank = lambda n: bank[4 + n % 2]
    pt_bank = bank[6]
    o_bank = lambda n: bank[(7, 3)[n % 2]]

    cst_d = T["shape_constants"]
    block = ctx.enter_context(nc.Block())

    @block.sync
    def _(sp):
        sp.dma_start(mem_tm, T["mem"][0].rearrange("(q p) c -> p q c", p=P)).then_inc(sem("mem_in"), 16)
        sp.dma_start(x_tm, T["x"][0].rearrange("(q p) c -> p q c", p=P)).then_inc(sem("x_in"), 16)
        for n, (name, loads) in enumerate(slots):
            if n >= RING:
                sp.wait_ge(unit_done, number[slots[n - RING][0]] + 1)
            if name == "f1_in4":
                sp.wait_ge(unit_done, number["f1_in0"] + 1)
                for gn, g in GAIN.items():
                    src = T[gn].rearrange("(a c) -> a c", a=1) if gn == "final_norm" else T[gn]
                    sp.dma_start(gains[:, g, :], src.to_broadcast((P, D))).then_inc(sem("gains_in"), 16)
                sp.dma_start(ws_raw, T["w_spatial_2"][0].rearrange("g t s -> t g s")).then_inc(sem("ws_in"), 16)
            r = n % RING
            for dst, src in loads(ring[:, r * SLOT:(r + 1) * SLOT]):
                sp.dma_start(dst, src).then_inc(slot_landed[r], 16)
        sp.wait_ge(sem("y_done"), 1)
        sp.dma_start(out[0].rearrange("(q p) c -> p q c", p=P), tm).then_inc(sem("y_out"), 16)
        sp.wait_ge(sem("y_out"), 16)

    @block.gpsimd
    def _(pool):
        own = counter("pool_step")
        pool.memset(vec_rows, 0.0).then_inc(tick(own, "vec_zero"), 1)
        pool.wait_ge(sem("cst_in"), 16)
        for h in range(H):
            ins = pool.tensor_scalar(alibi[:, h, :], C("dist"), SLOPES[h], None, ALU.mult)
        ins.then_inc(tick(own, "alibi_ready"), 1)
        pool.wait_ge(sem("tables"), 2)
        for v in range(2):
            pool.wait_ge(*evacuated(("kc", "vc")[v]))
            for g in range(2):
                src = kcvT[:, v, g, :].rearrange("p (m l) -> p l m", l=CMP_STRIDE)
                for half in range(2):
                    ls = slice(half * 16, half * 16 + 16)
                    ins = pool.tensor_tensor(
                        blocks[:, v, ls, g * NCMP:(g + 1) * NCMP],
                        src[:, :, half:half + NCMP],
                        posT[:, v * 32 + half * 16:v * 32 + half * 16 + 16].unsqueeze(2).to_broadcast((P, 16, NCMP)),
                        ALU.add)
            ins.then_inc(tick(own, "blocks_ready"), 1)

        pool.wait_ge(sem("csum_ready"), 1)
        pool.tensor_tensor(sg, csum, sg, ALU.subtract).then_inc(tick(own, "cexc_ready"), 1)
        for pr in range(2):
            pool.wait_ge(*evacuated(f"sc{pr}_{H - 1}"))
            for s in MERGES:
                for gi in range(3):
                    if pr or s > 2:
                        prev = (pr, MERGES[MERGES.index(s) - 1]) if s > 2 else (0, 32)
                        pool.wait_ge(*filled(f"e{prev[0]}_{prev[1]}_{gi}"))
                    pool.tensor_tensor(
                        cms[gi], sc[:, gi * 4:(gi + 1) * 4, 0, :],
                        C(f"merge{s}").unsqueeze(1).to_broadcast((P, 4, P)), ALU.mult).then_inc(tick(own, "merge_part"), 1)

    @block.tensor
    def _(pe):
        def begin(name):
            if name in slot_no:
                r, v = landed[name]
                pe.wait_ge(slot_landed[r], v)
            for b, before in uses.get(name, ()):
                if before:
                    pe.wait_ge(bank_free[b], before)

        def slot(name, n=SLOT):
            r = slot_no[name] % RING
            return ring[:, r * SLOT:r * SLOT + n]

        def fm_unit(name, act, n=256):
            begin(name)
            w = slot(name, KT * n).rearrange("p (k n) -> p k n", k=KT)
            for c in range(0, n, P):
                m = min(P, n - c)
                for k in range(KT):
                    ins = pe.matmul(bank_of(name)[0:m, c * 2:c * 2 + S], w[:, k, c:c + m], act[:, k, :],
                                    start=(k == 0), stop=(k == KT - 1))
            ins.then_inc(unit_done, 1)

        def tm_unit(name, act, n=256):
            begin(name)
            w = slot(name, KT * n).rearrange("p (k n) -> p k n", k=KT)
            for qt in range(QT):
                for k in range(KT):
                    ins = pe.matmul(bank_of(name)[:, qt * 256:qt * 256 + n], act[:, k, qt * P:(qt + 1) * P],
                                    w[:, k, :], start=(k == 0), stop=(k == KT - 1))
            ins.then_inc(unit_done, 1)

        def row_unit(tag, j, n, act):
            name = f"{tag}{j}"
            begin(name)
            w = slot(name).rearrange("p (k n) -> p k n", k=2)
            for a in range(2):
                k = 2 * j + a
                for qt in range(QT):
                    for half in range(2):
                        ins = pe.matmul(bank_of(f"{tag}0", 2 * qt + half)[:, :], act[:, k, qt * P:(qt + 1) * P],
                                        w[:, a, half * 512:(half + 1) * 512], start=(k == 0), stop=(k == 2 * n - 1))
            ins.then_inc(unit_done, 1)

        fm_event = [0]

        def to_fm(ready, value):
            e = fm_event[0]
            fm_event[0] += 1
            pe.wait_ge(sem(ready), value)
            for j in range(4):
                for a in range(2):
                    for qt in range(QT):
                        k = 2 * j + a
                        src = (mem_tm if e == 0 else tm)[:, qt, k * P:(k + 1) * P]
                        ins = pe.transpose(bank[4 + j][:, a * S + qt * P:a * S + (qt + 1) * P], src, ident)
                ins.then_inc(sem("fm_full"), 1)

        def fm_ready():
            e = fm_event[0]
            pe.wait_ge(sem("fm_act"), 2 * e)
            pe.wait_ge(sem("fm_dve"), 2 * e)

        def scores(n):
            q, k, _, _, segs = head_parts(n)
            kind, i = heads[n]
            if n >= 2 and n - 2 in stage:
                pe.wait_ge(sem("exp_done"), n - 1)
            for qt, c, nk in segs:
                ins = pe.matmul(score_bank(n)[:, c:c + nk], q[:, qt * P:(qt + 1) * P], k[:, 0:nk],
                                start=True, stop=(kind != "fox"))
                if kind == "fox":
                    ins = pe.matmul(score_bank(n)[:, c:c + nk], sel[0:NFH, i, :], ccum[0:NFH, 0:nk],
                                    start=False, stop=True)
            ins.then_inc(sem("scores_full"), 1)

        def turn(n):
            pe.wait_ge(sem("exp_done"), n + 1)
            if n >= 1:
                pe.wait_ge(sem("pt_copied"), n)
            for qt, kt, c in blocks_of(n):
                ins = pe.transpose(pt_bank[:, c:c + P], sbuf_p[:, (n % 2) * 512 + c:(n % 2) * 512 + c + P], ident)
            ins.then_inc(sem("pt_full"), 1)

        def values(n):
            _, _, v, w, _ = head_parts(n)
            pe.wait_ge(sem("pt_copied"), n + 1)
            if n >= 2:
                pe.wait_ge(sem("o_read"), n - 1)
            bl = blocks_of(n)
            for qt in range(QT):
                mine = [(kt, c) for q, kt, c in bl if q == qt]
                for m, (kt, c) in enumerate(mine):
                    o = qt * P
                    ins = pe.matmul(o_bank(n)[:, o:o + w], sbuf_pt[:, (n % 2) * 512 + c:(n % 2) * 512 + c + P],
                                    v[:, kt, :], start=(m == 0), stop=(m == len(mine) - 1))
            ins.then_inc(sem("o_full"), 1)

        stage = ()

        def attention(which):
            nonlocal stage
            stage = STAGES[which]
            pe.wait_ge(bank_free[3], min(before for name, u in uses.items() for b, before in u
                                         if b == 3 and number[name] >= number[AFTER_STAGE[which]]))
            for n in range(stage[0], stage[-1] + 3):
                if n in stage:
                    scores(n)
                if n - 1 in stage:
                    turn(n - 1)
                if n - 2 in stage:
                    values(n - 2)

        def ffn(tag):
            for j in range(FT):
                fm_unit(f"{tag}_in{j}", fm)
            pe.wait_ge(*evacuated(f"{tag}_in{FT - 1}"))
            for j in range(FT // 2):
                row_unit(f"{tag}_out", j, FT // 2, hT)

        def wkv():
            pe.wait_ge(sem("wkv_ready"), 1)
            for pr in range(2):
                tok = slice(pr * P, (pr + 1) * P)
                for w, src in enumerate((b_fm, k_fm, v_fm)):
                    for h in range(2):
                        name = f"tr{pr}_{w}_{h}"
                        begin(name)
                        for a in range(3):
                            ins = pe.transpose(bank_of(name)[:, a * P:(a + 1) * P], src[:, 3 * h + a, tok], ident)
                        ins.then_inc(unit_done, 1)
                for u in range(H):
                    p, i = divmod(u, NT)
                    r = slice(p * DH, (p + 1) * DH)
                    name = f"sc{pr}_{u}"
                    begin(name)
                    both = ar[r, i, pr, :, :].rearrange("p b t -> p (b t)")
                    pe.matmul(bank_of(name)[:, 0:S], b_fm[r, i, tok], both, start=True, stop=True)
                    pe.matmul(bank_of(name)[:, S:2 * S], k_fm[r, i, tok], both, start=True, stop=True).then_inc(unit_done, 1)
                pe.wait_ge(*evacuated(f"tr{pr}_2_1"))
                for p in range(2):
                    begin(f"y0{pr}_{p}")
                    pe.wait_ge(*evacuated(f"sc{pr}_{p * NT + NT - 1}"))
                    for i in range(NT):
                        ins = pe.matmul(bank_of(f"y0{pr}_{p}")[:, i * DH:(i + 1) * DH], sc[:, p * NT + i, 2, :],
                                        kbv_tm[:, 2, (2 * i + p) * DH:(2 * i + p + 1) * DH], start=True, stop=True)
                    ins.then_inc(unit_done, 1)
                for gi in range(3):
                    begin(f"ti{pr}_{gi}")
                    pe.wait_ge(sem("tt_init"), 3 * pr + gi + 1)
                    for a in range(4):
                        ins = pe.transpose(bank_of(f"ti{pr}_{gi}")[:, a * P:(a + 1) * P], tt[:, 4 * gi + a, :], ident)
                    ins.then_inc(unit_done, 1)
                for li, s in enumerate(MERGES):
                    for gi in range(3):
                        name = f"e{pr}_{s}_{gi}"
                        begin(name)
                        pe.wait_ge(sem("merge_part"), 15 * pr + 3 * li + gi + 1)
                        if li:
                            for b in range(2):
                                pe.wait_ge(*evacuated(f"t{pr}_{MERGES[li - 1]}_{gi}", b))
                        else:
                            pe.wait_ge(*evacuated(f"ti{pr}_{gi}"))
                        for a in range(4):
                            ins = pe.matmul(bank_of(name)[:, a * P:(a + 1) * P], cms[gi][:, a, :], tms[gi][:, a, :],
                                            start=True, stop=True)
                        ins.then_inc(unit_done, 1)
                    for gi in range(3):
                        name = f"t{pr}_{s}_{gi}"
                        begin(name)
                        pe.wait_ge(*evacuated(f"e{pr}_{s}_{gi}"))
                        for a in range(4):
                            ins = pe.matmul(bank_of(name, 0)[:, a * P:(a + 1) * P], ems[gi][:, a, :],
                                            tt[:, 4 * gi + a, :], start=True, stop=True)
                        if s < 32:
                            for a in range(4):
                                ins = pe.matmul(bank_of(name, 1)[:, a * P:(a + 1) * P], tt[:, 4 * gi + a, :],
                                                ems[gi][:, a, :], start=True, stop=True)
                        ins.then_inc(unit_done, 1)
                for gi in range(3):
                    pe.wait_ge(*evacuated(f"t{pr}_32_{gi}"))
                pe.wait_ge(*evacuated(f"tr{pr}_0_1")), pe.wait_ge(*evacuated(f"tr{pr}_1_1"))
                for q in range(2):
                    c = 2 * pr + q
                    rq = slice(q * CH, (q + 1) * CH)
                    if c:
                        begin(f"z{c}c")
                        if c == 1:
                            pe.wait_ge(*evacuated("h0c"))
                        else:
                            pe.wait_ge(sem("state_ready"), c - 1)
                        for p in range(2):
                            r = slice(p * DH, (p + 1) * DH)
                            for i in range(NT):
                                ins = pe.matmul(bank_of(f"z{c}c", p)[rq, i * DH:(i + 1) * DH],
                                                ar[r, i, pr, 0, q * CH:(q + 1) * CH], state[r, c % 2, i, :],
                                                start=True, stop=True)
                        ins.then_inc(unit_done, 1)
                    begin(f"u{c}c")
                    for p in range(2):
                        pe.wait_ge(*evacuated(f"z{c}c" if c else "y00_" + str(p), p if c else 0))
                    for p in range(2):
                        for i in range(NT):
                            u = p * NT + i
                            ins = pe.matmul(bank_of(f"u{c}c", p)[rq, i * DH:(i + 1) * DH],
                                            tt[rq, u, q * CH:(q + 1) * CH], y0[rq, u * DH:(u + 1) * DH],
                                            start=True, stop=True)
                    ins.then_inc(unit_done, 1)
                    if c < 3:
                        begin(f"h{c}c")
                        for p in range(2):
                            pe.wait_ge(*evacuated(f"u{c}c", p))
                        for p in range(2):
                            r = slice(p * DH, (p + 1) * DH)
                            for i in range(NT):
                                hc = slice((2 * i + p) * DH, (2 * i + p + 1) * DH)
                                o = bank_of(f"h{c}c")[r, i * DH:(i + 1) * DH]
                                pe.matmul(o, kbv_tm[rq, 0, hc], u_tm[rq, (p * NT + i) * DH:(p * NT + i + 1) * DH],
                                          start=True, stop=False)
                                ins = pe.matmul(o, kbv_tm[rq, 1, hc], kbv_tm[rq, 2, hc], start=False, stop=True)
                        ins.then_inc(unit_done, 1)
                    if c:
                        begin(f"oi{c}c")
                        for p in range(2):
                            r = slice(p * DH, (p + 1) * DH)
                            for i in range(NT):
                                ins = pe.matmul(bank_of(f"oi{c}c", p)[r, i * DH:(i + 1) * DH], state[r, c % 2, i, :],
                                                ar[r, i, pr, 1, q * CH:(q + 1) * CH], start=True, stop=True)
                        ins.then_inc(unit_done, 1)
                begin(f"oo{pr}")
                for p in range(2):
                    pe.wait_ge(*evacuated(f"u{2 * pr + 1}c", p))
                for i in range(NT):
                    for p in range(2):
                        r = slice(p * DH, (p + 1) * DH)
                        u = p * NT + i
                        o = bank_of(f"oo{pr}", i // 3)[r, (i % 3) * P:(i % 3 + 1) * P]
                        pe.matmul(o, u_tm[:, u * DH:(u + 1) * DH], sc[:, u, 1, :], start=True, stop=False)
                        ins = pe.matmul(o, kbv_tm[:, 2, (2 * i + p) * DH:(2 * i + p + 1) * DH], sc[:, u, 3, :],
                                        start=False, stop=True)
                ins.then_inc(unit_done, 1)

        pe.wait_ge(sem("cst_in"), 16)
        pe.wait_ge(sem("vec_in"), VEC_DMAS * 16)
        pe.transpose(bank[0][:, 0:P], vec_rows, ident).then_inc(sem("table_full"), 1)
        pe.wait_ge(sem("pos_in"), 48)
        pe.transpose(bank[1][:, 0:72], pos_rows[0:72, :], ident[0:72, 0:72]).then_inc(sem("table_full"), 1)
        to_fm("tm_ready", 1)
        fm_ready()
        fm_unit("kmem0", fm)
        tm_unit("vmem0", fm)
        fm_unit("kmem1", mem1_fm)
        tm_unit("vmem1", mem1_fm)
        to_fm("tm_ready", 2)
        fm_ready()
        for j in range(3):
            fm_unit(f"q{j}", fm)
        fm_unit("kc", fm), fm_unit("vc", fm), fm_unit("ks", fm), tm_unit("vs", fm)
        fm_unit("kw", fm), tm_unit("vw", fm), tm_unit("gl", fm, 3 * H), fm_unit("qm0", fm)
        for v in range(2):
            pe.wait_ge(sem("blocks_ready"), v + 1)
            for half in range(2):
                name = f"hid{v}_{half}"
                begin(name)
                w = slot(name).rearrange("p (l e) -> p l e", l=16)
                for l in range(16):
                    for p in range(2):
                        r = slice(p * DH, (p + 1) * DH)
                        ins = pe.matmul(bank_of(f"hid{v}_0", p)[:, 0:2 * NCMP], w[r, l, :],
                                        blocks[r, v, half * 16 + l, :],
                                        start=(half == 0 and l == 0), stop=(half == 1 and l == 15))
                ins.then_inc(unit_done, 1)
        pe.wait_ge(sem("small_in"), 16 * SMALL_DMAS)
        begin("kcb")
        for p in range(2):
            pe.wait_ge(*evacuated("hid0_0", p))
        for p in range(2):
            ins = pe.matmul(bank_of("kcb")[p * DH:(p + 1) * DH, 0:2 * NCMP], cmp_w2[:, 0:DH],
                            hid[:, 0, p * 30:(p + 1) * 30], start=True, stop=True)
        ins.then_inc(unit_done, 1)
        begin("vcb")
        for p in range(2):
            pe.wait_ge(*evacuated("hid1_0", p))
        for g in range(G):
            o = (g % 2) * 30 + (g // 2) * NCMP
            ins = pe.matmul(bank_of("vcb")[0:NCMP, g * DH:(g + 1) * DH], hid[:, 1, o:o + NCMP],
                            cmp_w2[:, DH:2 * DH], start=True, stop=True)
        ins.then_inc(unit_done, 1)
        pe.wait_ge(*evacuated("kcb"))
        pe.wait_ge(*evacuated("q2"))
        for p in range(2):
            begin(f"cs{p}")
            r = slice(p * DH, (p + 1) * DH)
            for qt in range(QT):
                for i in range(NT):
                    c = (qt * NT + i) * 16
                    ins = pe.matmul(bank_of(f"cs{p}")[:, c:c + NCMP], qT[r, i, qt * P:(qt + 1) * P],
                                    kcb[r, (i // R) * NCMP:(i // R + 1) * NCMP], start=True, stop=True)
            ins.then_inc(unit_done, 1)
        pe.wait_ge(sem("pcmp_ready"), 1)
        for j in range(8):
            begin(f"pct{j}")
            p, qt, hf = j // 4, (j // 2) % 2, j % 2
            for a in range(3):
                ins = pe.transpose(bank_of(f"pct{j}")[0:NCMP, a * P:(a + 1) * P],
                                   s_cmp[:, p, qt, hf * 3 + a, 0:NCMP], ident)
            ins.then_inc(unit_done, 1)
        pe.wait_ge(*evacuated("vcb"))
        for j in range(4):
            p, qt = j // 2, j % 2
            begin(f"oc{j}")
            pe.wait_ge(*evacuated(f"pct{2 * j}"))
            pe.wait_ge(*evacuated(f"pct{2 * j + 1}"))
            for i in range(NT):
                g = 2 * (i // R) + p
                ins = pe.matmul(bank_of(f"oc{j}")[:, i * DH:(i + 1) * DH],
                                p_cmpT[0:NCMP, 2 * j + i // 3, (i % 3) * P:(i % 3 + 1) * P],
                                vcb[0:NCMP, g * DH:(g + 1) * DH], start=True, stop=True)
            ins.then_inc(unit_done, 1)
        for name in ("kmem0", "vmem0", "ks", "vs", "kw", "vw", "qm0"):
            pe.wait_ge(*evacuated(name))
        attention("mem0")
        to_fm("o_read", 28)
        fm_ready()
        for j in range(4):
            row_unit("wo0_", j, 4, fm)
        to_fm("tm_ready", 3)
        fm_ready()
        ffn("f0")

        to_fm("tm_ready", 4)
        fm_ready()
        for j in range(10):
            fm_unit(f"z{j}", fm)
        fm_unit("z10", fm, 32)
        fm_unit("qm1", fm)
        pe.wait_ge(sem("lora_ready"), 3)
        for n, r in (("w2", slice(0, DH)), ("a2", slice(DH, P))):
            for j in range(3):
                begin(f"{n}_{j}")
                for a in range(2):
                    i = 2 * j + a
                    ins = pe.matmul(bank_of(f"{n}_{j}")[:, a * S:(a + 1) * S], rw_wa2[r, i * P:(i + 1) * P],
                                    lora[r, 0, :], start=True, stop=True)
                ins.then_inc(unit_done, 1)
        for j in range(3):
            begin(f"g2_{j}")
            for a in range(2):
                i = 2 * j + a
                o = bank_of(f"g2_{j}")[:, a * S:(a + 1) * S]
                pe.matmul(o, rw_g2[:, i * P:(i + 1) * P], lora[:, 1, :], start=True, stop=False)
                ins = pe.matmul(o, rw_g2[0:32, MW + i * P:MW + (i + 1) * P], lora[0:32, 2, :], start=False, stop=True)
            ins.then_inc(unit_done, 1)
        for n, src in (("kn", kk_sq), ("bs", bonus)):
            pe.wait_ge(sem("sumsrc_ready"), 1 if n == "kn" else 2)
            for j in range(3):
                begin(f"{n}_{j}")
                ins = pe.matmul(bank_of(f"{n}_{j}")[:, :], C("head_ones"),
                                src[:, 2 * j:2 * j + 2, :].rearrange("p a t -> p (a t)"), start=True, stop=True)
                ins.then_inc(unit_done, 1)
        pe.wait_ge(*evacuated("qm1"))
        attention("mem1")
        begin("crT")
        pe.wait_ge(sem("o_read"), 32)
        for a in range(2):
            for qt in range(QT):
                ins = pe.transpose(bank_of("crT")[:, a * S + qt * P:a * S + (qt + 1) * P],
                                   cross[:, qt, a * P:(a + 1) * P], ident)
        ins.then_inc(unit_done, 1)
        wkv()
        for n in ("gm", "gv"):
            if n == "gm":
                for a in range(2):
                    pe.wait_ge(*evacuated("oo1", a))
            else:
                pe.wait_ge(sem("squares_ready"), 1)
            for j in range(3):
                src = y_fm if n == "gm" else zt
                begin(f"{n}_{j}")
                pe.matmul(bank_of(f"{n}_{j}")[:, :], C("head_ones"),
                              src[:, 2 * j:2 * j + 2, :].rearrange("p a t -> p (a t)"), start=True, stop=True).then_inc(unit_done, 1)
        pe.wait_ge(*evacuated("crT"))
        pe.wait_ge(sem("mix1_ready"), 1)
        for j in range(4):
            row_unit("wo1_", j, 4, fm)
        to_fm("tm_ready", 5)
        fm_ready()
        ffn("f1")

        for j in range(2):
            begin(f"wsT{j}")
            pe.wait_ge(sem("ws_in"), 16)
            for a in range(4):
                ins = pe.transpose(bank_of(f"wsT{j}")[:, a * P:(a + 1) * P], ws_raw[:, 4 * j + a, :], ident)
            ins.then_inc(unit_done, 1)
        to_fm("tm_ready", 6)
        fm_ready()
        for name in ("sv", "su"):
            for j in range(4):
                tm_unit(f"{name}{j}", fm)
        tm_unit("sf", fm, 8)
        for name in ("fq", "fk"):
            for j in range(4):
                fm_unit(f"{name}{j}", fm)
        for name in ("fv", "ga", "gb"):
            for j in range(4):
                tm_unit(f"{name}{j}", fm)
        begin("cc")
        pe.wait_ge(sem("logf_ready"), 1)
        o = bank_of("cc")
        pe.matmul(o[0:NFH, 0:P], logf[:, 0, :], C("tri"), start=True, stop=True)
        pe.matmul(o[0:NFH, P:S], logf[:, 0, :], C("ones"), start=True, stop=False)
        pe.matmul(o[0:NFH, P:S], logf[:, 1, :], C("tri"), start=False, stop=True).then_inc(unit_done, 1)
        pe.wait_ge(sem("vn_ready"), 1)
        for j in range(2):
            pe.wait_ge(*evacuated(f"wsT{j}"))
        for j in range(4):
            begin(f"sgu{j}")
            qt, half = j // 2, j % 2
            for a in range(4):
                g = 4 * half + a
                ins = pe.matmul(bank_of(f"sgu{j}")[:, a * P:(a + 1) * P], wsT[:, g, :],
                                v_n[:, qt, g * P:(g + 1) * P], start=True, stop=True)
            ins.then_inc(unit_done, 1)
        pe.wait_ge(*evacuated("cc"))
        for j in range(4):
            for name in ("fq", "fk", "fv"):
                pe.wait_ge(*evacuated(f"{name}{j}"))
        attention("fox")
        to_fm("tm_ready", 7)
        fm_ready()
        for j in range(4):
            row_unit("wo2_", j, 4, fm)
        to_fm("tm_ready", 8)
        fm_ready()
        ffn("f2")

    @block.scalar
    def _(act):
        own = counter("act_step")
        copy = ACT.Identity

        act.dma_start(cst[:, :], cst_d).then_inc(sem("cst_in"), 16)
        act.wait_ge(sem("vec_zero"), 1)
        for name, (o, k) in VEC.items():
            src = T[name]
            if name == "rw_mu":
                src = src[0:1, 0:k * P].rearrange("a (k c) -> (a k) c", c=P)
            elif name == "rw_r_k":
                src = src.rearrange("a (i h) d -> (a i) (h d)", h=2)
            else:
                src = src.rearrange("a (k c) -> (a k) c", c=P)
            act.dma_start(vec_rows[o:o + k, :], src).then_inc(sem("vec_in"), 16)
        act.dma_start(vec_rows[MU_LAST:MU_LAST + 1, 0:MU_TAIL], T["rw_mu"][0:1, 20 * P:]).then_inc(sem("vec_in"), 16)
        for p in range(2):
            act.dma_start(pos_rows[0:2 * CMP_BLOCK, p * DH:(p + 1) * DH],
                          T["nsa_cmp_pos"][0].rearrange("v l d -> (v l) d")).then_inc(sem("pos_in"), 16)
        act.dma_start(pos_rows[64:72, :], T["b_spatial_2"][0]).then_inc(sem("pos_in"), 16)
        smalls = [
            (cmp_w2[:, 0:DH], T["nsa_cmp_w2"][0, 0]), (cmp_w2[:, DH:2 * DH], T["nsa_cmp_w2"][0, 1]),
            (rw_wa2[0:DH, :], T["rw_w2"][0]), (rw_wa2[DH:P, :], T["rw_a2"][0]),
            (rw_g2[:, 0:MW], T["rw_g2"][0, 0:P]), (rw_g2[0:32, MW:2 * MW], T["rw_g2"][0, P:P + 32]),
            (gate_b, T["nsa_gate_b"].to_broadcast((P, 3 * H))),
            (b_forget, T["b_forget_2"].to_broadcast((P, NFH)))]
        for dst, src in smalls:
            act.dma_start(dst, src).then_inc(sem("small_in"), 16)

        def squares(r, src):
            if last(own):
                act.wait_ge(*last(own))
            act.activation(scratch[:, :], src[:, 0, :], ACT.Square, accum_out=ssq[:, r, 0:1]).then_inc(tick(own, "sq_act"), 1)

        def root(r):
            act.wait_ge(sem("ms_ready"), r + 1)
            act.activation(rms[:, r, :], ssq[:, r, :], ACT.Sqrt).then_inc(tick(own, "rt_ready"), 1)

        fm_event = [0]

        def from_banks(outs):
            e = fm_event[0]
            fm_event[0] += 1
            for j in range(2):
                act.wait_ge(sem("fm_full"), 4 * e + j + 1)
                for k in (2 * j, 2 * j + 1):
                    for dst, gain in outs:
                        b = bank[4 + j][:, (k % 2) * S:(k % 2 + 1) * S]
                        if gain is None:
                            ins = act.activation(dst[:, k, :], b, copy)
                        else:
                            ins = act.activation(dst[:, k, :], b, copy, scale=V(*gain(k)))
                ins.then_inc(tick(own, "fm_act"), 1)

        def evac(name, dst, func=copy, scale=1.0, src=None):
            act.wait_ge(*filled(name))
            act.activation(dst, bank_of(name)[:, :] if src is None else src, func, scale=scale).then_inc(freed(own, name), 1)

        def two(name):
            return bank_of(name)[:, :].rearrange("p (q c) -> p q c", q=2)

        def exps(n):
            kind, _ = heads[n]
            act.wait_ge(sem("nmax_ready"), n + 1)
            if n >= 2:
                act.wait_ge(sem("pt_full"), n - 1)
            for qt, c, nk in head_parts(n)[4]:
                src = score_bank(n) if kind in ("mem0", "mem1") else sbuf_s[:, (n % 2) * 512:]
                o = (n % 2) * 512 + c
                ins = act.activation(sbuf_p[:, o:o + nk], src[:, c:c + nk], ACT.Exp, bias=nmax[:, n, qt:qt + 1],
                                     accum_out=rsum[:, n, qt:qt + 1])
            ins.then_inc(tick(own, "exp_done"), 1)

        def copy_pt(n):
            act.wait_ge(sem("pt_full"), n + 1)
            if n >= 2:
                act.wait_ge(sem("o_full"), n - 1)
            w = P * len(blocks_of(n))
            act.activation(sbuf_pt[:, (n % 2) * 512:(n % 2) * 512 + w], pt_bank[:, 0:w], copy).then_inc(tick(own, "pt_copied"), 1)

        def attention(which):
            st = STAGES[which]
            for n in range(st[0], st[-1] + 2):
                if n in st:
                    exps(n)
                if n - 1 in st:
                    copy_pt(n - 1)

        def ffn(tag, base):
            for j in range(FT):
                act.wait_ge(*filled(f"{tag}_in{j}"))
                if j >= 2:
                    act.wait_ge(*evacuated(f"{tag}_in{j - 2}"))
                act.activation(silu[:, j % 2, :], bank_of(f"{tag}_in{j}")[:, 0:S], ACT.Silu).then_inc(tick(own, "silu_ready"), 1)

        act.wait_ge(sem("mem_in"), 16)
        squares(0, mem_tm)
        act.wait_ge(sem("x_in"), 16)
        squares(1, x_tm)
        root(0), root(1)
        act.wait_ge(sem("tables"), 2)
        from_banks([(fm, lambda k: ("norm_mem", k)), (mem1_fm, lambda k: ("norm_mem", 8 + k))])
        evac("kmem0", kmem0)
        evac("kmem1", kmem1[:, :])
        from_banks([(fm, lambda k: ("norm1", k))])
        for j in range(3):
            evac(f"q{j}", qT[:, 2 * j:2 * j + 2, :].rearrange("p i t -> p (i t)"), scale=DH ** -0.5)
        evac("ks", kselT.rearrange("p g t -> p (g t)"))
        evac("kw", kwinT.rearrange("p g t -> p (g t)"))
        evac("qm0", qmem[:, :], scale=DH ** -0.5)
        act.wait_ge(*evacuated("gl"))
        act.activation(gates, gates, ACT.Sigmoid).then_inc(tick(own, "gates_ready"), 1)
        for v in range(2):
            act.wait_ge(*filled(f"hid{v}_1"))
            for p in range(2):
                act.activation(hid[:, v, p * 30:(p + 1) * 30], bank_of(f"hid{v}_0", p)[:, 0:30],
                                        ACT.Gelu_apprx_tanh).then_inc(freed(own, f"hid{v}_0", p), 1)
        act.wait_ge(sem("scmp_ready"), 1)
        sall = s_cmp.rearrange("p h q i n -> p (h q i) n")[:, :, 0:NCMP]
        act.activation(sall, sall, ACT.Exp).then_inc(tick(own, "ecmp_ready"), 1)
        for j in range(8):
            evac(f"pct{j}", p_cmpT[0:NCMP, j, :], src=bank_of(f"pct{j}")[0:NCMP, 0:384])
        attention("mem0")
        from_banks([(fm, None)])
        act.wait_ge(*evacuated("wo0_0", 1))
        squares(2, x_tm)
        root(2)
        from_banks([(fm, lambda k: ("norm2", k))])
        ffn("f0", 0)
        act.wait_ge(*evacuated("f0_out0", 1))
        squares(3, x_tm)
        root(3)

        from_banks([(fm, lambda k: ("norm1", 8 + k))])
        zs = zshift[:, :].rearrange("p (b a t) -> p b a t", b=2, a=2)
        act.wait_ge(sem("zcol_ready"), 1)
        for j in range(11):
            if j >= 2:
                act.wait_ge(sem("zmix_ready"), j - 1)
            if j < 10:
                evac(f"z{j}", zs[:, j % 2, :, 1:S + 1], src=two(f"z{j}"))
            else:
                evac("z10", zs[0:32, 0, 0, 1:S + 1], src=bank_of("z10")[0:32, 0:S])
        evac("qm1", qmem[:, :], scale=DH ** -0.5)
        act.wait_ge(sem("zmix_ready"), 11)
        act.activation(lora[0:DH, 0, :], lora[0:DH, 0, :], ACT.Tanh).then_inc(tick(own, "lora_ready"), 1)
        act.activation(lora[:, 1, :], lora[:, 1, :], ACT.Sigmoid).then_inc(tick(own, "lora_ready"), 1)
        act.activation(lora[0:32, 2, :], lora[0:32, 2, :], ACT.Sigmoid).then_inc(tick(own, "lora_ready"), 1)
        for n, dst, b0 in (("w2", sg, "rw_w0"), ("a2", iclr, "rw_a0")):
            for j in range(3):
                act.wait_ge(*filled(f"{n}_{j}"))
                act.activation(dst[:, 2 * j, :], bank_of(f"{n}_{j}")[:, 0:S], ACT.Sigmoid, bias=V(b0, 2 * j))
                act.activation(dst[:, 2 * j + 1, :], bank_of(f"{n}_{j}")[:, S:2 * S], ACT.Sigmoid,
                                        bias=V(b0, 2 * j + 1)).then_inc(freed(own, f"{n}_{j}"), 1)
        for j in range(3):
            evac(f"kn_{j}", k_fm[:, 2 * j:2 * j + 2, :].rearrange("p a t -> p (a t)"), ACT.Sqrt)
        act.wait_ge(sem("csum_ready"), 1)
        flat = lambda a: a.rearrange("p i t -> p (i t)")
        act.activation(flat(e_in), flat(csum), ACT.Exp, scale=-C0).then_inc(tick(own, "exps_ready"), 1)
        act.activation(flat(e_neg), flat(csum), ACT.Exp, scale=C0).then_inc(tick(own, "exps_ready"), 1)
        act.wait_ge(sem("cexc_ready"), 1)
        act.activation(flat(sg), flat(sg), ACT.Exp, scale=-C0).then_inc(tick(own, "exps_ready"), 1)
        attention("mem1")
        evac("crT", fm[:, 6:8, :].rearrange("p k t -> p (k t)"))
        for pr in range(2):
            for w in range(3):
                evac(f"tr{pr}_{w}_1", kbv_tm[:, w, 384:768], src=bank_of(f"tr{pr}_{w}_1")[:, 0:384])
            for gi in range(3):
                evac(f"ti{pr}_{gi}", tms[gi].rearrange("p u t -> p (u t)"))
            for s in MERGES:
                for gi in range(3):
                    evac(f"e{pr}_{s}_{gi}", ems[gi].rearrange("p u t -> p (u t)"))
            for q in range(2):
                c = 2 * pr + q
                rq = slice(q * CH, (q + 1) * CH)
                act.wait_ge(*filled(f"u{c}c"))
                for p in range(2):
                    act.activation(u_tm[rq, p * 384:(p + 1) * 384], bank_of(f"u{c}c", p)[rq, 0:384], copy).then_inc(freed(own, f"u{c}c", p), 1)
                if c:
                    act.wait_ge(*filled(f"oi{c}c"))
                    act.wait_ge(sem("yzero_ready"), 1)
                    for p in range(2):
                        r = slice(p * DH, (p + 1) * DH)
                        act.activation(
                            y_fm[r, :, c * CH:(c + 1) * CH],
                            bank_of(f"oi{c}c", p)[r, 0:384].rearrange("p (i t) -> p i t", i=NT), copy).then_inc(freed(own, f"oi{c}c", p), 1)
        for j in range(3):
            act.wait_ge(*evacuated(f"gv_{j}"))
        act.activation(flat(zt), flat(zt), ACT.Sqrt).then_inc(tick(own, "gstd_ready"), 1)
        act.wait_ge(*evacuated("wo1_0", 1))
        squares(4, x_tm)
        root(4)
        from_banks([(fm, lambda k: ("norm2", 8 + k))])
        ffn("f1", FT)
        act.wait_ge(*evacuated("f1_out0", 1))
        squares(5, x_tm)
        root(5)

        act.wait_ge(sem("x2_ready"), 1)
        squares(6, x_tm)
        root(6)
        from_banks([(fm, lambda k: ("mix_pre_g_2", k))])
        for name, dst in (("sv", v_n), ("su", u_g)):
            for j in range(4):
                evac(f"{name}{j}", dst[:, :, j * 256:(j + 1) * 256], ACT.Gelu_apprx_tanh, src=two(f"{name}{j}"))
        act.wait_ge(sem("lnvar_ready"), 1)
        act.activation(mv[:, 4:6], mv[:, 4:6], ACT.Sqrt).then_inc(tick(own, "lnstd_ready"), 1)
        act.wait_ge(sem("fabs_ready"), 1)
        act.activation(tmpf[:, 1], tmpf[:, 1], ACT.Exp, scale=-1.0).then_inc(tick(own), 1)
        act.wait_ge(*last(own))
        act.activation(tmpf[:, 1], tmpf[:, 1], ACT.Ln, bias=1.0).then_inc(tick(own, "fln_ready"), 1)
        for j in range(4):
            evac(f"fq{j}", q2[:, 2 * j:2 * j + 2, :].rearrange("p i t -> p (i t)"), scale=P ** -0.5)
        for name, dst in (("ga", sga), ("gb", sgb)):
            for j in range(4):
                evac(f"{name}{j}", dst[:, :, j * 256:(j + 1) * 256], ACT.Sigmoid, src=two(f"{name}{j}"))
        attention("fox")
        from_banks([(fm, None)])
        act.wait_ge(*evacuated("wo2_0", 1))
        squares(7, u_g)
        root(7)
        act.wait_ge(sem("x3_ready"), 1)
        squares(8, x_tm)
        root(8)
        from_banks([(fm, lambda k: ("ffn_pre_g_2", k))])
        ffn("f2", 2 * FT)
        act.wait_ge(*evacuated("f2_out0", 1))
        squares(9, u_g)
        root(9)

    @block.vector
    def _(dve):
        own = counter("dve_step")
        flat = lambda a: a.rearrange("p i t -> p (i t)")

        def mean_square(r, src):
            dve.tensor_tensor_reduce(out=sbuf_s[:, :], in0=src[:, 1, :], in1=src[:, 1, :], scale=1.0, scalar=0.0,
                                              op0=ALU.mult, op1=ALU.add, accum_out=ssq[:, r, 1:2]).then_inc(tick(own), 1)
            dve.wait_ge(*last(own))
            dve.wait_ge(sem("sq_act"), r + 1)
            dve.tensor_scalar(ssq[:, r, :], ssq[:, r, :], 1.0 / D, EPS, ALU.mult, ALU.add).then_inc(tick(own, "ms_ready"), 1)

        def inverse(r):
            dve.wait_ge(sem("rt_ready"), r + 1)
            dve.reciprocal(rms[:, r, :], rms[:, r, :]).then_inc(tick(own), 1)
            dve.wait_ge(*last(own))

        def rms_norm(r, src, dst):
            mean_square(r, src)
            inverse(r)
            for qt in range(QT):
                ins = dve.tensor_scalar(dst[:, qt, :], src[:, qt, :], rms[:, r, qt:qt + 1], None, ALU.mult)
            ins.then_inc(tick(own, "tm_ready"), 1)

        def rms_gain(r, src, dst, gain):
            mean_square(r, src)
            inverse(r)
            for qt in range(QT):
                ins = dve.scalar_tensor_tensor(out=dst[:, qt, :], in0=src[:, qt, :], scalar=rms[:, r, qt:qt + 1],
                                               in1=gains[:, GAIN[gain], :], op0=ALU.mult, op1=ALU.mult)
            return ins

        fm_event = [0]

        def from_banks(outs):
            e = fm_event[0]
            fm_event[0] += 1
            for j in (2, 3):
                dve.wait_ge(sem("fm_full"), 4 * e + j + 1)
                for k in (2 * j, 2 * j + 1):
                    for dst, gain in outs:
                        b = bank[4 + j][:, (k % 2) * S:(k % 2 + 1) * S]
                        if gain is None:
                            ins = dve.tensor_copy(dst[:, k, :], b)
                        else:
                            ins = dve.tensor_scalar(dst[:, k, :], b, V(*gain(k)), None, ALU.mult)
                ins.then_inc(tick(own, "fm_dve"), 1)

        def evac(name, dst, src=None):
            dve.wait_ge(*filled(name))
            dve.tensor_copy(dst, bank_of(name)[:, :] if src is None else src).then_inc(freed(own, name), 1)

        def two(name):
            return bank_of(name)[:, :].rearrange("p (q c) -> p q c", q=2)

        def residual(tag, final):
            dve.wait_ge(*filled(final))
            for i in range(4):
                o = x_tm[:, i // 2, (i % 2) * 512:(i % 2 + 1) * 512]
                dve.tensor_tensor(o, bank_of(tag, i)[:, :], o, ALU.add).then_inc(freed(own, tag, i), 1)
            dve.wait_ge(*last(own))

        def maxima(n):
            kind, i = heads[n]
            dve.wait_ge(sem("scores_full"), n + 1)
            if kind in ("mem0", "mem1"):
                ins = dve.tensor_reduce(nmax[:, n, :], score_bank(n)[:, :].rearrange("p (q k) -> p q k", q=2),
                                        AX.X, ALU.max, negate=True)
                ins.then_inc(tick(own, "nmax_ready"), 1)
                return
            if n >= 2:
                dve.wait_ge(sem("exp_done"), n - 1)
            table = C("causal") if kind == "fox" else alibi[:, i, :]
            for qt, c, nk in head_parts(n)[4]:
                o = (n % 2) * 512 + c
                dve.tensor_tensor_reduce(
                    out=sbuf_s[:, o:o + nk], in0=score_bank(n)[:, c:c + nk], in1=table[:, c:c + nk], scale=1.0,
                    scalar=-3e38, op0=ALU.add, op1=ALU.max, accum_out=nmax[:, n, qt:qt + 1]).then_inc(tick(own), 1)
            dve.wait_ge(*last(own))
            dve.tensor_scalar(nmax[:, n, :], nmax[:, n, :], -1.0, None, ALU.mult).then_inc(tick(own, "nmax_ready"), 1)

        def finish(n):
            kind, i = heads[n]
            dve.wait_ge(sem("o_full"), n + 1)
            dve.reciprocal(coef[:, n, :], rsum[:, n, :]).then_inc(tick(own), 1)
            dve.wait_ge(*last(own))
            if kind in ("sel", "win"):
                br = 1 if kind == "sel" else 2
                dve.tensor_tensor(coef[:, n, :], coef[:, n, :], gates[:, :, br * H + i], ALU.mult).then_inc(tick(own), 1)
                dve.wait_ge(*last(own))
            for qt in range(QT):
                o = qt * P
                if kind in ("sel", "win"):
                    dst = tm[:, qt, i * DH:(i + 1) * DH]
                    ins = dve.scalar_tensor_tensor(out=dst, in0=o_bank(n)[:, o:o + DH], scalar=coef[:, n, qt:qt + 1],
                                                   in1=dst, op0=ALU.mult, op1=ALU.add)
                else:
                    w = P if kind == "fox" else DH
                    dst = {"mem0": tm[:, :, MW:], "mem1": cross, "fox": tm}[kind][:, qt, i * w:(i + 1) * w]
                    ins = dve.tensor_scalar(dst, o_bank(n)[:, o:o + w], coef[:, n, qt:qt + 1], None, ALU.mult)
            ins.then_inc(tick(own, "o_read"), 1)

        def attention(which):
            st = STAGES[which]
            for n in range(st[0], st[-1] + 3):
                if n in st:
                    maxima(n)
                if n - 2 in st:
                    finish(n - 2)
            dve.wait_ge(*last(own))

        def ffn(tag, base):
            for j in range(FT):
                dve.wait_ge(sem("silu_ready"), base + j + 1)
                dve.tensor_tensor(hT[:, j, :], bank_of(f"{tag}_in{j}")[:, S:2 * S], silu[:, j % 2, :],
                                           ALU.mult).then_inc(freed(own, f"{tag}_in{j}"), 1)

        dve.wait_ge(sem("table_full"), 1)
        dve.tensor_copy(vec[:, :], bank[0][:, 0:P]).then_inc(tick(own, "tables"), 1)
        dve.wait_ge(sem("table_full"), 2)
        dve.tensor_copy(posT, bank[1][:, 0:64])
        dve.tensor_copy(vecs2, bank[1][:, 64:72]).then_inc(tick(own, "tables"), 1)
        dve.wait_ge(*last(own))
        dve.wait_ge(sem("mem_in"), 16)
        rms_norm(0, mem_tm, mem_tm)
        dve.wait_ge(sem("x_in"), 16)
        rms_norm(1, x_tm, tm)
        from_banks([(fm, lambda k: ("norm_mem", k)), (mem1_fm, lambda k: ("norm_mem", 8 + k))])
        evac("vmem0", vmem0)
        evac("vmem1", vmem1[:, :])
        from_banks([(fm, lambda k: ("norm1", k))])
        evac("kc", kcvT[:, 0].rearrange("p g t -> p (g t)"))
        evac("vc", kcvT[:, 1].rearrange("p g t -> p (g t)"))
        evac("vs", vsel.rearrange("p q c -> p (q c)"))
        evac("vw", vwin.rearrange("p q c -> p (q c)"))
        dve.wait_ge(*filled("gl"))
        dve.wait_ge(sem("small_in"), 16 * SMALL_DMAS)
        dve.tensor_tensor(gates, two("gl")[:, :, 0:3 * H], gate_b.unsqueeze(1).to_broadcast((P, QT, 3 * H)),
                                   ALU.add).then_inc(freed(own, "gl"), 1)
        evac("kcb", kcb, src=bank_of("kcb")[:, 0:30])
        evac("vcb", vcb[0:NCMP, :], src=bank_of("vcb")[0:NCMP, 0:256])
        sv = s_cmp.rearrange("p h q i n -> p (h q i) n")
        bias = C("cmp_bias").rearrange("p (u n) -> p u n", n=16)
        for p in range(2):
            dve.wait_ge(*filled(f"cs{p}"))
            dve.tensor_tensor(
                sv[:, p * 12:(p + 1) * 12, 0:NCMP],
                bank_of(f"cs{p}")[:, 0:192].rearrange("p (u n) -> p u n", n=16)[:, :, 0:NCMP],
                bias[:, p * 12:(p + 1) * 12, 0:NCMP], ALU.add).then_inc(freed(own, f"cs{p}"), 1)
        dve.wait_ge(*last(own))
        dve.tensor_reduce(m_cmp, sv[:, :, 0:NCMP], AX.X, ALU.max).then_inc(tick(own), 1)
        dve.wait_ge(*last(own))
        dve.tensor_tensor(sv[:, :, 0:NCMP], sv[:, :, 0:NCMP],
                                     m_cmp.unsqueeze(2).to_broadcast((P, 24, NCMP)), ALU.subtract).then_inc(tick(own, "scmp_ready"), 1)
        dve.wait_ge(sem("ecmp_ready"), 1)
        dve.tensor_reduce(c_cmp, sv[:, :, 0:NCMP], AX.X, ALU.add).then_inc(tick(own), 1)
        dve.wait_ge(*last(own))
        mask = C("cmp_mask").rearrange("p (q n) -> p q n", q=QT)
        for p in range(2):
            for qt in range(QT):
                v = s_cmp[:, p, qt, :, 0:NCMP]
                ins = dve.tensor_tensor(v, v, mask[:, qt, 0:NCMP].unsqueeze(1).to_broadcast((P, NT, NCMP)), ALU.mult)
        ins.then_inc(tick(own, "pcmp_ready"), 1)
        dve.reciprocal(c_cmp, c_cmp).then_inc(tick(own), 1)
        dve.wait_ge(*last(own))
        dve.wait_ge(sem("gates_ready"), 1)
        cc4 = c_cmp.rearrange("p (h q g r) -> p h q g r", h=2, q=QT, g=2)
        gc = gates[:, :, 0:H].rearrange("p q (g h r) -> p h q g r", g=2, h=2)
        for p in range(2):
            dve.tensor_tensor(cc4[:, p], cc4[:, p], gc[:, p], ALU.mult).then_inc(tick(own), 1)
        dve.wait_ge(*last(own))
        for j in range(4):
            p, qt = divmod(j, 2)
            dve.wait_ge(*filled(f"oc{j}"))
            for gp in range(2):
                base = (2 * gp + p) * R * DH
                ins = dve.tensor_tensor(
                    tm[:, qt, base:base + R * DH].rearrange("p (r d) -> p r d", r=R),
                    bank_of(f"oc{j}")[:, gp * R * DH:(gp + 1) * R * DH].rearrange("p (r d) -> p r d", r=R),
                    cc4[:, p, qt, gp].unsqueeze(2).to_broadcast((P, R, DH)), ALU.mult)
            ins.then_inc(freed(own, f"oc{j}"), 1)
        dve.wait_ge(*last(own))
        dve.wait_ge(sem("alibi_ready"), 1)
        attention("mem0")
        from_banks([(fm, None)])
        residual("wo0_0", "wo0_3")
        rms_norm(2, x_tm, tm)
        from_banks([(fm, lambda k: ("norm2", k))])
        ffn("f0", 0)
        residual("f0_out0", f"f0_out{FT // 2 - 1}")
        rms_norm(3, x_tm, tm)

        zs = zshift[:, :].rearrange("p (b a t) -> p b a t", b=2, a=2)
        dve.memset(zs[:, :, :, 0:1], 0.0).then_inc(tick(own, "zcol_ready"), 1)
        dve.wait_ge(*last(own))
        from_banks([(fm, lambda k: ("norm1", 8 + k))])
        zd = zdelta[:, :].rearrange("p (a t) -> p a t", a=2)
        dsts = [r_fm[:, i, :] for i in range(NT)] + [kraw[:, i, :] for i in range(NT)] + \
               [v_fm[:, i, :] for i in range(NT)] + [lora[:, i, :] for i in range(3)]
        for j in range(11):
            dve.wait_ge(*evacuated(f"z{j}"))
            z = zs[:, j % 2]
            rows = slice(0, P) if j < 10 else slice(0, 32)
            n = 2 if j < 10 else 1
            dve.tensor_tensor(zd[rows, 0:n, :], z[rows, 0:n, 0:S], z[rows, 0:n, 1:S + 1], ALU.subtract).then_inc(tick(own), 1)
            dve.wait_ge(*last(own))
            for a in range(n):
                i = 2 * j + a
                mu = V("rw_mu", i) if j < 10 else vec[0:32, MU_LAST:MU_LAST + 1]
                ins = dve.scalar_tensor_tensor(out=dsts[i][rows], in0=zd[rows, a, :], scalar=mu,
                                               in1=z[rows, a, 1:S + 1], op0=ALU.mult, op1=ALU.add)
            ins.then_inc(tick(own, "zmix_ready"), 1)
            dve.wait_ge(*last(own))
        for i in range(NT):
            dve.tensor_scalar(kk[:, i, :], kraw[:, i, :], V("rw_k_k", i), None, ALU.mult).then_inc(tick(own), 1)
        dve.wait_ge(*last(own))
        dve.tensor_tensor(kk_sq, kk, kk, ALU.mult).then_inc(tick(own, "sumsrc_ready"), 1)
        for j in range(3):
            dve.wait_ge(*evacuated(f"w2_{j}"))
            for i in (2 * j, 2 * j + 1):
                ins = dve.tensor_tensor_scan(csum[:, i, :], C("chunk_keep"), sg[:, i, :], 0.0, ALU.mult, ALU.add)
        ins.then_inc(tick(own, "csum_ready"), 1)
        for j in range(3):
            evac(f"g2_{j}", g_fm[:, 2 * j:2 * j + 2, :].rearrange("p a t -> p (a t)"))
        for j in range(3):
            dve.wait_ge(*evacuated(f"kn_{j}"))
        dve.tensor_scalar(flat(k_fm), flat(k_fm), 1e-12, None, ALU.max).then_inc(tick(own), 1)
        dve.wait_ge(*last(own))
        dve.reciprocal(flat(k_fm), flat(k_fm)).then_inc(tick(own), 1)
        dve.wait_ge(*last(own))
        dve.scalar_tensor_tensor(out=flat(kk), in0=flat(kk), scalar=-1.0, in1=flat(k_fm),
                                          op0=ALU.mult, op1=ALU.mult).then_inc(tick(own), 1)
        dve.wait_ge(sem("exps_ready"), 3)
        for i in range(NT):
            dve.tensor_scalar(csum[:, i, :], iclr[:, i, :], 1.0, V("rw_k_a", i), ALU.subtract, ALU.mult).then_inc(tick(own), 1)
        dve.wait_ge(*last(own))
        dve.scalar_tensor_tensor(out=flat(kraw), in0=flat(csum), scalar=1.0, in1=flat(kraw),
                                          op0=ALU.add, op1=ALU.mult).then_inc(tick(own), 1)
        dve.wait_ge(*last(own))
        for i in range(NT):
            ins = dve.scalar_tensor_tensor(out=bonus[:, i, :], in0=r_fm[:, i, :], scalar=V("rw_r_k", i),
                                           in1=kraw[:, i, :], op0=ALU.mult, op1=ALU.mult)
        ins.then_inc(tick(own, "sumsrc_ready"), 1)
        dve.scalar_tensor_tensor(out=flat(b_fm), in0=flat(kk), scalar=-1.0, in1=flat(iclr),
                                          op0=ALU.mult, op1=ALU.mult).then_inc(tick(own), 1)
        dve.wait_ge(*last(own))
        dve.tensor_tensor(flat(b_fm), flat(b_fm), flat(e_neg), ALU.mult)
        dve.tensor_tensor(flat(k_fm), flat(kraw), flat(e_neg), ALU.mult)
        by_pair = lambda a: a.rearrange("p i (c t) -> p i c t", c=2)
        dve.tensor_tensor(ar[:, :, :, 0, :], by_pair(kk), by_pair(sg), ALU.mult)
        dve.tensor_tensor(ar[:, :, :, 1, :], by_pair(r_fm), by_pair(e_in), ALU.mult).then_inc(tick(own, "wkv_ready"), 1)
        dve.tensor_copy(p_end, e_in.rearrange("p i (c t) -> p i c t", t=CH)[:, :, :, CH - 1]).then_inc(tick(own), 1)
        dve.wait_ge(*last(own))
        dve.memset(y_fm[:, :, 0:CH], 0.0).then_inc(tick(own, "yzero_ready"), 1)
        for j in range(3):
            dve.wait_ge(*filled(f"bs_{j}"))
            t = slice(2 * j, 2 * j + 2)
            dve.tensor_tensor(bonus[:, t, :], two(f"bs_{j}"), v_fm[:, t, :], ALU.mult).then_inc(freed(own, f"bs_{j}"), 1)
        attention("mem1")
        wmask = C("wkv_mask").unsqueeze(1).to_broadcast((P, 2, S))
        for pr in range(2):
            tok = slice(pr * P, (pr + 1) * P)
            for w in range(3):
                evac(f"tr{pr}_{w}_0", kbv_tm[:, w, 0:384], src=bank_of(f"tr{pr}_{w}_0")[:, 0:384])
            for u in range(H):
                dve.wait_ge(*filled(f"sc{pr}_{u}"))
                dve.tensor_tensor(sc[:, u].rearrange("p (c b) t -> p c (b t)", c=2), two(f"sc{pr}_{u}"),
                                           wmask, ALU.mult).then_inc(freed(own, f"sc{pr}_{u}"), 1)
            dve.wait_ge(*last(own))
            for gi in range(3):
                us = slice(4 * gi, 4 * gi + 4)
                dve.tensor_tensor(tt[:, us, :], sc[:, us, 0, :],
                                           C("merge1").unsqueeze(1).to_broadcast((P, 4, P)), ALU.mult).then_inc(tick(own), 1)
                dve.wait_ge(*last(own))
                dve.tensor_tensor(tt[:, us, :], tt[:, us, :],
                                             ident.unsqueeze(1).to_broadcast((P, 4, P)), ALU.add).then_inc(tick(own, "tt_init"), 1)
            for p in range(2):
                evac(f"y0{pr}_{p}", y0[:, p * 384:(p + 1) * 384], src=bank_of(f"y0{pr}_{p}")[:, 0:384])
            for s in MERGES:
                for gi in range(3):
                    name = f"t{pr}_{s}_{gi}"
                    dve.wait_ge(*filled(name))
                    us = slice(4 * gi, 4 * gi + 4)
                    v4 = lambda b: b[:, :].rearrange("p (u t) -> p u t", u=4)
                    dve.tensor_tensor(tt[:, us, :], v4(bank_of(name, 0)), tt[:, us, :], ALU.add).then_inc(freed(own, name, 0), 1)
                    if s < 32:
                        dve.tensor_tensor(tms[gi], v4(bank_of(name, 1)), tms[gi], ALU.add).then_inc(freed(own, name, 1), 1)
                dve.wait_ge(*last(own))
            for q in range(2):
                c = 2 * pr + q
                rq = slice(q * CH, (q + 1) * CH)
                if c:
                    dve.wait_ge(*filled(f"z{c}c"))
                    for p in range(2):
                        y = y0[rq, p * 384:(p + 1) * 384]
                        dve.tensor_tensor(y, bank_of(f"z{c}c", p)[rq, 0:384], y, ALU.add).then_inc(freed(own, f"z{c}c", p), 1)
                if c < 3:
                    dve.wait_ge(*filled(f"h{c}c"))
                    new = state[:, (c + 1) % 2]
                    h = bank_of(f"h{c}c")[:, 0:384].rearrange("p (i v) -> p i v", i=NT)
                    decay = p_end[:, :, c].unsqueeze(2).to_broadcast((P, NT, DH))
                    if c:
                        dve.tensor_tensor(new, h, state[:, c % 2], ALU.add).then_inc(freed(own, f"h{c}c"), 1)
                        dve.wait_ge(*last(own))
                        dve.tensor_tensor(new, new, decay, ALU.mult).then_inc(tick(own, "state_ready"), 1)
                    else:
                        dve.tensor_tensor(new, h, decay, ALU.mult).then_inc(freed(own, f"h{c}c"), 1)
            dve.wait_ge(*filled(f"oo{pr}"))
            for c in (2 * pr, 2 * pr + 1):
                if c:
                    for p in range(2):
                        dve.wait_ge(*evacuated(f"oi{c}c", p))
            for a in range(2):
                y = y_fm[:, 3 * a:3 * a + 3, tok]
                dve.tensor_tensor(y, bank_of(f"oo{pr}", a)[:, 0:384].rearrange("p (i t) -> p i t", i=3), y,
                                           ALU.add).then_inc(freed(own, f"oo{pr}", a), 1)
        dve.wait_ge(*last(own))
        for j in range(3):
            dve.wait_ge(*filled(f"gm_{j}"))
            t = slice(2 * j, 2 * j + 2)
            dve.scalar_tensor_tensor(out=flat(y_fm[:, t, :]), in0=bank_of(f"gm_{j}")[:, :],
                                              scalar=-1.0 / DH, in1=flat(y_fm[:, t, :]), op0=ALU.mult, op1=ALU.add).then_inc(freed(own, f"gm_{j}"), 1)
        dve.wait_ge(*last(own))
        dve.tensor_tensor(zt, y_fm, y_fm, ALU.mult).then_inc(tick(own, "squares_ready"), 1)
        for j in range(3):
            dve.wait_ge(*filled(f"gv_{j}"))
            dve.tensor_scalar(flat(zt[:, 2 * j:2 * j + 2, :]), bank_of(f"gv_{j}")[:, :], 1.0 / DH, GN_EPS,
                                       ALU.mult, ALU.add).then_inc(freed(own, f"gv_{j}"), 1)
        dve.wait_ge(sem("gstd_ready"), 1)
        dve.reciprocal(flat(zt), flat(zt)).then_inc(tick(own), 1)
        dve.wait_ge(*last(own))
        dve.tensor_tensor(y_fm, y_fm, zt, ALU.mult).then_inc(tick(own), 1)
        dve.wait_ge(*last(own))
        for i in range(NT):
            dve.tensor_scalar(y_fm[:, i, :], y_fm[:, i, :], V("rw_lnx_w", i), V("rw_lnx_b", i),
                                       ALU.mult, ALU.add).then_inc(tick(own), 1)
        dve.wait_ge(*last(own))
        dve.tensor_tensor(y_fm, y_fm, bonus, ALU.add).then_inc(tick(own), 1)
        dve.wait_ge(*last(own))
        dve.tensor_tensor(fm[:, 0:NT, :], y_fm, g_fm, ALU.mult).then_inc(tick(own, "mix1_ready"), 1)
        residual("wo1_0", "wo1_3")
        rms_norm(4, x_tm, tm)
        from_banks([(fm, lambda k: ("norm2", 8 + k))])
        ffn("f1", FT)
        residual("f1_out0", f"f1_out{FT // 2 - 1}")

        dve.wait_ge(sem("gains_in"), 16 * len(GAIN))
        rms_gain(5, x_tm, x_tm, "final_norm").then_inc(tick(own, "x2_ready"), 1)
        dve.wait_ge(*last(own))
        for j in range(2):
            dve.wait_ge(*filled(f"wsT{j}"))
            dve.tensor_tensor(wsT[:, 4 * j:4 * j + 4, :],
                                       bank_of(f"wsT{j}")[:, :].rearrange("p (g t) -> p g t", g=4),
                                       C("tri").unsqueeze(1).to_broadcast((P, 4, P)), ALU.mult).then_inc(freed(own, f"wsT{j}"), 1)
        rms_norm(6, x_tm, tm)
        from_banks([(fm, lambda k: ("mix_pre_g_2", k))])
        for j in range(4):
            dve.wait_ge(*evacuated(f"sv{j}"))
        bnv = bn.rearrange("p (q a s) -> p q a s", q=2, a=2)
        mvv = mv[:, 0:4].rearrange("p (q s) -> p q s", q=2)
        for qt in range(QT):
            for a in range(2):
                dve.bn_stats(bnv[:, qt, a, :], v_n[:, qt, a * 512:(a + 1) * 512]).then_inc(tick(own), 1)
        dve.wait_ge(*last(own))
        for qt in range(QT):
            dve.bn_aggr(mvv[:, qt, :], bnv[:, qt].rearrange("p a s -> p (a s)")).then_inc(tick(own), 1)
        dve.wait_ge(*last(own))
        dve.tensor_scalar(mv[:, 4:6], mvv[:, :, 1], EPS, None, ALU.add).then_inc(tick(own, "lnvar_ready"), 1)
        dve.wait_ge(sem("lnstd_ready"), 1)
        dve.reciprocal(mv[:, 4:6], mv[:, 4:6]).then_inc(tick(own), 1)
        dve.wait_ge(*last(own))
        for qt in range(QT):
            dve.tensor_scalar(v_n[:, qt, :], v_n[:, qt, :], mvv[:, qt, 0:1], mv[:, 4 + qt:5 + qt],
                                       ALU.subtract, ALU.mult).then_inc(tick(own), 1)
        dve.wait_ge(*last(own))
        gsg = gains[:, GAIN["sgu_norm_g_2"], :].unsqueeze(1).to_broadcast((P, QT, D))
        dve.tensor_tensor(v_n, v_n, gsg, ALU.mult).then_inc(tick(own, "vn_ready"), 1)
        dve.wait_ge(*filled("sf"))
        dve.tensor_tensor(tmpf[:, 0], two("sf")[:, :, 0:NFH],
                                   b_forget.unsqueeze(1).to_broadcast((P, QT, NFH)), ALU.add).then_inc(freed(own, "sf"), 1)
        dve.wait_ge(*last(own))
        dve.tensor_scalar(tmpf[:, 2], tmpf[:, 0], -1.0, None, ALU.mult).then_inc(tick(own), 1)
        dve.wait_ge(*last(own))
        dve.tensor_tensor(tmpf[:, 1], tmpf[:, 0], tmpf[:, 2], ALU.max).then_inc(tick(own, "fabs_ready"), 1)
        dve.tensor_scalar(tmpf[:, 0], tmpf[:, 0], 0.0, None, ALU.min).then_inc(tick(own), 1)
        dve.wait_ge(sem("fln_ready"), 1)
        dve.wait_ge(*last(own))
        dve.tensor_tensor(logf, tmpf[:, 0], tmpf[:, 1], ALU.subtract).then_inc(tick(own, "logf_ready"), 1)
        dve.tensor_copy(sel[0:NFH], ident[0:NFH, 0:NFH].unsqueeze(2).to_broadcast((NFH, NFH, P))).then_inc(tick(own), 1)
        for j in range(4):
            evac(f"fk{j}", k2[:, 2 * j:2 * j + 2, :].rearrange("p i t -> p (i t)"))
        for j in range(4):
            evac(f"fv{j}", v_a[:, :, j * 256:(j + 1) * 256], src=two(f"fv{j}"))
        dve.wait_ge(*filled("cc"))
        dve.tensor_scalar(ccum[0:NFH, :], bank_of("cc")[0:NFH, 0:S], -1.0, None, ALU.mult).then_inc(freed(own, "cc"), 1)
        for j in range(4):
            dve.wait_ge(*evacuated(f"su{j}"))
            dve.wait_ge(*evacuated(f"ga{j}"))
            dve.wait_ge(*evacuated(f"gb{j}"))
        for j in range(4):
            dve.wait_ge(*filled(f"sgu{j}"))
            qt, half = divmod(j, 2)
            for a in range(4):
                g = 4 * half + a
                u = u_g[:, qt, g * P:(g + 1) * P]
                ins = dve.scalar_tensor_tensor(out=u, in0=bank_of(f"sgu{j}")[:, a * P:(a + 1) * P],
                                               scalar=vecs2[:, g:g + 1], in1=u, op0=ALU.add, op1=ALU.mult)
            ins.then_inc(freed(own, f"sgu{j}"), 1)
        dve.wait_ge(*last(own))
        dve.tensor_tensor(u_g, u_g, sga, ALU.mult).then_inc(tick(own), 1)
        attention("fox")
        dve.tensor_tensor(tm, tm, sgb, ALU.mult).then_inc(tick(own), 1)
        dve.wait_ge(*last(own))
        dve.tensor_tensor(tm, tm, u_g, ALU.add).then_inc(tick(own, "tm_ready"), 1)
        from_banks([(fm, None)])

        def product_out(tag, final):
            dve.wait_ge(*filled(final))
            for i in range(4):
                dve.tensor_copy(u_g[:, i // 2, (i % 2) * 512:(i % 2 + 1) * 512], bank_of(tag, i)[:, :]).then_inc(freed(own, tag, i), 1)
            dve.wait_ge(*last(own))

        product_out("wo2_0", "wo2_3")
        rms_gain(7, u_g, u_g, "mix_post_g_2").then_inc(tick(own), 1)
        dve.wait_ge(*last(own))
        dve.tensor_tensor(x_tm, x_tm, u_g, ALU.add).then_inc(tick(own, "x3_ready"), 1)
        dve.wait_ge(*last(own))
        rms_norm(8, x_tm, tm)
        from_banks([(fm, lambda k: ("ffn_pre_g_2", k))])
        ffn("f2", 2 * FT)
        product_out("f2_out0", f"f2_out{FT // 2 - 1}")
        rms_gain(9, u_g, u_g, "ffn_post_g_2").then_inc(tick(own), 1)
        dve.wait_ge(*last(own))
        dve.tensor_tensor(tm, u_g, x_tm, ALU.add).then_inc(tick(own, "y_done"), 1)


INPUTS = [
    "x", "mem", "norm1", "norm_mem", "w_mem_kv", "w_o", "norm2", "w_ffn_in", "w_ffn_out", "nsa_w_in", "nsa_gate_b",
    "nsa_cmp_pos", "nsa_cmp_w1", "nsa_cmp_w2", "rw_w_in", "rw_mu", "rw_w0", "rw_w2", "rw_a0", "rw_a2", "rw_g2",
    "rw_k_k", "rw_k_a", "rw_r_k", "rw_lnx_w", "rw_lnx_b", "final_norm", "mix_pre_g_2", "w_in_2", "b_forget_2",
    "sgu_norm_g_2", "w_spatial_2", "b_spatial_2", "w_out_2", "mix_post_g_2", "ffn_pre_g_2", "w_gate_2", "w_up_2",
    "w_down_2", "ffn_post_g_2"]


def kernel(**inputs):
    import numpy as _np
    import concourse.bacc as _bacc
    from concourse import mybir as _mybir
    from concourse.bass_utils import run_bass_kernel_spmd as _run

    nc = _bacc.Bacc("TRN2", target_bir_lowering=False, num_devices=1)
    arrays, tensors = {}, {}
    for name in INPUTS:
        a = _np.ascontiguousarray(inputs[name])
        arrays[f"in_{name}"] = a
        tensors[name] = nc.dram_tensor(f"in_{name}", a.shape, _mybir.dt.from_np(a.dtype), kind="ExternalInput").ap()
    constants = shape_constants()[1]
    arrays["shape_constants"] = constants
    tensors["shape_constants"] = nc.dram_tensor("shape_constants", constants.shape, F32, kind="ExternalInput").ap()
    out = nc.dram_tensor("out_0", (1, S, D), F32, kind="ExternalOutput").ap()
    kernel_program(nc, tensors, out)
    r = _run(nc, [arrays], core_ids=[0])
    return r.results[0]["out_0"]
```

```python
import math
from contextlib import ExitStack

import numpy as np

import concourse.bass as bass
from concourse import mybir

F32 = mybir.dt.float32
F32R = mybir.dt.float32r
ALU = mybir.AluOpType
ACT = mybir.ActivationFunctionType
AX = mybir.AxisListType

P = 128
D = 1024
S = 256
QT = S // P
KT = D // P
DH = 64
H = 12
G = 4
R = H // G
MH = 4
FFN = 2816
FT = FFN // P
CMP_BLOCK, CMP_STRIDE = 32, 16
NCMP = (S - CMP_BLOCK) // CMP_STRIDE + 1
CH = 64
NT = H * DH // P
EPS = 1e-6
GN_EPS = 64e-5
MERGES = (2, 4, 8, 16, 32)
NEG = -1e30
C0 = math.exp(-0.5)
NFH = 8
RING = 3
SPLITS = 2
PIECES = 2
SLOT = 2048


def alibi_slopes(n):
    def pow2(m):
        start = 2.0 ** (-8.0 / m)
        return [start ** (i + 1) for i in range(m)]
    c = 2 ** int(math.floor(math.log2(n)))
    s = pow2(c)
    if c < n:
        s = s + pow2(2 * c)[0::2][: n - c]
    return [float(np.float32(v)) for v in s]


SLOPES = alibi_slopes(H)


def head_of(p, i):
    gp, r = divmod(i, R)
    return (2 * gp + p) * R + r


def shape_constants():
    i = np.arange(P)[:, None]
    t = np.arange(P)[None, :]
    parts = {}
    parts["ident"] = (i == t)
    same = (i // CH) == (t // CH)
    parts["wkv_mask"] = np.concatenate([same & (i < t), same & (i <= t)], 1)
    for s in (1, 2, 4, 8, 16, 32):
        parts[f"merge{s}"] = (i // (2 * s) == t // (2 * s)) & (i % (2 * s) < s) & (t % (2 * s) >= s)
    parts["head_ones"] = (i // DH) == (t // DH)
    parts["tri"] = i <= t
    parts["ones"] = np.ones((P, P))
    dist, causal = [], []
    for qt in range(QT):
        k = np.arange((qt + 1) * P)[None, :]
        d = (qt * P + i) - k
        dist.append(np.where(d >= 0, -d, NEG))
        causal.append(np.where(d >= 0, 0.0, NEG))
    parts["dist"] = np.concatenate(dist, 1)
    parts["causal"] = np.concatenate(causal, 1)
    parts["chunk_keep"] = np.broadcast_to((np.arange(S)[None, :] % CH) != 0, (P, S))
    end = np.arange(16)[None, :] * CMP_STRIDE + CMP_BLOCK - 1
    bias = np.zeros((P, 2, QT, NT, 16))
    mask = np.zeros((P, QT, 16))
    for qt in range(QT):
        d = qt * P + i - end
        mask[:, qt] = (d >= 0) & (np.arange(16)[None, :] < NCMP)
        for p in range(2):
            for j in range(NT):
                bias[:, p, qt, j] = np.where(d >= 0, -SLOPES[head_of(p, j)] * d, NEG)
    parts["cmp_bias"] = bias.reshape(P, -1)
    parts["cmp_mask"] = mask.reshape(P, -1)
    at, cols = {}, 0
    for name, a in parts.items():
        at[name] = (cols, a.shape[1])
        cols += a.shape[1]
    return at, np.ascontiguousarray(np.concatenate([np.asarray(a, np.float32) for a in parts.values()], 1))


VEC = {}
for _n, _k in (("norm1", 16), ("norm_mem", 16), ("norm2", 16), ("mix_pre_g_2", 8), ("ffn_pre_g_2", 8),
               ("rw_w0", 6), ("rw_a0", 6), ("rw_k_k", 6), ("rw_k_a", 6), ("rw_r_k", 6),
               ("rw_lnx_w", 6), ("rw_lnx_b", 6), ("rw_mu", 20)):
    VEC[_n] = (sum(k for _, k in VEC.values()), _k)
MU_LAST = sum(k for _, k in VEC.values())
MU_TAIL = 32


def kernel_program(nc, T, out):
    ctx = ExitStack()
    with ctx:
        build(nc, T, out, ctx)


def build(nc, T, out, ctx):
    def sb(name, n):
        return ctx.enter_context(nc.sbuf_tensor(name, [P, n], F32))

    sems = {}

    def sem(name):
        if name not in sems:
            sems[name] = ctx.enter_context(nc.semaphore(name))
        return sems[name]

    CAT, cst_np = shape_constants()

    base = (nc.sbuf_base + 63) // 64 * 64
    fixed_at = [0]

    def place(name, n, at=None, dtype=F32):
        if at is None:
            column = fixed_at[0]
            fixed_at[0] += (n + 7) // 8 * 8
        else:
            column = SHARED + at
        assert base + 4 * (column + n) <= nc.sbuf_usable_end
        return nc.alloc_sbuf_tensor_at(name, [P, n], dtype, offset=base + 4 * column)[:, :]

    ring = place("ring", RING * SLOT)
    x_res = place("x_res", QT * D)
    act_hi = place("act_hi", KT * S, dtype=F32R)
    act_lo = place("act_lo", KT * S, dtype=F32R)
    rows_tm = place("rows_tm", QT * D)
    cst = place("cst", cst_np.shape[1])
    vec = place("vec", P)
    cmp_w2 = place("cmp_w2", 2 * DH)
    kmem1 = place("kmem1", 2 * S)
    vmem1 = place("vmem1", QT * 256)
    qmem = place("qmem", 2 * S)
    sbuf_s = place("sbuf_s", 2 * 512)
    sbuf_p = place("sbuf_p", 2 * 512)
    sbuf_pt = place("sbuf_pt", 2 * 512)
    zshift = place("zshift", 2 * 2 * (S + 1))
    zdelta = place("zdelta", 2 * S)
    small = place("small", 512)
    SHARED = fixed_at[0]
    ARENA = 28728
    arena = place("arena", ARENA, 0)
    W_HI, W_LO = 0, SPLITS * SLOT
    w_hi = place("w_hi", SPLITS * SLOT, W_HI, F32R)
    w_lo = place("w_lo", SPLITS * SLOT, W_LO, F32R)
    FREE = 2 * SPLITS * SLOT
    hT_hi = place("hT_hi", FT * S, FREE, F32R)
    hT_lo = place("hT_lo", FT * S, FREE + FT * S, F32R)
    HT_END = FREE + 2 * FT * S

    x_tm = x_res.rearrange("p (q c) -> p q c", q=QT)
    tm = rows_tm.rearrange("p (q c) -> p q c", q=QT)

    def tiles(a):
        return a.rearrange("p (k t) -> p k t", t=S)

    fm = (tiles(act_hi), tiles(act_lo))
    hT = (tiles(hT_hi), tiles(hT_lo))

    def C(name, rows=P):
        o, n = CAT[name]
        return cst[0:rows, o:o + n]

    ident = C("ident")

    def V(name, i, j=0):
        o, _ = VEC[name]
        return vec[:, o + i:o + i + 1]

    arena_at = [0]

    def take(n):
        a = arena[:, arena_at[0]:arena_at[0] + n]
        arena_at[0] += n
        assert arena_at[0] <= ARENA
        return a

    small_at = [0]

    def tiny(n):
        a = small[:, small_at[0]:small_at[0] + n]
        small_at[0] += n
        assert small_at[0] <= 512
        return a

    arena_at[0] = HT_END
    silu = take(2 * S).rearrange("p (b t) -> p b t", b=2)
    hidden = take(2 * S).rearrange("p (b t) -> p b t", b=2)
    L2_START = arena_at[0]
    arena_at[0] = FREE
    qT = take(NT * S).rearrange("p (i t) -> p i t", i=NT)
    kcvT = take(2 * 2 * S).rearrange("p (v g t) -> p v g t", v=2, g=2)
    kselT = take(2 * S).rearrange("p (g t) -> p g t", g=2)
    kwinT = take(2 * S).rearrange("p (g t) -> p g t", g=2)
    vsel = take(QT * 256).rearrange("p (q c) -> p q c", q=QT)
    vwin = take(QT * 256).rearrange("p (q c) -> p q c", q=QT)
    kmem0 = take(2 * S)
    vmem0 = take(QT * 256)
    blocks = take(2 * CMP_BLOCK * 2 * NCMP).rearrange("p (v l n) -> p v l n", v=2, l=CMP_BLOCK)
    hid = take(2 * 4 * NCMP).rearrange("p (v n) -> p v n", v=2)
    kcb = take(2 * NCMP)
    vcb = take(256)
    s_cmp = take(2 * QT * NT * 16).rearrange("p (h q i n) -> p h q i n", h=2, q=QT, i=NT)
    p_cmpT = take(8 * 384).rearrange("p (u c) -> p u c", u=8)
    arena_at[0] = ALIBI = (arena_at[0] + 7) // 8 * 8
    alibi = take(H * 384).rearrange("p (h c) -> p h c", h=H)
    posT = take(64)
    pos_rows = take(P)
    vec_rows = take(P)
    gate_b = take(3 * H)
    mem_tm = take(QT * D).rearrange("p (q c) -> p q c", q=QT)
    gates = tiny(QT * 3 * H).rearrange("p (q c) -> p q c", q=QT)
    rsum = tiny(2 * 40).rearrange("p (u q) -> p u q", q=QT)
    nmax = tiny(2 * 40).rearrange("p (u q) -> p u q", q=QT)
    coef = tiny(2 * 40).rearrange("p (u q) -> p u q", q=QT)
    ssq = tiny(2 * 10).rearrange("p (r q) -> p r q", q=QT)
    rms = tiny(2 * 10).rearrange("p (r q) -> p r q", q=QT)
    c_cmp = tiny(24)
    m_cmp = tiny(24)
    vecs2 = tiny(8)
    mem1_fm = (tiles(place("mem1_hi", KT * S, ALIBI, F32R)), tiles(place("mem1_lo", KT * S, ALIBI + KT * S, F32R)))

    arena_at[0] = 0
    ar = take(NT * 2 * 2 * P).rearrange("p (i c b t) -> p i c b t", i=NT, c=2, b=2)
    b_fm = take(NT * S).rearrange("p (i t) -> p i t", i=NT)
    k_fm = take(NT * S).rearrange("p (i t) -> p i t", i=NT)
    g_fm = take(NT * S).rearrange("p (i t) -> p i t", i=NT)
    bonus = take(NT * S).rearrange("p (i t) -> p i t", i=NT)
    v_fm = take(NT * S).rearrange("p (i t) -> p i t", i=NT)
    AFTER = arena_at[0]
    r_fm = take(NT * S).rearrange("p (i t) -> p i t", i=NT)
    kraw = take(NT * S).rearrange("p (i t) -> p i t", i=NT)
    lora = take(3 * S).rearrange("p (i t) -> p i t", i=3)
    iclr = take(NT * S).rearrange("p (i t) -> p i t", i=NT)
    sg = take(NT * S).rearrange("p (i t) -> p i t", i=NT)
    csum = take(NT * S).rearrange("p (i t) -> p i t", i=NT)
    e_in = take(NT * S).rearrange("p (i t) -> p i t", i=NT)
    kk = take(NT * S).rearrange("p (i t) -> p i t", i=NT)
    e_neg = rows_tm[:, 0:NT * S].rearrange("p (i t) -> p i t", i=NT)
    arena_at[0] = AFTER
    sc = take(H * 512).rearrange("p (u b t) -> p u b t", u=H, b=4)
    tt = take(H * P).rearrange("p (u t) -> p u t", u=H)
    tmat = take(2 * 512).rearrange("p (b u t) -> p b u t", b=2, u=4)
    emat = take(2 * 512).rearrange("p (b u t) -> p b u t", b=2, u=4)
    cmat = take(2 * 512).rearrange("p (b u t) -> p b u t", b=2, u=4)
    cmat3 = take(512)
    kbv_tm = take(3 * H * DH).rearrange("p (w c) -> p w c", w=3)
    p_end = tiny(NT * 4).rearrange("p (i c) -> p i c", i=NT)
    y_fm = rows_tm[:, 0:NT * S].rearrange("p (i t) -> p i t", i=NT)
    y0 = sbuf_s[:, 0:H * DH]
    u_tm = sbuf_p[:, 0:H * DH]
    state = sbuf_pt[:, 0:2 * NT * DH].rearrange("p (b i v) -> p b i v", b=2, i=NT)
    cross = zdelta.rearrange("p (q c) -> p q c", q=QT)
    zt = arena[:, AFTER:AFTER + NT * S].rearrange("p (i t) -> p i t", i=NT)
    kk_sq = b_fm
    mix_fm = zt
    arena_at[0] = ARENA - 3 * H * DH
    rw_wa2 = take(H * DH)
    rw_g2 = take(2 * H * DH)
    tms = [tmat[:, 0], tmat[:, 1], zshift[:, 0:512].rearrange("p (u t) -> p u t", u=4)]
    ems = [emat[:, 0], emat[:, 1], zshift[:, 512:1024].rearrange("p (u t) -> p u t", u=4)]
    cms = [cmat[:, 0], cmat[:, 1], cmat3.rearrange("p (u t) -> p u t", u=4)]
    VEC_DMAS, SMALL_DMAS = len(VEC) + 1, 4

    arena_at[0] = L2_START
    gains = take(4 * D).rearrange("p (g c) -> p g c", g=4)
    GAIN = {"final_norm": 0, "sgu_norm_g_2": 1, "mix_post_g_2": 2, "ffn_post_g_2": 3}
    u_g = take(QT * D).rearrange("p (q c) -> p q c", q=QT)
    v_a = take(QT * D)
    ws_raw = v_a[:, 0:NFH * P].rearrange("p (g t) -> p g t", g=NFH)
    v_a = v_a.rearrange("p (q c) -> p q c", q=QT)
    arena_at[0] = FREE
    q2, k2 = tiles(take(KT * S)), tiles(take(KT * S))
    logf = take(16).rearrange("p (q h) -> p q h", q=QT)
    tmpf = take(48).rearrange("p (a q h) -> p a q h", a=3, q=QT)
    ccum = take(S)
    sel = take(NFH * P).rearrange("p (h t) -> p h t", h=NFH)
    sga = take(QT * D).rearrange("p (q c) -> p q c", q=QT)
    sgb = take(QT * D).rearrange("p (q c) -> p q c", q=QT)
    v_n = take(QT * D).rearrange("p (q c) -> p q c", q=QT)
    assert arena_at[0] <= L2_START
    wsT = zshift[:, 0:NFH * P].rearrange("p (g t) -> p g t", g=NFH)
    bn = tiny(24)
    mv = tiny(8)
    b_forget = tiny(8)

    bank = [ctx.enter_context(nc.psum_tensor(f"bank{i}", [P, 512], F32)) for i in range(8)]

    number, uses, slots = {}, {}, []
    turn_of, fills = [0, 0], [0] * 8

    def unit(name, banks=1, slot=None, upper=False):
        number[name] = len(number)
        uses[name] = []
        for _ in range(banks):
            b = 4 + turn_of[1] % 4 if upper else turn_of[0] % 4
            turn_of[upper] += 1
            uses[name].append((b, fills[b]))
            fills[b] += 1
        if slot:
            slots.append((name, slot))

    def align():
        turn_of[0] += -turn_of[0] % 4


    def cols(w, a, b):
        return w[:, a:b].rearrange("(k p) n -> p k n", p=P)

    def slot_cols(w, a, b):
        return lambda dst: [(dst[:, 0:KT * (b - a)].rearrange("p (k n) -> p k n", k=KT), cols(w, a, b))]

    def slot_rows(w, j):
        return lambda dst: [(dst.rearrange("p (k n) -> p k n", k=2),
                             w[2 * j * P:(2 * j + 2) * P, :].rearrange("(k p) n -> p k n", p=P))]

    def slot_pair(wa, a, wb, b):
        return lambda dst: [
            (dst.rearrange("p (k n) -> p k n", k=KT)[:, :, 0:P], cols(wa, a, a + P)),
            (dst.rearrange("p (k n) -> p k n", k=KT)[:, :, P:2 * P], cols(wb, b, b + P))]

    def slot_q(w, j):
        def loads(dst):
            d = dst.rearrange("p (k n) -> p k n", k=KT)
            for a in range(2):
                for p in range(2):
                    h = head_of(p, 2 * j + a)
                    yield (d[:, :, a * P + p * DH:a * P + (p + 1) * DH], cols(w, h * DH, (h + 1) * DH))
        return loads

    def slot_cmp(v, half):
        def loads(dst):
            w = T["nsa_cmp_w1"][0, v, half * 16:half * 16 + 16].rearrange("l d e -> d l e")
            for p in range(2):
                yield (dst[p * DH:(p + 1) * DH, :].rearrange("p (l e) -> p l e", l=16), w)
        return loads

    def ffn_units(tag, wa, a0, wb, b0, wo):
        for j in range(FT):
            unit(f"{tag}_in{j}", 1, slot_pair(wa, a0 + j * P, wb, b0 + j * P))
        align()
        for j in range(FT // 2):
            unit(f"{tag}_out{j}", 4 if j == 0 else 0, slot_rows(wo, j))

    nsa = T["nsa_w_in"][0]
    MW = H * DH
    GL = MW + 6 * 256
    proj = {name: slot_cols(nsa, MW + j * 256, MW + (j + 1) * 256)
            for j, name in enumerate(("kc", "vc", "ks", "vs", "kw", "vw"))}
    proj |= {f"q{j}": slot_q(nsa, j) for j in range(3)}
    proj |= {"gl": slot_cols(nsa, GL, GL + 3 * H), "qm0": slot_cols(nsa, GL + 3 * H, GL + 3 * H + 256)}
    for name in ("kc", "vc", "q0", "q1", "q2", "ks", "vs", "kw", "vw", "gl", "qm0"):
        unit(name, 1, proj[name])
    mem_w = {f"{n}mem{l}": slot_cols(T["w_mem_kv"][l], o, o + 256) for l in range(2) for n, o in (("k", 0), ("v", 256))}
    unit("kmem0", 1, mem_w["kmem0"])
    for v in range(2):
        unit(f"hid{v}_0", 2, slot_cmp(v, 0))
        unit(f"hid{v}_1", 0, slot_cmp(v, 1))
    unit("vmem0", 1, mem_w["vmem0"])
    unit("kcb"), unit("vcb")
    unit("kmem1", 1, mem_w["kmem1"])
    unit("cs0"), unit("cs1")
    unit("vmem1", 1, mem_w["vmem1"])
    for j in range(8):
        unit(f"pct{j}")
    for j in range(4):
        unit(f"oc{j}")
    align()
    for j in range(4):
        unit(f"wo0_{j}", 4 if j == 0 else 0, slot_rows(T["w_o"][0], j))
    ffn_units("f0", T["w_ffn_in"][0], 0, T["w_ffn_in"][0], FFN, T["w_ffn_out"][0])
    rw = T["rw_w_in"][0]
    for j in range(10):
        unit(f"z{j}", 1, slot_cols(rw, j * 256, (j + 1) * 256))
    unit("z10", 1, slot_cols(rw, 2560, 2560 + P))
    unit("qm1", 1, slot_cols(rw, 2592, 2848))
    for n in ("w2", "a2", "g2", "kn", "bs"):
        for j in range(3):
            unit(f"{n}_{j}")
    unit("crT")
    for pr in range(2):
        for w in range(3):
            for h in range(2):
                unit(f"tr{pr}_{w}_{h}", 1, upper=True)
        for u in range(H):
            unit(f"sc{pr}_{u}", 1, upper=True)
        for p in range(2):
            unit(f"y0{pr}_{p}", 1)
        for gi in range(3):
            unit(f"ti{pr}_{gi}", 1)
        for s in MERGES:
            for gi in range(3):
                unit(f"e{pr}_{s}_{gi}", 1, upper=True)
            for gi in range(3):
                unit(f"t{pr}_{s}_{gi}", 1 if s == 32 else 2)
        for c in (2 * pr, 2 * pr + 1):
            if c:
                unit(f"z{c}c", 2, upper=True)
            unit(f"u{c}c", 2)
            if c < 3:
                unit(f"h{c}c", 1, upper=True)
            if c:
                unit(f"oi{c}c", 2, upper=True)
        unit(f"oo{pr}", 2)
    for n in ("gm", "gv"):
        for j in range(3):
            unit(f"{n}_{j}")
    align()
    for j in range(4):
        unit(f"wo1_{j}", 4 if j == 0 else 0, slot_rows(T["w_o"][1], j))
    ffn_units("f1", T["w_ffn_in"][1], 0, T["w_ffn_in"][1], FFN, T["w_ffn_out"][1])
    w2in = T["w_in_2"][0]
    unit("wsT0"), unit("wsT1")
    for name, base2 in (("sv", 1024), ("su", 0)):
        for j in range(4):
            unit(f"{name}{j}", 1, slot_cols(w2in, base2 + j * 256, base2 + (j + 1) * 256))
    unit("sf", 1, slot_cols(w2in, 7168, 7176))
    for name, base2 in (("fq", 2048), ("fk", 3072), ("fv", 4096)):
        for j in range(4):
            unit(f"{name}{j}", 1, slot_cols(w2in, base2 + j * 256, base2 + (j + 1) * 256))
    unit("cc")
    for j in range(4):
        unit(f"sgu{j}")
    GATE_UNITS = []
    for name, base2 in (("ga", 5120), ("gb", 6144)):
        for j in range(4):
            GATE_UNITS.append(f"{name}{j}")
            unit(f"{name}{j}", 1, slot_cols(w2in, base2 + j * 256, base2 + (j + 1) * 256))
    align()
    for j in range(4):
        unit(f"wo2_{j}", 4 if j == 0 else 0, slot_rows(T["w_out_2"][0], j))
    ffn_units("f2", T["w_gate_2"][0], 0, T["w_up_2"][0], 0, T["w_down_2"][0])

    slot_no = {name: n for n, (name, _) in enumerate(slots)}
    landed, total = {}, [0] * RING
    for n, (name, loads) in enumerate(slots):
        k = len(list(loads(ring[:, 0:SLOT])))
        total[n % RING] += 16 * k
        landed[name] = (n % RING, total[n % RING])

    split_names = [name for name, _ in slots if not name.startswith("hid")]
    split_no = {name: m for m, name in enumerate(split_names)}
    width = {name: SLOT for name in split_names}
    width |= {"gl": KT * 3 * H, "sf": KT * NFH, "z10": KT * P}

    HOLD = {"qm0": "kmem0", "kmem0": "kmem0", "z10": "qm1"}

    def split_end(name):
        if name in HOLD:
            return split_no[HOLD[name]] + 1
        return min(split_no[name] + SPLITS + 1, len(split_names))

    def pieces(name):
        w = width[name] // PIECES
        return [(i * w, (i + 1) * w) for i in range(PIECES)]

    unit_done = sem("unit_done")
    slot_landed = [sem(f"slot_landed{r}") for r in range(RING)]
    bank_free = [sem(f"bank_free{b}") for b in range(8)]

    def bank_of(name, i=0):
        return bank[uses[name][i][0]]

    def filled(name):
        return unit_done, number[name] + 1

    def evacuated(name, i=0):
        b, before = uses[name][i]
        return bank_free[b], before + 1

    def counter(name):
        return {"step": name, "counts": {}, "last": None}

    def tick(own, name=None):
        name = name or own["step"]
        own["counts"][name] = own["counts"].get(name, 0) + 1
        own["last"] = (sem(name), own["counts"][name])
        return sem(name)

    def freed(own, name, i=0):
        b, before = uses[name][i]
        own["last"] = (bank_free[b], before + 1)
        return bank_free[b]

    def last(own):
        return own["last"]

    hid_base = {"f0": 0, "f1": FT, "f2": 2 * FT}

    heads = [("mem0", i) for i in range(MH)]
    for h in range(H):
        heads += [("sel", h), ("win", h)]
    heads += [("mem1", i) for i in range(MH)]
    heads += [("fox", i) for i in range(NFH)]
    first = {}
    for n, (kind, _) in enumerate(heads):
        first.setdefault(kind, n)
    AFTER_STAGE = {"mem0": "wo0_0", "mem1": "crT"}
    STAGES = {"mem0": range(0, 28), "mem1": range(28, 32), "fox": range(32, 40)}

    def head_parts(n):
        kind, i = heads[n]
        if kind in ("mem0", "mem1"):
            k = (kmem0 if kind == "mem0" else kmem1[:, :]).rearrange("p (g t) -> p g t", g=2)
            v = (vmem0 if kind == "mem0" else vmem1[:, :]).rearrange("p (q c) -> p q c", q=QT)
            q = qmem[:, :].rearrange("p (g t) -> p g t", g=2)
            r = slice((i % 2) * DH, (i % 2) * DH + DH)
            return q[r, i // 2, :], k[r, i // 2, :], v[:, :, i * DH:(i + 1) * DH], DH, [(0, 0, S), (1, S, S)]
        causal = [(0, 0, P), (1, P, S)]
        if kind == "fox":
            return q2[:, i, :], k2[:, i, :], v_a[:, :, i * P:(i + 1) * P], P, causal
        g, r = divmod(i, R)
        p, gp = g % 2, g // 2
        rows = slice(p * DH, (p + 1) * DH)
        k = kselT if kind == "sel" else kwinT
        v = vsel if kind == "sel" else vwin
        return qT[rows, gp * R + r, :], k[rows, gp, :], v[:, :, g * DH:(g + 1) * DH], DH, causal

    def blocks_of(n):
        *_, segs = head_parts(n)
        return [(qt, kt, c + kt * P) for qt, c, nk in segs for kt in range(nk // P)]

    score_bank = lambda n: bank[4 + n % 2]
    pt_bank = bank[6]
    o_bank = lambda n: bank[3 if n % 2 and heads[n][0] != "fox" else 7]

    cst_d = T["shape_constants"]
    block = ctx.enter_context(nc.Block())

    @block.sync
    def _(sp):
        sp.dma_start(mem_tm, T["mem"][0].rearrange("(q p) c -> p q c", p=P)).then_inc(sem("mem_in"), 16)
        sp.dma_start(x_tm, T["x"][0].rearrange("(q p) c -> p q c", p=P)).then_inc(sem("x_in"), 16)
        for n, (name, loads) in enumerate(slots):
            if n >= RING:
                before = slots[n - RING][0]
                if before in split_no:
                    sp.wait_ge(sem("lo_ready"), PIECES * (split_no[before] + 1))
                else:
                    sp.wait_ge(*filled(before))
            if name == "f0_in4":
                sp.wait_ge(*filled("f0_in0"))
                for dst, src in ((rw_wa2[0:DH, :], T["rw_w2"][0]), (rw_wa2[DH:P, :], T["rw_a2"][0]),
                                 (rw_g2[:, 0:MW], T["rw_g2"][0, 0:P]),
                                 (rw_g2[0:32, MW:2 * MW], T["rw_g2"][0, P:P + 32])):
                    sp.dma_start(dst, src).then_inc(sem("lora_in"), 16)
            if name == "f1_in4":
                sp.wait_ge(unit_done, number["f1_in0"] + 1)
                for gn, g in GAIN.items():
                    src = T[gn].rearrange("(a c) -> a c", a=1) if gn == "final_norm" else T[gn]
                    sp.dma_start(gains[:, g, :], src.to_broadcast((P, D))).then_inc(sem("gains_in"), 16)
                sp.dma_start(ws_raw, T["w_spatial_2"][0].rearrange("g t s -> t g s")).then_inc(sem("ws_in"), 16)
            r = n % RING
            for dst, src in loads(ring[:, r * SLOT:(r + 1) * SLOT]):
                sp.dma_start(dst, src).then_inc(slot_landed[r], 16)
        sp.wait_ge(sem("y_done"), 1)
        sp.dma_start(out[0].rearrange("(q p) c -> p q c", p=P), tm).then_inc(sem("y_out"), 16)
        sp.wait_ge(sem("y_out"), 16)

    @block.gpsimd
    def _(pool):
        own = counter("pool_step")
        pool.memset(vec_rows, 0.0).then_inc(tick(own, "vec_zero"), 1)
        pool.wait_ge(sem("tables"), 2)
        for v in range(2):
            pool.wait_ge(*evacuated(("kc", "vc")[v]))
            for g in range(2):
                src = kcvT[:, v, g, :].rearrange("p (m l) -> p l m", l=CMP_STRIDE)
                for half in range(2):
                    ls = slice(half * 16, half * 16 + 16)
                    ins = pool.tensor_tensor(
                        blocks[:, v, ls, g * NCMP:(g + 1) * NCMP],
                        src[:, :, half:half + NCMP],
                        posT[:, v * 32 + half * 16:v * 32 + half * 16 + 16].unsqueeze(2).to_broadcast((P, 16, NCMP)),
                        ALU.add)
            ins.then_inc(tick(own, "blocks_ready"), 1)

        pool.wait_ge(sem("cst_in"), 16)
        pool.wait_ge(*filled("vmem1"))
        for h in range(H):
            ins = pool.tensor_scalar(alibi[:, h, :], C("dist"), SLOPES[h], None, ALU.mult)
        ins.then_inc(tick(own, "alibi_ready"), 1)
        pool.wait_ge(sem("csum_ready"), 1)
        pool.tensor_tensor(sg, csum, sg, ALU.subtract).then_inc(tick(own, "cexc_ready"), 1)
        for pr in range(2):
            pool.wait_ge(*evacuated(f"sc{pr}_{H - 1}"))
            for s in MERGES:
                for gi in range(3):
                    if pr or s > 2:
                        prev = (pr, MERGES[MERGES.index(s) - 1]) if s > 2 else (0, 32)
                        pool.wait_ge(*filled(f"e{prev[0]}_{prev[1]}_{gi}"))
                    pool.tensor_tensor(
                        cms[gi], sc[:, gi * 4:(gi + 1) * 4, 0, :],
                        C(f"merge{s}").unsqueeze(1).to_broadcast((P, 4, P)), ALU.mult).then_inc(tick(own, "merge_part"), 1)

    @block.tensor
    def _(pe):
        def begin(name):
            if name in slot_no and name not in split_no:
                r, v = landed[name]
                pe.wait_ge(slot_landed[r], v)
            for b, before in uses.get(name, ()):
                if before:
                    pe.wait_ge(bank_free[b], before)

        def slot(name):
            r = slot_no[name] % RING
            return ring[:, r * SLOT:(r + 1) * SLOT]

        def split(name, k):
            b, n = split_no[name] % SPLITS, width[name]
            return [w[:, b * SLOT:b * SLOT + n].rearrange("p (k n) -> p k n", k=k) for w in (w_hi, w_lo)]

        def piece(name, i):
            pe.wait_ge(sem("lo_ready"), PIECES * split_no[name] + i + 1)

        def product(o, ahl, bhl, first, final):
            pe.matmul(o, ahl[0], bhl[0], start=first, stop=False)
            pe.matmul(o, ahl[0], bhl[1], start=False, stop=False)
            return pe.matmul(o, ahl[1], bhl[0], start=False, stop=final)

        def fm_unit(name, act):
            begin(name)
            n = width[name] // KT
            w = split(name, KT)
            for c in range(0, n, P):
                for k in range(KT):
                    if c == 0 and k % (KT // PIECES) == 0:
                        piece(name, k // (KT // PIECES))
                    ins = product(bank_of(name)[:, c * 2:c * 2 + S], [a[:, k, c:c + P] for a in w],
                                  [a[:, k, :] for a in act], k == 0, k == KT - 1)
            ins.then_inc(unit_done, 1)

        def tm_unit(name, act):
            begin(name)
            n = width[name] // KT
            w = split(name, KT)
            for qt in range(QT):
                for k in range(KT):
                    if qt == 0 and k % (KT // PIECES) == 0:
                        piece(name, k // (KT // PIECES))
                    ins = product(bank_of(name)[:, qt * 256:qt * 256 + n],
                                  [a[:, k, qt * P:(qt + 1) * P] for a in act], [a[:, k, :] for a in w],
                                  k == 0, k == KT - 1)
            ins.then_inc(unit_done, 1)

        def row_unit(tag, j, n, act):
            name = f"{tag}{j}"
            begin(name)
            w = split(name, 2)
            for a in range(2):
                k = 2 * j + a
                piece(name, a)
                for qt in range(QT):
                    for half in range(2):
                        ins = product(bank_of(f"{tag}0", 2 * qt + half)[:, :],
                                      [v[:, k, qt * P:(qt + 1) * P] for v in act],
                                      [v[:, a, half * 512:(half + 1) * 512] for v in w], k == 0, k == 2 * n - 1)
            ins.then_inc(unit_done, 1)

        fm_event = [0]

        def to_fm(ready, value):
            e = fm_event[0]
            fm_event[0] += 1
            pe.wait_ge(sem(ready), value)
            for j in range(4):
                for a in range(2):
                    for qt in range(QT):
                        k = 2 * j + a
                        src = (mem_tm if e == 1 else tm)[:, qt, k * P:(k + 1) * P]
                        ins = pe.transpose(bank[4 + j][:, a * S + qt * P:a * S + (qt + 1) * P], src, ident)
                ins.then_inc(sem("fm_full"), 1)

        def fm_ready():
            e = fm_event[0]
            pe.wait_ge(sem("fm_lo"), 4 * e)

        def scores(n):
            q, k, _, _, segs = head_parts(n)
            kind, i = heads[n]
            if n >= 2 and n - 2 in stage:
                pe.wait_ge(sem("exp_done"), n - 1)
            for qt, c, nk in segs:
                ins = pe.matmul(score_bank(n)[:, c:c + nk], q[:, qt * P:(qt + 1) * P], k[:, 0:nk],
                                start=True, stop=(kind != "fox"))
                if kind == "fox":
                    ins = pe.matmul(score_bank(n)[:, c:c + nk], sel[0:NFH, i, :], ccum[0:NFH, 0:nk],
                                    start=False, stop=True)
            ins.then_inc(sem("scores_full"), 1)

        def turn(n):
            pe.wait_ge(sem("exp_done"), n + 1)
            if n >= 1:
                pe.wait_ge(sem("pt_copied"), n)
            for qt, kt, c in blocks_of(n):
                ins = pe.transpose(pt_bank[:, c:c + P], sbuf_p[:, (n % 2) * 512 + c:(n % 2) * 512 + c + P], ident)
            ins.then_inc(sem("pt_full"), 1)

        def values(n):
            _, _, v, w, _ = head_parts(n)
            pe.wait_ge(sem("pt_copied"), n + 1)
            if n >= 2:
                pe.wait_ge(sem("o_read"), n if heads[n][0] == "fox" else n - 1)
            bl = blocks_of(n)
            for qt in range(QT):
                mine = [(kt, c) for q, kt, c in bl if q == qt]
                for m, (kt, c) in enumerate(mine):
                    o = qt * P
                    ins = pe.matmul(o_bank(n)[:, o:o + w], sbuf_pt[:, (n % 2) * 512 + c:(n % 2) * 512 + c + P],
                                    v[:, kt, :], start=(m == 0), stop=(m == len(mine) - 1))
            ins.then_inc(sem("o_full"), 1)

        stage = ()

        def attention(which, between=()):
            nonlocal stage
            stage = STAGES[which]
            if which != "fox":
                pe.wait_ge(bank_free[3], min(before for name, u in uses.items() for b, before in u
                                             if b == 3 and number[name] >= number[AFTER_STAGE[which]]))
            for n in range(stage[0], stage[-1] + 3):
                if n in stage:
                    scores(n)
                if n - stage[0] < len(between):
                    tm_unit(between[n - stage[0]], fm)
                if n - 1 in stage:
                    turn(n - 1)
                if n - 2 in stage:
                    values(n - 2)

        def ffn(tag):
            for j in range(FT):
                fm_unit(f"{tag}_in{j}", fm)
            pe.wait_ge(sem("hidden_lo"), hid_base[tag] + FT)
            for j in range(FT // 2):
                row_unit(f"{tag}_out", j, FT // 2, hT)

        def wkv():
            pe.wait_ge(sem("wkv_ready"), 1)
            for pr in range(2):
                tok = slice(pr * P, (pr + 1) * P)
                for w, src in enumerate((b_fm, k_fm, v_fm)):
                    for h in range(2):
                        name = f"tr{pr}_{w}_{h}"
                        begin(name)
                        for a in range(3):
                            ins = pe.transpose(bank_of(name)[:, a * P:(a + 1) * P], src[:, 3 * h + a, tok], ident)
                        ins.then_inc(unit_done, 1)
                for u in range(H):
                    p, i = divmod(u, NT)
                    r = slice(p * DH, (p + 1) * DH)
                    name = f"sc{pr}_{u}"
                    begin(name)
                    both = ar[r, i, pr, :, :].rearrange("p b t -> p (b t)")
                    pe.matmul(bank_of(name)[:, 0:S], b_fm[r, i, tok], both, start=True, stop=True)
                    pe.matmul(bank_of(name)[:, S:2 * S], k_fm[r, i, tok], both, start=True, stop=True).then_inc(unit_done, 1)
                pe.wait_ge(*evacuated(f"tr{pr}_2_1"))
                for p in range(2):
                    begin(f"y0{pr}_{p}")
                    pe.wait_ge(*evacuated(f"sc{pr}_{p * NT + NT - 1}"))
                    for i in range(NT):
                        ins = pe.matmul(bank_of(f"y0{pr}_{p}")[:, i * DH:(i + 1) * DH], sc[:, p * NT + i, 2, :],
                                        kbv_tm[:, 2, (2 * i + p) * DH:(2 * i + p + 1) * DH], start=True, stop=True)
                    ins.then_inc(unit_done, 1)
                for gi in range(3):
                    begin(f"ti{pr}_{gi}")
                    pe.wait_ge(sem("tt_init"), 3 * pr + gi + 1)
                    for a in range(4):
                        ins = pe.transpose(bank_of(f"ti{pr}_{gi}")[:, a * P:(a + 1) * P], tt[:, 4 * gi + a, :], ident)
                    ins.then_inc(unit_done, 1)
                for li, s in enumerate(MERGES):
                    for gi in range(3):
                        name = f"e{pr}_{s}_{gi}"
                        begin(name)
                        pe.wait_ge(sem("merge_part"), 15 * pr + 3 * li + gi + 1)
                        if li:
                            for b in range(2):
                                pe.wait_ge(*evacuated(f"t{pr}_{MERGES[li - 1]}_{gi}", b))
                        else:
                            pe.wait_ge(*evacuated(f"ti{pr}_{gi}"))
                        for a in range(4):
                            ins = pe.matmul(bank_of(name)[:, a * P:(a + 1) * P], cms[gi][:, a, :], tms[gi][:, a, :],
                                            start=True, stop=True)
                        ins.then_inc(unit_done, 1)
                    for gi in range(3):
                        name = f"t{pr}_{s}_{gi}"
                        begin(name)
                        pe.wait_ge(*evacuated(f"e{pr}_{s}_{gi}"))
                        for a in range(4):
                            ins = pe.matmul(bank_of(name, 0)[:, a * P:(a + 1) * P], ems[gi][:, a, :],
                                            tt[:, 4 * gi + a, :], start=True, stop=True)
                        if s < 32:
                            for a in range(4):
                                ins = pe.matmul(bank_of(name, 1)[:, a * P:(a + 1) * P], tt[:, 4 * gi + a, :],
                                                ems[gi][:, a, :], start=True, stop=True)
                        ins.then_inc(unit_done, 1)
                for gi in range(3):
                    pe.wait_ge(*evacuated(f"t{pr}_32_{gi}"))
                pe.wait_ge(*evacuated(f"tr{pr}_0_1")), pe.wait_ge(*evacuated(f"tr{pr}_1_1"))
                for q in range(2):
                    c = 2 * pr + q
                    rq = slice(q * CH, (q + 1) * CH)
                    if c:
                        begin(f"z{c}c")
                        if c == 1:
                            pe.wait_ge(*evacuated("h0c"))
                        else:
                            pe.wait_ge(sem("state_ready"), c - 1)
                        for p in range(2):
                            r = slice(p * DH, (p + 1) * DH)
                            for i in range(NT):
                                ins = pe.matmul(bank_of(f"z{c}c", p)[rq, i * DH:(i + 1) * DH],
                                                ar[r, i, pr, 0, q * CH:(q + 1) * CH], state[r, c % 2, i, :],
                                                start=True, stop=True)
                        ins.then_inc(unit_done, 1)
                    begin(f"u{c}c")
                    for p in range(2):
                        pe.wait_ge(*evacuated(f"z{c}c" if c else "y00_" + str(p), p if c else 0))
                    for p in range(2):
                        for i in range(NT):
                            u = p * NT + i
                            ins = pe.matmul(bank_of(f"u{c}c", p)[rq, i * DH:(i + 1) * DH],
                                            tt[rq, u, q * CH:(q + 1) * CH], y0[rq, u * DH:(u + 1) * DH],
                                            start=True, stop=True)
                    ins.then_inc(unit_done, 1)
                    if c < 3:
                        begin(f"h{c}c")
                        for p in range(2):
                            pe.wait_ge(*evacuated(f"u{c}c", p))
                        for p in range(2):
                            r = slice(p * DH, (p + 1) * DH)
                            for i in range(NT):
                                hc = slice((2 * i + p) * DH, (2 * i + p + 1) * DH)
                                o = bank_of(f"h{c}c")[r, i * DH:(i + 1) * DH]
                                pe.matmul(o, kbv_tm[rq, 0, hc], u_tm[rq, (p * NT + i) * DH:(p * NT + i + 1) * DH],
                                          start=True, stop=False)
                                ins = pe.matmul(o, kbv_tm[rq, 1, hc], kbv_tm[rq, 2, hc], start=False, stop=True)
                        ins.then_inc(unit_done, 1)
                    if c:
                        begin(f"oi{c}c")
                        for p in range(2):
                            r = slice(p * DH, (p + 1) * DH)
                            for i in range(NT):
                                ins = pe.matmul(bank_of(f"oi{c}c", p)[r, i * DH:(i + 1) * DH], state[r, c % 2, i, :],
                                                ar[r, i, pr, 1, q * CH:(q + 1) * CH], start=True, stop=True)
                        ins.then_inc(unit_done, 1)
                begin(f"oo{pr}")
                for p in range(2):
                    pe.wait_ge(*evacuated(f"u{2 * pr + 1}c", p))
                for i in range(NT):
                    for p in range(2):
                        r = slice(p * DH, (p + 1) * DH)
                        u = p * NT + i
                        o = bank_of(f"oo{pr}", i // 3)[r, (i % 3) * P:(i % 3 + 1) * P]
                        pe.matmul(o, u_tm[:, u * DH:(u + 1) * DH], sc[:, u, 1, :], start=True, stop=False)
                        ins = pe.matmul(o, kbv_tm[:, 2, (2 * i + p) * DH:(2 * i + p + 1) * DH], sc[:, u, 3, :],
                                        start=False, stop=True)
                ins.then_inc(unit_done, 1)

        pe.wait_ge(sem("cst_in"), 16)
        pe.wait_ge(sem("vec_in"), VEC_DMAS * 16)
        pe.transpose(bank[0][:, 0:P], vec_rows, ident).then_inc(sem("table_full"), 1)
        pe.wait_ge(sem("pos_in"), 48)
        pe.transpose(bank[1][:, 0:72], pos_rows[0:72, :], ident[0:72, 0:72]).then_inc(sem("table_full"), 1)
        to_fm("tm_ready", 1)
        fm_ready()
        for name in ("kc", "vc", "q0", "q1", "q2", "ks"):
            fm_unit(name, fm)
        tm_unit("vs", fm), fm_unit("kw", fm), tm_unit("vw", fm), tm_unit("gl", fm), fm_unit("qm0", fm)
        to_fm("tm_ready", 2)
        fm_ready()
        fm_unit("kmem0", fm)
        for v in range(2):
            pe.wait_ge(sem("blocks_ready"), v + 1)
            for half in range(2):
                name = f"hid{v}_{half}"
                begin(name)
                w = slot(name).rearrange("p (l e) -> p l e", l=16)
                for l in range(16):
                    for p in range(2):
                        r = slice(p * DH, (p + 1) * DH)
                        ins = pe.matmul(bank_of(f"hid{v}_0", p)[:, 0:2 * NCMP], w[r, l, :],
                                        blocks[r, v, half * 16 + l, :],
                                        start=(half == 0 and l == 0), stop=(half == 1 and l == 15))
                ins.then_inc(unit_done, 1)
        tm_unit("vmem0", fm)
        pe.wait_ge(sem("small_in"), 16 * SMALL_DMAS)
        begin("kcb")
        for p in range(2):
            pe.wait_ge(*evacuated("hid0_0", p))
        for p in range(2):
            ins = pe.matmul(bank_of("kcb")[p * DH:(p + 1) * DH, 0:2 * NCMP], cmp_w2[:, 0:DH],
                            hid[:, 0, p * 30:(p + 1) * 30], start=True, stop=True)
        ins.then_inc(unit_done, 1)
        begin("vcb")
        for p in range(2):
            pe.wait_ge(*evacuated("hid1_0", p))
        for g in range(G):
            o = (g % 2) * 30 + (g // 2) * NCMP
            ins = pe.matmul(bank_of("vcb")[0:NCMP, g * DH:(g + 1) * DH], hid[:, 1, o:o + NCMP],
                            cmp_w2[:, DH:2 * DH], start=True, stop=True)
        ins.then_inc(unit_done, 1)
        fm_unit("kmem1", mem1_fm)
        pe.wait_ge(*evacuated("kcb"))
        pe.wait_ge(*evacuated("q2"))
        for p in range(2):
            begin(f"cs{p}")
            r = slice(p * DH, (p + 1) * DH)
            for qt in range(QT):
                for i in range(NT):
                    c = (qt * NT + i) * 16
                    ins = pe.matmul(bank_of(f"cs{p}")[:, c:c + NCMP], qT[r, i, qt * P:(qt + 1) * P],
                                    kcb[r, (i // R) * NCMP:(i // R + 1) * NCMP], start=True, stop=True)
            ins.then_inc(unit_done, 1)
        tm_unit("vmem1", mem1_fm)
        pe.wait_ge(sem("pcmp_ready"), 1)
        for j in range(8):
            begin(f"pct{j}")
            p, qt, hf = j // 4, (j // 2) % 2, j % 2
            for a in range(3):
                ins = pe.transpose(bank_of(f"pct{j}")[0:NCMP, a * P:(a + 1) * P],
                                   s_cmp[:, p, qt, hf * 3 + a, 0:NCMP], ident)
            ins.then_inc(unit_done, 1)
        pe.wait_ge(*evacuated("vcb"))
        for j in range(4):
            p, qt = j // 2, j % 2
            begin(f"oc{j}")
            pe.wait_ge(*evacuated(f"pct{2 * j}"))
            pe.wait_ge(*evacuated(f"pct{2 * j + 1}"))
            for i in range(NT):
                g = 2 * (i // R) + p
                ins = pe.matmul(bank_of(f"oc{j}")[:, i * DH:(i + 1) * DH],
                                p_cmpT[0:NCMP, 2 * j + i // 3, (i % 3) * P:(i % 3 + 1) * P],
                                vcb[0:NCMP, g * DH:(g + 1) * DH], start=True, stop=True)
            ins.then_inc(unit_done, 1)
        for name in ("kmem0", "vmem0", "ks", "vs", "kw", "vw", "qm0"):
            pe.wait_ge(*evacuated(name))
        attention("mem0")
        to_fm("o_read", 28)
        fm_ready()
        for j in range(4):
            row_unit("wo0_", j, 4, fm)
        to_fm("tm_ready", 3)
        fm_ready()
        ffn("f0")

        to_fm("tm_ready", 4)
        fm_ready()
        for j in range(10):
            fm_unit(f"z{j}", fm)
        fm_unit("z10", fm)
        fm_unit("qm1", fm)
        pe.wait_ge(sem("lora_in"), 64)
        pe.wait_ge(sem("lora_ready"), 3)
        for n, r in (("w2", slice(0, DH)), ("a2", slice(DH, P))):
            for j in range(3):
                begin(f"{n}_{j}")
                for a in range(2):
                    i = 2 * j + a
                    ins = pe.matmul(bank_of(f"{n}_{j}")[:, a * S:(a + 1) * S], rw_wa2[r, i * P:(i + 1) * P],
                                    lora[r, 0, :], start=True, stop=True)
                ins.then_inc(unit_done, 1)
        for j in range(3):
            begin(f"g2_{j}")
            for a in range(2):
                i = 2 * j + a
                o = bank_of(f"g2_{j}")[:, a * S:(a + 1) * S]
                pe.matmul(o, rw_g2[:, i * P:(i + 1) * P], lora[:, 1, :], start=True, stop=False)
                ins = pe.matmul(o, rw_g2[0:32, MW + i * P:MW + (i + 1) * P], lora[0:32, 2, :], start=False, stop=True)
            ins.then_inc(unit_done, 1)
        for n, src in (("kn", kk_sq), ("bs", bonus)):
            pe.wait_ge(sem("sumsrc_ready"), 1 if n == "kn" else 2)
            for j in range(3):
                begin(f"{n}_{j}")
                ins = pe.matmul(bank_of(f"{n}_{j}")[:, :], C("head_ones"),
                                src[:, 2 * j:2 * j + 2, :].rearrange("p a t -> p (a t)"), start=True, stop=True)
                ins.then_inc(unit_done, 1)
        pe.wait_ge(*evacuated("qm1"))
        attention("mem1")
        begin("crT")
        pe.wait_ge(sem("o_read"), 32)
        for a in range(2):
            for qt in range(QT):
                ins = pe.transpose(bank_of("crT")[:, a * S + qt * P:a * S + (qt + 1) * P],
                                   cross[:, qt, a * P:(a + 1) * P], ident)
        ins.then_inc(unit_done, 1)
        wkv()
        for n in ("gm", "gv"):
            if n == "gm":
                for a in range(2):
                    pe.wait_ge(*evacuated("oo1", a))
            else:
                pe.wait_ge(sem("squares_ready"), 1)
            for j in range(3):
                src = y_fm if n == "gm" else zt
                begin(f"{n}_{j}")
                pe.matmul(bank_of(f"{n}_{j}")[:, :], C("head_ones"),
                              src[:, 2 * j:2 * j + 2, :].rearrange("p a t -> p (a t)"), start=True, stop=True).then_inc(unit_done, 1)
        pe.wait_ge(*evacuated("crT"))
        pe.wait_ge(sem("mix1_lo"), 1)
        for j in range(4):
            row_unit("wo1_", j, 4, fm)
        to_fm("tm_ready", 5)
        fm_ready()
        ffn("f1")

        for j in range(2):
            begin(f"wsT{j}")
            pe.wait_ge(sem("ws_in"), 16)
            for a in range(4):
                ins = pe.transpose(bank_of(f"wsT{j}")[:, a * P:(a + 1) * P], ws_raw[:, 4 * j + a, :], ident)
            ins.then_inc(unit_done, 1)
        to_fm("tm_ready", 6)
        fm_ready()
        for name in ("sv", "su"):
            for j in range(4):
                tm_unit(f"{name}{j}", fm)
        tm_unit("sf", fm)
        for name in ("fq", "fk"):
            for j in range(4):
                fm_unit(f"{name}{j}", fm)
        for j in range(4):
            tm_unit(f"fv{j}", fm)
        begin("cc")
        pe.wait_ge(sem("logf_ready"), 1)
        o = bank_of("cc")
        pe.matmul(o[0:NFH, 0:P], logf[:, 0, :], C("tri"), start=True, stop=True)
        pe.matmul(o[0:NFH, P:S], logf[:, 0, :], C("ones"), start=True, stop=False)
        pe.matmul(o[0:NFH, P:S], logf[:, 1, :], C("tri"), start=False, stop=True).then_inc(unit_done, 1)
        pe.wait_ge(sem("vn_ready"), 1)
        for j in range(2):
            pe.wait_ge(*evacuated(f"wsT{j}"))
        for j in range(4):
            begin(f"sgu{j}")
            qt, half = j // 2, j % 2
            for a in range(4):
                g = 4 * half + a
                ins = pe.matmul(bank_of(f"sgu{j}")[:, a * P:(a + 1) * P], wsT[:, g, :],
                                v_n[:, qt, g * P:(g + 1) * P], start=True, stop=True)
            ins.then_inc(unit_done, 1)
        pe.wait_ge(*evacuated("cc"))
        for j in range(4):
            for name in ("fq", "fk", "fv"):
                pe.wait_ge(*evacuated(f"{name}{j}"))
        attention("fox", GATE_UNITS)
        to_fm("tm_ready", 7)
        fm_ready()
        for j in range(4):
            row_unit("wo2_", j, 4, fm)
        to_fm("tm_ready", 8)
        fm_ready()
        ffn("f2")

    @block.scalar
    def _(act):
        own = counter("act_step")
        tiles2 = lambda a: a.rearrange("p i t -> p (i t)")
        copy = ACT.Identity

        act.dma_start(cst[:, :], cst_d).then_inc(sem("cst_in"), 16)
        act.wait_ge(sem("vec_zero"), 1)
        for name, (o, k) in VEC.items():
            src = T[name]
            if name == "rw_mu":
                src = src[0:1, 0:k * P].rearrange("a (k c) -> (a k) c", c=P)
            elif name == "rw_r_k":
                src = src.rearrange("a (i h) d -> (a i) (h d)", h=2)
            else:
                src = src.rearrange("a (k c) -> (a k) c", c=P)
            act.dma_start(vec_rows[o:o + k, :], src).then_inc(sem("vec_in"), 16)
        act.dma_start(vec_rows[MU_LAST:MU_LAST + 1, 0:MU_TAIL], T["rw_mu"][0:1, 20 * P:]).then_inc(sem("vec_in"), 16)
        for p in range(2):
            act.dma_start(pos_rows[0:2 * CMP_BLOCK, p * DH:(p + 1) * DH],
                          T["nsa_cmp_pos"][0].rearrange("v l d -> (v l) d")).then_inc(sem("pos_in"), 16)
        act.dma_start(pos_rows[64:72, :], T["b_spatial_2"][0]).then_inc(sem("pos_in"), 16)
        smalls = [
            (cmp_w2[:, 0:DH], T["nsa_cmp_w2"][0, 0]), (cmp_w2[:, DH:2 * DH], T["nsa_cmp_w2"][0, 1]),
            (gate_b, T["nsa_gate_b"].to_broadcast((P, 3 * H))),
            (b_forget, T["b_forget_2"].to_broadcast((P, NFH)))]
        for dst, src in smalls:
            act.dma_start(dst, src).then_inc(sem("small_in"), 16)

        def squares(r, src):
            if last(own):
                act.wait_ge(*last(own))
            act.activation(sbuf_p, src[:, 0, :], ACT.Square, accum_out=ssq[:, r, 0:1]).then_inc(tick(own, "sq_act"), 1)

        def root(r):
            act.wait_ge(sem("ms_ready"), r + 1)
            act.activation(rms[:, r, :], ssq[:, r, :], ACT.Sqrt).then_inc(tick(own, "rt_ready"), 1)

        fm_event = [0]

        def from_banks(outs):
            e = fm_event[0]
            fm_event[0] += 1
            for j in range(4):
                act.wait_ge(sem("fm_full"), 4 * e + j + 1)
                for k in (2 * j, 2 * j + 1):
                    for dst, gain in outs:
                        b = bank[4 + j][:, (k % 2) * S:(k % 2 + 1) * S]
                        if gain is None:
                            ins = act.activation(dst[0][:, k, :], b, copy)
                        else:
                            ins = act.activation(dst[0][:, k, :], b, copy, scale=V(*gain(k)))
                ins.then_inc(tick(own, "fm_hi"), 1)

        split_at = [0]

        def ahead(name):
            split_to(split_end(name))

        def split_to(end):
            while split_at[0] < end:
                m = split_at[0]
                split_at[0] += 1
                new = split_names[m]
                r, v = landed[new]
                act.wait_ge(slot_landed[r], v)
                if m >= SPLITS:
                    act.wait_ge(*filled(split_names[m - SPLITS]))
                for lo, hi in pieces(new):
                    act.activation(w_hi[:, (m % SPLITS) * SLOT + lo:(m % SPLITS) * SLOT + hi],
                                   ring[:, r * SLOT + lo:r * SLOT + hi], copy).then_inc(tick(own, "hi_ready"), 1)

        def evac(name, dst, func=copy, scale=1.0, src=None):
            act.wait_ge(*filled(name))
            act.activation(dst, bank_of(name)[:, :] if src is None else src, func, scale=scale).then_inc(freed(own, name), 1)

        def two(name):
            return bank_of(name)[:, :].rearrange("p (q c) -> p q c", q=2)

        def exps(n):
            kind, _ = heads[n]
            act.wait_ge(sem("nmax_ready"), n + 1)
            if n >= 2:
                act.wait_ge(sem("pt_full"), n - 1)
            for qt, c, nk in head_parts(n)[4]:
                src = score_bank(n) if kind in ("mem0", "mem1") else sbuf_s[:, (n % 2) * 512:]
                o = (n % 2) * 512 + c
                ins = act.activation(sbuf_p[:, o:o + nk], src[:, c:c + nk], ACT.Exp, bias=nmax[:, n, qt:qt + 1],
                                     accum_out=rsum[:, n, qt:qt + 1])
            ins.then_inc(tick(own, "exp_done"), 1)

        def copy_pt(n):
            act.wait_ge(sem("pt_full"), n + 1)
            if n >= 2:
                act.wait_ge(sem("o_full"), n - 1)
            w = P * len(blocks_of(n))
            act.activation(sbuf_pt[:, (n % 2) * 512:(n % 2) * 512 + w], pt_bank[:, 0:w], copy).then_inc(tick(own, "pt_copied"), 1)

        def attention(which, between=None):
            st = STAGES[which]
            for n in range(st[0], st[-1] + 2):
                if n in st:
                    exps(n)
                if n - 1 in st:
                    copy_pt(n - 1)
                if between and n in st:
                    between(n - st[0])

        def high_hidden(tag, j):
            act.wait_ge(*evacuated(f"{tag}_in{j}"))
            act.activation(hT[0][:, j, :], hidden[:, j % 2, :], copy).then_inc(tick(own, "hidden_hi"), 1)

        def linear(names, outs):
            for name in names:
                ahead(name)
                if name in outs:
                    evac(name, *outs[name])

        def rows_ahead(tag):
            for j in range(4):
                ahead(f"{tag}_{j}")

        def ffn(tag, base):
            for j in range(FT):
                ahead(f"{tag}_in{j}")
                act.wait_ge(*filled(f"{tag}_in{j}"))
                if j >= 2:
                    act.wait_ge(*evacuated(f"{tag}_in{j - 2}"))
                act.activation(silu[:, j % 2, :], bank_of(f"{tag}_in{j}")[:, 0:S], ACT.Silu).then_inc(tick(own, "silu_ready"), 1)
                if j:
                    high_hidden(tag, j - 1)
            high_hidden(tag, FT - 1)
            for j in range(FT // 2):
                ahead(f"{tag}_out{j}")

        act.wait_ge(sem("x_in"), 16)
        squares(0, x_tm)
        root(0)
        act.wait_ge(sem("mem_in"), 16)
        act.wait_ge(*last(own))
        squares(1, mem_tm)
        root(1)
        act.wait_ge(sem("tables"), 2)
        from_banks([(fm, lambda k: ("norm1", k))])
        flat_q = lambda j: tiles2(qT[:, 2 * j:2 * j + 2, :])
        linear(("kc", "vc", "q0", "q1", "q2", "ks", "vs", "kw", "vw", "gl"),
               {"q0": (flat_q(0), copy, DH ** -0.5), "q1": (flat_q(1), copy, DH ** -0.5),
                "q2": (flat_q(2), copy, DH ** -0.5), "ks": (tiles2(kselT),), "kw": (tiles2(kwinT),)})
        act.wait_ge(*evacuated("gl"))
        act.activation(gates, gates, ACT.Sigmoid).then_inc(tick(own, "gates_ready"), 1)
        linear(("qm0",), {"qm0": (qmem, copy, DH ** -0.5)})
        from_banks([(fm, lambda k: ("norm_mem", k)), (mem1_fm, lambda k: ("norm_mem", 8 + k))])
        linear(("kmem0",), {"kmem0": (kmem0,)})
        for v in range(2):
            act.wait_ge(*filled(f"hid{v}_1"))
            for p in range(2):
                act.activation(hid[:, v, p * 30:(p + 1) * 30], bank_of(f"hid{v}_0", p)[:, 0:30],
                               ACT.Gelu_apprx_tanh).then_inc(freed(own, f"hid{v}_0", p), 1)
            if v == 0:
                split_to(split_no["vmem0"] + 1)
        linear(("vmem0", "kmem1"), {"kmem1": (kmem1,)})
        act.wait_ge(sem("scmp_ready"), 1)
        sall = s_cmp.rearrange("p h q i n -> p (h q i) n")[:, :, 0:NCMP]
        act.activation(sall, sall, ACT.Exp).then_inc(tick(own, "ecmp_ready"), 1)
        ahead("vmem1")
        for j in range(8):
            evac(f"pct{j}", p_cmpT[0:NCMP, j, :], src=bank_of(f"pct{j}")[0:NCMP, 0:384])
        attention("mem0")
        from_banks([(fm, None)])
        rows_ahead("wo0")
        act.wait_ge(*evacuated("wo0_0", 1))
        squares(2, x_tm)
        root(2)
        from_banks([(fm, lambda k: ("norm2", k))])
        ffn("f0", 0)
        act.wait_ge(*evacuated("f0_out0", 1))
        squares(3, x_tm)
        root(3)

        from_banks([(fm, lambda k: ("norm1", 8 + k))])
        zs = zshift[:, :].rearrange("p (b a t) -> p b a t", b=2, a=2)
        act.wait_ge(sem("zcol_ready"), 1)
        for j in range(11):
            ahead(f"z{j}")
            if j >= 2:
                act.wait_ge(sem("zmix_ready"), j - 1)
            if j < 10:
                evac(f"z{j}", zs[:, j % 2, :, 1:S + 1], src=two(f"z{j}"))
            else:
                evac("z10", zs[0:32, 0, 0, 1:S + 1], src=bank_of("z10")[0:32, 0:S])
        evac("qm1", qmem, scale=DH ** -0.5)
        act.wait_ge(sem("zmix_ready"), 11)
        act.activation(lora[0:DH, 0, :], lora[0:DH, 0, :], ACT.Tanh).then_inc(tick(own, "lora_ready"), 1)
        act.activation(lora[:, 1, :], lora[:, 1, :], ACT.Sigmoid).then_inc(tick(own, "lora_ready"), 1)
        act.activation(lora[0:32, 2, :], lora[0:32, 2, :], ACT.Sigmoid).then_inc(tick(own, "lora_ready"), 1)
        for n, dst, b0 in (("w2", sg, "rw_w0"), ("a2", iclr, "rw_a0")):
            for j in range(3):
                act.wait_ge(*filled(f"{n}_{j}"))
                act.activation(dst[:, 2 * j, :], bank_of(f"{n}_{j}")[:, 0:S], ACT.Sigmoid, bias=V(b0, 2 * j))
                act.activation(dst[:, 2 * j + 1, :], bank_of(f"{n}_{j}")[:, S:2 * S], ACT.Sigmoid,
                                        bias=V(b0, 2 * j + 1)).then_inc(freed(own, f"{n}_{j}"), 1)
        for j in range(3):
            evac(f"kn_{j}", k_fm[:, 2 * j:2 * j + 2, :].rearrange("p a t -> p (a t)"), ACT.Sqrt)
        act.wait_ge(sem("csum_ready"), 1)
        flat = lambda a: a.rearrange("p i t -> p (i t)")
        act.activation(flat(e_in), flat(csum), ACT.Exp, scale=-C0).then_inc(tick(own, "exps_ready"), 1)
        act.activation(flat(e_neg), flat(csum), ACT.Exp, scale=C0).then_inc(tick(own, "exps_ready"), 1)
        act.wait_ge(sem("cexc_ready"), 1)
        act.activation(flat(sg), flat(sg), ACT.Exp, scale=-C0).then_inc(tick(own, "exps_ready"), 1)
        attention("mem1")
        act.wait_ge(*filled("crT"))
        act.activation(fm[0][:, 6:8, :], two("crT"), copy).then_inc(tick(own, "cross_hi"), 1)
        for pr in range(2):
            for w in range(3):
                evac(f"tr{pr}_{w}_1", kbv_tm[:, w, 384:768], src=bank_of(f"tr{pr}_{w}_1")[:, 0:384])
            for gi in range(3):
                evac(f"ti{pr}_{gi}", tms[gi].rearrange("p u t -> p (u t)"))
            for s in MERGES:
                for gi in range(3):
                    evac(f"e{pr}_{s}_{gi}", ems[gi].rearrange("p u t -> p (u t)"))
            for q in range(2):
                c = 2 * pr + q
                rq = slice(q * CH, (q + 1) * CH)
                act.wait_ge(*filled(f"u{c}c"))
                for p in range(2):
                    act.activation(u_tm[rq, p * 384:(p + 1) * 384], bank_of(f"u{c}c", p)[rq, 0:384], copy).then_inc(freed(own, f"u{c}c", p), 1)
                if c:
                    act.wait_ge(*filled(f"oi{c}c"))
                    act.wait_ge(sem("yzero_ready"), 1)
                    for p in range(2):
                        r = slice(p * DH, (p + 1) * DH)
                        act.activation(
                            y_fm[r, :, c * CH:(c + 1) * CH],
                            bank_of(f"oi{c}c", p)[r, 0:384].rearrange("p (i t) -> p i t", i=NT), copy).then_inc(freed(own, f"oi{c}c", p), 1)
        for j in range(3):
            act.wait_ge(*evacuated(f"gv_{j}"))
        act.activation(flat(zt), flat(zt), ACT.Sqrt).then_inc(tick(own, "gstd_ready"), 1)
        act.wait_ge(sem("mix1_ready"), 1)
        ahead("qm1")
        act.activation(fm[0][:, 0:NT, :], mix_fm, copy).then_inc(tick(own, "mix1_hi"), 1)
        rows_ahead("wo1")
        act.wait_ge(*evacuated("wo1_0", 1))
        squares(4, x_tm)
        root(4)
        from_banks([(fm, lambda k: ("norm2", 8 + k))])
        ffn("f1", FT)
        act.wait_ge(*evacuated("f1_out0", 1))
        squares(5, x_tm)
        root(5)

        act.wait_ge(sem("x2_ready"), 1)
        squares(6, x_tm)
        root(6)
        from_banks([(fm, lambda k: ("mix_pre_g_2", k))])
        part = lambda dst, j: dst[:, :, j * 256:(j + 1) * 256]
        for name, dst in (("sv", v_n), ("su", u_g)):
            for j in range(4):
                linear((f"{name}{j}",), {f"{name}{j}": (part(dst, j), ACT.Gelu_apprx_tanh, 1.0, two(f"{name}{j}"))})
                if name == "su" and j == 0:
                    act.wait_ge(sem("lnvar_ready"), 1)
                    act.activation(mv[:, 4:6], mv[:, 4:6], ACT.Sqrt).then_inc(tick(own, "lnstd_ready"), 1)
        ahead("sf")
        act.wait_ge(sem("fabs_ready"), 1)
        act.activation(tmpf[:, 1], tmpf[:, 1], ACT.Exp, scale=-1.0).then_inc(tick(own), 1)
        act.wait_ge(*last(own))
        act.activation(tmpf[:, 1], tmpf[:, 1], ACT.Ln, bias=1.0).then_inc(tick(own, "fln_ready"), 1)
        for j in range(4):
            linear((f"fq{j}",), {f"fq{j}": (tiles2(q2[:, 2 * j:2 * j + 2, :]), copy, P ** -0.5)})
        for name in ("fk", "fv"):
            for j in range(4):
                ahead(f"{name}{j}")

        def gate(j):
            name = GATE_UNITS[j]
            dst = sga if name.startswith("ga") else sgb
            ahead(name)
            evac(name, part(dst, j % 4), ACT.Sigmoid, 1.0, two(name))

        attention("fox", gate)
        from_banks([(fm, None)])
        rows_ahead("wo2")
        act.wait_ge(*evacuated("wo2_0", 1))
        squares(7, u_g)
        root(7)
        act.wait_ge(sem("x3_ready"), 1)
        squares(8, x_tm)
        root(8)
        from_banks([(fm, lambda k: ("ffn_pre_g_2", k))])
        ffn("f2", 2 * FT)
        act.wait_ge(*evacuated("f2_out0", 1))
        squares(9, u_g)
        root(9)

    @block.vector
    def _(dve):
        own = counter("dve_step")
        flat = lambda a: a.rearrange("p i t -> p (i t)")

        def mean_square(r, src):
            dve.tensor_tensor_reduce(out=sbuf_s[:, :], in0=src[:, 1, :], in1=src[:, 1, :], scale=1.0, scalar=0.0,
                                              op0=ALU.mult, op1=ALU.add, accum_out=ssq[:, r, 1:2]).then_inc(tick(own), 1)
            dve.wait_ge(*last(own))
            dve.wait_ge(sem("sq_act"), r + 1)
            dve.tensor_scalar(ssq[:, r, :], ssq[:, r, :], 1.0 / D, EPS, ALU.mult, ALU.add).then_inc(tick(own, "ms_ready"), 1)

        def inverse(r):
            dve.wait_ge(sem("rt_ready"), r + 1)
            dve.reciprocal(rms[:, r, :], rms[:, r, :]).then_inc(tick(own), 1)
            dve.wait_ge(*last(own))

        def rms_norm(r, src, dst):
            mean_square(r, src)
            inverse(r)
            for qt in range(QT):
                ins = dve.tensor_scalar(dst[:, qt, :], src[:, qt, :], rms[:, r, qt:qt + 1], None, ALU.mult)
            ins.then_inc(tick(own, "tm_ready"), 1)

        def rms_gain(r, src, dst, gain):
            mean_square(r, src)
            inverse(r)
            for qt in range(QT):
                ins = dve.scalar_tensor_tensor(out=dst[:, qt, :], in0=src[:, qt, :], scalar=rms[:, r, qt:qt + 1],
                                               in1=gains[:, GAIN[gain], :], op0=ALU.mult, op1=ALU.mult)
            return ins

        fm_event = [0]

        def from_banks(outs):
            e = fm_event[0]
            fm_event[0] += 1
            for j in range(4):
                dve.wait_ge(sem("fm_hi"), 4 * e + j + 1)
                for k in (2 * j, 2 * j + 1):
                    for dst, gain in outs:
                        b = bank[4 + j][:, (k % 2) * S:(k % 2 + 1) * S]
                        hi = dst[0][:, k, :].bitcast(F32)
                        if gain is None:
                            ins = dve.tensor_tensor(dst[1][:, k, :], b, hi, ALU.subtract)
                        else:
                            ins = dve.scalar_tensor_tensor(out=dst[1][:, k, :], in0=b, scalar=V(*gain(k)), in1=hi,
                                                           op0=ALU.mult, op1=ALU.subtract)
                ins.then_inc(tick(own, "fm_lo"), 1)

        split_at = [0]

        def ahead(name):
            split_to(split_end(name))

        def split_to(end):
            while split_at[0] < end:
                m = split_at[0]
                split_at[0] += 1
                new = split_names[m]
                r, _ = landed[new]
                for i, (lo, hi) in enumerate(pieces(new)):
                    dve.wait_ge(sem("hi_ready"), PIECES * m + i + 1)
                    c = slice((m % SPLITS) * SLOT + lo, (m % SPLITS) * SLOT + hi)
                    dve.tensor_tensor(w_lo[:, c], ring[:, r * SLOT + lo:r * SLOT + hi], w_hi[:, c].bitcast(F32),
                                      ALU.subtract).then_inc(tick(own, "lo_ready"), 1)

        def linear(names, outs):
            for name in names:
                ahead(name)
                if name in outs:
                    evac(name, *outs[name])

        def rows_ahead(tag):
            for j in range(4):
                ahead(f"{tag}_{j}")

        def evac(name, dst, src=None):
            dve.wait_ge(*filled(name))
            dve.tensor_copy(dst, bank_of(name)[:, :] if src is None else src).then_inc(freed(own, name), 1)

        def two(name):
            return bank_of(name)[:, :].rearrange("p (q c) -> p q c", q=2)

        def residual(tag, final):
            dve.wait_ge(*filled(final))
            for i in range(4):
                o = x_tm[:, i // 2, (i % 2) * 512:(i % 2 + 1) * 512]
                dve.tensor_tensor(o, bank_of(tag, i)[:, :], o, ALU.add).then_inc(freed(own, tag, i), 1)
            dve.wait_ge(*last(own))

        def maxima(n):
            kind, i = heads[n]
            dve.wait_ge(sem("scores_full"), n + 1)
            if kind in ("mem0", "mem1"):
                ins = dve.tensor_reduce(nmax[:, n, :], score_bank(n)[:, :].rearrange("p (q k) -> p q k", q=2),
                                        AX.X, ALU.max, negate=True)
                ins.then_inc(tick(own, "nmax_ready"), 1)
                return
            if n >= 2:
                dve.wait_ge(sem("exp_done"), n - 1)
            table = C("causal") if kind == "fox" else alibi[:, i, :]
            for qt, c, nk in head_parts(n)[4]:
                o = (n % 2) * 512 + c
                dve.tensor_tensor_reduce(
                    out=sbuf_s[:, o:o + nk], in0=score_bank(n)[:, c:c + nk], in1=table[:, c:c + nk], scale=1.0,
                    scalar=-3e38, op0=ALU.add, op1=ALU.max, accum_out=nmax[:, n, qt:qt + 1]).then_inc(tick(own), 1)
            dve.wait_ge(*last(own))
            dve.tensor_scalar(nmax[:, n, :], nmax[:, n, :], -1.0, None, ALU.mult).then_inc(tick(own, "nmax_ready"), 1)

        def finish(n):
            kind, i = heads[n]
            dve.wait_ge(sem("o_full"), n + 1)
            dve.reciprocal(coef[:, n, :], rsum[:, n, :]).then_inc(tick(own), 1)
            dve.wait_ge(*last(own))
            if kind in ("sel", "win"):
                br = 1 if kind == "sel" else 2
                dve.tensor_tensor(coef[:, n, :], coef[:, n, :], gates[:, :, br * H + i], ALU.mult).then_inc(tick(own), 1)
                dve.wait_ge(*last(own))
            for qt in range(QT):
                o = qt * P
                if kind in ("sel", "win"):
                    dst = tm[:, qt, i * DH:(i + 1) * DH]
                    ins = dve.scalar_tensor_tensor(out=dst, in0=o_bank(n)[:, o:o + DH], scalar=coef[:, n, qt:qt + 1],
                                                   in1=dst, op0=ALU.mult, op1=ALU.add)
                else:
                    w = P if kind == "fox" else DH
                    dst = {"mem0": tm[:, :, MW:], "mem1": cross, "fox": tm}[kind][:, qt, i * w:(i + 1) * w]
                    ins = dve.tensor_scalar(dst, o_bank(n)[:, o:o + w], coef[:, n, qt:qt + 1], None, ALU.mult)
            ins.then_inc(tick(own, "o_read"), 1)

        def attention(which, between=None):
            st = STAGES[which]
            for n in range(st[0], st[-1] + 3):
                if n in st:
                    maxima(n)
                if between and n in st:
                    between(n - st[0])
                if n - 2 in st:
                    finish(n - 2)
            dve.wait_ge(*last(own))

        def low_hidden(j, base):
            dve.wait_ge(sem("hidden_hi"), base + j + 1)
            dve.tensor_tensor(hT[1][:, j, :], hidden[:, j % 2, :], hT[0][:, j, :].bitcast(F32),
                              ALU.subtract).then_inc(tick(own, "hidden_lo"), 1)

        def ffn(tag, base):
            for j in range(FT):
                ahead(f"{tag}_in{j}")
                dve.wait_ge(sem("silu_ready"), base + j + 1)
                if last(own):
                    dve.wait_ge(*last(own))
                dve.tensor_tensor(hidden[:, j % 2, :], bank_of(f"{tag}_in{j}")[:, S:2 * S], silu[:, j % 2, :],
                                  ALU.mult).then_inc(freed(own, f"{tag}_in{j}"), 1)
                if j:
                    low_hidden(j - 1, base)
            low_hidden(FT - 1, base)
            for j in range(FT // 2):
                ahead(f"{tag}_out{j}")

        dve.wait_ge(sem("table_full"), 1)
        dve.tensor_copy(vec[:, :], bank[0][:, 0:P]).then_inc(tick(own, "tables"), 1)
        dve.wait_ge(sem("table_full"), 2)
        dve.tensor_copy(posT, bank[1][:, 0:64])
        dve.tensor_copy(vecs2, bank[1][:, 64:72]).then_inc(tick(own, "tables"), 1)
        dve.wait_ge(*last(own))
        dve.wait_ge(sem("x_in"), 16)
        rms_norm(0, x_tm, tm)
        dve.wait_ge(sem("mem_in"), 16)
        rms_norm(1, mem_tm, mem_tm)
        from_banks([(fm, lambda k: ("norm1", k))])
        linear(("kc", "vc", "q0", "q1", "q2", "ks", "vs", "kw", "vw", "gl"),
               {"kc": (flat(kcvT[:, 0]),), "vc": (flat(kcvT[:, 1]),),
                "vs": (flat(vsel),), "vw": (flat(vwin),)})
        dve.wait_ge(*filled("gl"))
        dve.wait_ge(sem("small_in"), 16 * SMALL_DMAS)
        dve.tensor_tensor(gates, two("gl")[:, :, 0:3 * H], gate_b.unsqueeze(1).to_broadcast((P, QT, 3 * H)),
                          ALU.add).then_inc(freed(own, "gl"), 1)
        ahead("qm0")
        from_banks([(fm, lambda k: ("norm_mem", k)), (mem1_fm, lambda k: ("norm_mem", 8 + k))])
        ahead("kmem0")
        split_to(split_no["vmem0"] + 1)
        linear(("vmem0",), {"vmem0": (vmem0,)})
        evac("kcb", kcb, bank_of("kcb")[:, 0:30])
        evac("vcb", vcb[0:NCMP, :], bank_of("vcb")[0:NCMP, 0:256])
        ahead("kmem1")
        sv = s_cmp.rearrange("p h q i n -> p (h q i) n")
        bias = C("cmp_bias").rearrange("p (u n) -> p u n", n=16)
        for p in range(2):
            dve.wait_ge(*filled(f"cs{p}"))
            dve.tensor_tensor(
                sv[:, p * 12:(p + 1) * 12, 0:NCMP],
                bank_of(f"cs{p}")[:, 0:192].rearrange("p (u n) -> p u n", n=16)[:, :, 0:NCMP],
                bias[:, p * 12:(p + 1) * 12, 0:NCMP], ALU.add).then_inc(freed(own, f"cs{p}"), 1)
        dve.wait_ge(*last(own))
        dve.tensor_reduce(m_cmp, sv[:, :, 0:NCMP], AX.X, ALU.max).then_inc(tick(own), 1)
        dve.wait_ge(*last(own))
        dve.tensor_tensor(sv[:, :, 0:NCMP], sv[:, :, 0:NCMP],
                                     m_cmp.unsqueeze(2).to_broadcast((P, 24, NCMP)), ALU.subtract).then_inc(tick(own, "scmp_ready"), 1)
        linear(("vmem1",), {"vmem1": (vmem1,)})
        dve.wait_ge(sem("ecmp_ready"), 1)
        dve.tensor_reduce(c_cmp, sv[:, :, 0:NCMP], AX.X, ALU.add).then_inc(tick(own), 1)
        dve.wait_ge(*last(own))
        mask = C("cmp_mask").rearrange("p (q n) -> p q n", q=QT)
        for p in range(2):
            for qt in range(QT):
                v = s_cmp[:, p, qt, :, 0:NCMP]
                ins = dve.tensor_tensor(v, v, mask[:, qt, 0:NCMP].unsqueeze(1).to_broadcast((P, NT, NCMP)), ALU.mult)
        ins.then_inc(tick(own, "pcmp_ready"), 1)
        dve.reciprocal(c_cmp, c_cmp).then_inc(tick(own), 1)
        dve.wait_ge(*last(own))
        dve.wait_ge(sem("gates_ready"), 1)
        cc4 = c_cmp.rearrange("p (h q g r) -> p h q g r", h=2, q=QT, g=2)
        gc = gates[:, :, 0:H].rearrange("p q (g h r) -> p h q g r", g=2, h=2)
        for p in range(2):
            dve.tensor_tensor(cc4[:, p], cc4[:, p], gc[:, p], ALU.mult).then_inc(tick(own), 1)
        dve.wait_ge(*last(own))
        for j in range(4):
            p, qt = divmod(j, 2)
            dve.wait_ge(*filled(f"oc{j}"))
            for gp in range(2):
                base = (2 * gp + p) * R * DH
                ins = dve.tensor_tensor(
                    tm[:, qt, base:base + R * DH].rearrange("p (r d) -> p r d", r=R),
                    bank_of(f"oc{j}")[:, gp * R * DH:(gp + 1) * R * DH].rearrange("p (r d) -> p r d", r=R),
                    cc4[:, p, qt, gp].unsqueeze(2).to_broadcast((P, R, DH)), ALU.mult)
            ins.then_inc(freed(own, f"oc{j}"), 1)
        dve.wait_ge(*last(own))
        dve.wait_ge(sem("alibi_ready"), 1)
        attention("mem0")
        from_banks([(fm, None)])
        rows_ahead("wo0")
        residual("wo0_0", "wo0_3")
        rms_norm(2, x_tm, tm)
        from_banks([(fm, lambda k: ("norm2", k))])
        ffn("f0", 0)
        residual("f0_out0", f"f0_out{FT // 2 - 1}")
        rms_norm(3, x_tm, tm)

        zs = zshift[:, :].rearrange("p (b a t) -> p b a t", b=2, a=2)
        dve.memset(zs[:, :, :, 0:1], 0.0).then_inc(tick(own, "zcol_ready"), 1)
        dve.wait_ge(*last(own))
        from_banks([(fm, lambda k: ("norm1", 8 + k))])
        zd = zdelta[:, :].rearrange("p (a t) -> p a t", a=2)
        dsts = [r_fm[:, i, :] for i in range(NT)] + [kraw[:, i, :] for i in range(NT)] + \
               [v_fm[:, i, :] for i in range(NT)] + [lora[:, i, :] for i in range(3)]
        for j in range(11):
            ahead(f"z{j}")
            dve.wait_ge(*evacuated(f"z{j}"))
            z = zs[:, j % 2]
            rows = slice(0, P) if j < 10 else slice(0, 32)
            n = 2 if j < 10 else 1
            dve.tensor_tensor(zd[rows, 0:n, :], z[rows, 0:n, 0:S], z[rows, 0:n, 1:S + 1], ALU.subtract).then_inc(tick(own), 1)
            dve.wait_ge(*last(own))
            for a in range(n):
                i = 2 * j + a
                mu = V("rw_mu", i) if j < 10 else vec[0:32, MU_LAST:MU_LAST + 1]
                ins = dve.scalar_tensor_tensor(out=dsts[i][rows], in0=zd[rows, a, :], scalar=mu,
                                               in1=z[rows, a, 1:S + 1], op0=ALU.mult, op1=ALU.add)
            ins.then_inc(tick(own, "zmix_ready"), 1)
            dve.wait_ge(*last(own))
        dve.wait_ge(*filled("qm1"))
        for i in range(NT):
            dve.tensor_scalar(kk[:, i, :], kraw[:, i, :], V("rw_k_k", i), None, ALU.mult).then_inc(tick(own), 1)
        dve.wait_ge(*last(own))
        dve.tensor_tensor(kk_sq, kk, kk, ALU.mult).then_inc(tick(own, "sumsrc_ready"), 1)
        for j in range(3):
            dve.wait_ge(*evacuated(f"w2_{j}"))
            for i in (2 * j, 2 * j + 1):
                ins = dve.tensor_tensor_scan(csum[:, i, :], C("chunk_keep"), sg[:, i, :], 0.0, ALU.mult, ALU.add)
        ins.then_inc(tick(own, "csum_ready"), 1)
        for j in range(3):
            evac(f"g2_{j}", g_fm[:, 2 * j:2 * j + 2, :].rearrange("p a t -> p (a t)"))
        for j in range(3):
            dve.wait_ge(*evacuated(f"kn_{j}"))
        dve.tensor_scalar(flat(k_fm), flat(k_fm), 1e-12, None, ALU.max).then_inc(tick(own), 1)
        dve.wait_ge(*last(own))
        dve.reciprocal(flat(k_fm), flat(k_fm)).then_inc(tick(own), 1)
        dve.wait_ge(*last(own))
        dve.scalar_tensor_tensor(out=flat(kk), in0=flat(kk), scalar=-1.0, in1=flat(k_fm),
                                          op0=ALU.mult, op1=ALU.mult).then_inc(tick(own), 1)
        dve.wait_ge(sem("exps_ready"), 3)
        for i in range(NT):
            dve.tensor_scalar(csum[:, i, :], iclr[:, i, :], 1.0, V("rw_k_a", i), ALU.subtract, ALU.mult).then_inc(tick(own), 1)
        dve.wait_ge(*last(own))
        dve.scalar_tensor_tensor(out=flat(kraw), in0=flat(csum), scalar=1.0, in1=flat(kraw),
                                          op0=ALU.add, op1=ALU.mult).then_inc(tick(own), 1)
        dve.wait_ge(*last(own))
        for i in range(NT):
            ins = dve.scalar_tensor_tensor(out=bonus[:, i, :], in0=r_fm[:, i, :], scalar=V("rw_r_k", i),
                                           in1=kraw[:, i, :], op0=ALU.mult, op1=ALU.mult)
        ins.then_inc(tick(own, "sumsrc_ready"), 1)
        dve.scalar_tensor_tensor(out=flat(b_fm), in0=flat(kk), scalar=-1.0, in1=flat(iclr),
                                          op0=ALU.mult, op1=ALU.mult).then_inc(tick(own), 1)
        dve.wait_ge(*last(own))
        dve.tensor_tensor(flat(b_fm), flat(b_fm), flat(e_neg), ALU.mult)
        dve.tensor_tensor(flat(k_fm), flat(kraw), flat(e_neg), ALU.mult)
        by_pair = lambda a: a.rearrange("p i (c t) -> p i c t", c=2)
        dve.tensor_tensor(ar[:, :, :, 0, :], by_pair(kk), by_pair(sg), ALU.mult)
        dve.tensor_tensor(ar[:, :, :, 1, :], by_pair(r_fm), by_pair(e_in), ALU.mult).then_inc(tick(own, "wkv_ready"), 1)
        dve.tensor_copy(p_end, e_in.rearrange("p i (c t) -> p i c t", t=CH)[:, :, :, CH - 1]).then_inc(tick(own), 1)
        dve.wait_ge(*last(own))
        dve.memset(y_fm[:, :, 0:CH], 0.0).then_inc(tick(own, "yzero_ready"), 1)
        for j in range(3):
            dve.wait_ge(*filled(f"bs_{j}"))
            t = slice(2 * j, 2 * j + 2)
            dve.tensor_tensor(bonus[:, t, :], two(f"bs_{j}"), v_fm[:, t, :], ALU.mult).then_inc(freed(own, f"bs_{j}"), 1)
        attention("mem1")
        dve.wait_ge(sem("cross_hi"), 1)
        dve.tensor_tensor(fm[1][:, 6:8, :], two("crT"), fm[0][:, 6:8, :].bitcast(F32),
                          ALU.subtract).then_inc(freed(own, "crT"), 1)
        wmask = C("wkv_mask").unsqueeze(1).to_broadcast((P, 2, S))
        for pr in range(2):
            tok = slice(pr * P, (pr + 1) * P)
            for w in range(3):
                evac(f"tr{pr}_{w}_0", kbv_tm[:, w, 0:384], src=bank_of(f"tr{pr}_{w}_0")[:, 0:384])
            for u in range(H):
                dve.wait_ge(*filled(f"sc{pr}_{u}"))
                dve.tensor_tensor(sc[:, u].rearrange("p (c b) t -> p c (b t)", c=2), two(f"sc{pr}_{u}"),
                                           wmask, ALU.mult).then_inc(freed(own, f"sc{pr}_{u}"), 1)
            dve.wait_ge(*last(own))
            for gi in range(3):
                us = slice(4 * gi, 4 * gi + 4)
                dve.tensor_tensor(tt[:, us, :], sc[:, us, 0, :],
                                           C("merge1").unsqueeze(1).to_broadcast((P, 4, P)), ALU.mult).then_inc(tick(own), 1)
                dve.wait_ge(*last(own))
                dve.tensor_tensor(tt[:, us, :], tt[:, us, :],
                                             ident.unsqueeze(1).to_broadcast((P, 4, P)), ALU.add).then_inc(tick(own, "tt_init"), 1)
            for p in range(2):
                evac(f"y0{pr}_{p}", y0[:, p * 384:(p + 1) * 384], src=bank_of(f"y0{pr}_{p}")[:, 0:384])
            for s in MERGES:
                for gi in range(3):
                    name = f"t{pr}_{s}_{gi}"
                    dve.wait_ge(*filled(name))
                    us = slice(4 * gi, 4 * gi + 4)
                    v4 = lambda b: b[:, :].rearrange("p (u t) -> p u t", u=4)
                    dve.tensor_tensor(tt[:, us, :], v4(bank_of(name, 0)), tt[:, us, :], ALU.add).then_inc(freed(own, name, 0), 1)
                    if s < 32:
                        dve.tensor_tensor(tms[gi], v4(bank_of(name, 1)), tms[gi], ALU.add).then_inc(freed(own, name, 1), 1)
                dve.wait_ge(*last(own))
            for q in range(2):
                c = 2 * pr + q
                rq = slice(q * CH, (q + 1) * CH)
                if c:
                    dve.wait_ge(*filled(f"z{c}c"))
                    for p in range(2):
                        y = y0[rq, p * 384:(p + 1) * 384]
                        dve.tensor_tensor(y, bank_of(f"z{c}c", p)[rq, 0:384], y, ALU.add).then_inc(freed(own, f"z{c}c", p), 1)
                if c < 3:
                    dve.wait_ge(*filled(f"h{c}c"))
                    new = state[:, (c + 1) % 2]
                    h = bank_of(f"h{c}c")[:, 0:384].rearrange("p (i v) -> p i v", i=NT)
                    decay = p_end[:, :, c].unsqueeze(2).to_broadcast((P, NT, DH))
                    if c:
                        dve.tensor_tensor(new, h, state[:, c % 2], ALU.add).then_inc(freed(own, f"h{c}c"), 1)
                        dve.wait_ge(*last(own))
                        dve.tensor_tensor(new, new, decay, ALU.mult).then_inc(tick(own, "state_ready"), 1)
                    else:
                        dve.tensor_tensor(new, h, decay, ALU.mult).then_inc(freed(own, f"h{c}c"), 1)
            dve.wait_ge(*filled(f"oo{pr}"))
            for c in (2 * pr, 2 * pr + 1):
                if c:
                    for p in range(2):
                        dve.wait_ge(*evacuated(f"oi{c}c", p))
            for a in range(2):
                y = y_fm[:, 3 * a:3 * a + 3, tok]
                dve.tensor_tensor(y, bank_of(f"oo{pr}", a)[:, 0:384].rearrange("p (i t) -> p i t", i=3), y,
                                           ALU.add).then_inc(freed(own, f"oo{pr}", a), 1)
        dve.wait_ge(*last(own))
        for j in range(3):
            dve.wait_ge(*filled(f"gm_{j}"))
            t = slice(2 * j, 2 * j + 2)
            dve.scalar_tensor_tensor(out=flat(y_fm[:, t, :]), in0=bank_of(f"gm_{j}")[:, :],
                                              scalar=-1.0 / DH, in1=flat(y_fm[:, t, :]), op0=ALU.mult, op1=ALU.add).then_inc(freed(own, f"gm_{j}"), 1)
        dve.wait_ge(*last(own))
        dve.tensor_tensor(zt, y_fm, y_fm, ALU.mult).then_inc(tick(own, "squares_ready"), 1)
        for j in range(3):
            dve.wait_ge(*filled(f"gv_{j}"))
            dve.tensor_scalar(flat(zt[:, 2 * j:2 * j + 2, :]), bank_of(f"gv_{j}")[:, :], 1.0 / DH, GN_EPS,
                                       ALU.mult, ALU.add).then_inc(freed(own, f"gv_{j}"), 1)
        dve.wait_ge(sem("gstd_ready"), 1)
        dve.reciprocal(flat(zt), flat(zt)).then_inc(tick(own), 1)
        dve.wait_ge(*last(own))
        dve.tensor_tensor(y_fm, y_fm, zt, ALU.mult).then_inc(tick(own), 1)
        dve.wait_ge(*last(own))
        for i in range(NT):
            dve.tensor_scalar(y_fm[:, i, :], y_fm[:, i, :], V("rw_lnx_w", i), V("rw_lnx_b", i),
                                       ALU.mult, ALU.add).then_inc(tick(own), 1)
        dve.wait_ge(*last(own))
        dve.tensor_tensor(y_fm, y_fm, bonus, ALU.add).then_inc(tick(own), 1)
        dve.wait_ge(*last(own))
        dve.tensor_tensor(mix_fm, y_fm, g_fm, ALU.mult).then_inc(tick(own, "mix1_ready"), 1)
        ahead("qm1")
        dve.wait_ge(sem("mix1_hi"), 1)
        dve.tensor_tensor(fm[1][:, 0:NT, :], mix_fm, fm[0][:, 0:NT, :].bitcast(F32),
                          ALU.subtract).then_inc(tick(own, "mix1_lo"), 1)
        rows_ahead("wo1")
        residual("wo1_0", "wo1_3")
        rms_norm(4, x_tm, tm)
        from_banks([(fm, lambda k: ("norm2", 8 + k))])
        ffn("f1", FT)
        residual("f1_out0", f"f1_out{FT // 2 - 1}")

        dve.wait_ge(sem("gains_in"), 16 * len(GAIN))
        rms_gain(5, x_tm, x_tm, "final_norm").then_inc(tick(own, "x2_ready"), 1)
        dve.wait_ge(*last(own))
        for j in range(2):
            dve.wait_ge(*filled(f"wsT{j}"))
            dve.tensor_tensor(wsT[:, 4 * j:4 * j + 4, :],
                                       bank_of(f"wsT{j}")[:, :].rearrange("p (g t) -> p g t", g=4),
                                       C("tri").unsqueeze(1).to_broadcast((P, 4, P)), ALU.mult).then_inc(freed(own, f"wsT{j}"), 1)
        rms_norm(6, x_tm, tm)
        from_banks([(fm, lambda k: ("mix_pre_g_2", k))])
        for j in range(4):
            ahead(f"sv{j}")
            dve.wait_ge(*evacuated(f"sv{j}"))
        ahead("su0")
        bnv = bn.rearrange("p (q a s) -> p q a s", q=2, a=2)
        mvv = mv[:, 0:4].rearrange("p (q s) -> p q s", q=2)
        for qt in range(QT):
            for a in range(2):
                dve.bn_stats(bnv[:, qt, a, :], v_n[:, qt, a * 512:(a + 1) * 512]).then_inc(tick(own), 1)
        dve.wait_ge(*last(own))
        for qt in range(QT):
            dve.bn_aggr(mvv[:, qt, :], bnv[:, qt].rearrange("p a s -> p (a s)")).then_inc(tick(own), 1)
        dve.wait_ge(*last(own))
        dve.tensor_scalar(mv[:, 4:6], mvv[:, :, 1], EPS, None, ALU.add).then_inc(tick(own, "lnvar_ready"), 1)
        dve.wait_ge(sem("lnstd_ready"), 1)
        dve.reciprocal(mv[:, 4:6], mv[:, 4:6]).then_inc(tick(own), 1)
        dve.wait_ge(*last(own))
        for qt in range(QT):
            dve.tensor_scalar(v_n[:, qt, :], v_n[:, qt, :], mvv[:, qt, 0:1], mv[:, 4 + qt:5 + qt],
                                       ALU.subtract, ALU.mult).then_inc(tick(own), 1)
        dve.wait_ge(*last(own))
        gsg = gains[:, GAIN["sgu_norm_g_2"], :].unsqueeze(1).to_broadcast((P, QT, D))
        dve.tensor_tensor(v_n, v_n, gsg, ALU.mult).then_inc(tick(own, "vn_ready"), 1)
        for j in range(1, 4):
            ahead(f"su{j}")
        ahead("sf")
        dve.wait_ge(*filled("sf"))
        dve.tensor_tensor(tmpf[:, 0], two("sf")[:, :, 0:NFH],
                                   b_forget.unsqueeze(1).to_broadcast((P, QT, NFH)), ALU.add).then_inc(freed(own, "sf"), 1)
        dve.wait_ge(*last(own))
        dve.tensor_scalar(tmpf[:, 2], tmpf[:, 0], -1.0, None, ALU.mult).then_inc(tick(own), 1)
        dve.wait_ge(*last(own))
        dve.tensor_tensor(tmpf[:, 1], tmpf[:, 0], tmpf[:, 2], ALU.max).then_inc(tick(own, "fabs_ready"), 1)
        dve.tensor_scalar(tmpf[:, 0], tmpf[:, 0], 0.0, None, ALU.min).then_inc(tick(own), 1)
        dve.wait_ge(sem("fln_ready"), 1)
        dve.wait_ge(*last(own))
        dve.tensor_tensor(logf, tmpf[:, 0], tmpf[:, 1], ALU.subtract).then_inc(tick(own, "logf_ready"), 1)
        dve.tensor_copy(sel[0:NFH], ident[0:NFH, 0:NFH].unsqueeze(2).to_broadcast((NFH, NFH, P))).then_inc(tick(own), 1)
        for j in range(4):
            ahead(f"fq{j}")
        for j in range(4):
            linear((f"fk{j}",), {f"fk{j}": (flat(k2[:, 2 * j:2 * j + 2, :]),)})
        for j in range(4):
            linear((f"fv{j}",), {f"fv{j}": (v_a[:, :, j * 256:(j + 1) * 256], two(f"fv{j}"))})
        dve.wait_ge(*filled("cc"))
        dve.tensor_scalar(ccum[0:NFH, :], bank_of("cc")[0:NFH, 0:S], -1.0, None, ALU.mult).then_inc(freed(own, "cc"), 1)
        for j in range(4):
            dve.wait_ge(*evacuated(f"su{j}"))
        for j in range(4):
            dve.wait_ge(*filled(f"sgu{j}"))
            qt, half = divmod(j, 2)
            for a in range(4):
                g = 4 * half + a
                u = u_g[:, qt, g * P:(g + 1) * P]
                ins = dve.scalar_tensor_tensor(out=u, in0=bank_of(f"sgu{j}")[:, a * P:(a + 1) * P],
                                               scalar=vecs2[:, g:g + 1], in1=u, op0=ALU.add, op1=ALU.mult)
            ins.then_inc(freed(own, f"sgu{j}"), 1)
        attention("fox", lambda j: ahead(GATE_UNITS[j]))
        for j in range(8):
            dve.wait_ge(*evacuated(GATE_UNITS[j]))
        dve.tensor_tensor(u_g, u_g, sga, ALU.mult).then_inc(tick(own), 1)
        dve.tensor_tensor(tm, tm, sgb, ALU.mult).then_inc(tick(own), 1)
        dve.wait_ge(*last(own))
        dve.tensor_tensor(tm, tm, u_g, ALU.add).then_inc(tick(own, "tm_ready"), 1)
        from_banks([(fm, None)])

        def product_out(tag, final):
            dve.wait_ge(*filled(final))
            for i in range(4):
                dve.tensor_copy(u_g[:, i // 2, (i % 2) * 512:(i % 2 + 1) * 512], bank_of(tag, i)[:, :]).then_inc(freed(own, tag, i), 1)
            dve.wait_ge(*last(own))

        rows_ahead("wo2")
        product_out("wo2_0", "wo2_3")
        rms_gain(7, u_g, u_g, "mix_post_g_2").then_inc(tick(own), 1)
        dve.wait_ge(*last(own))
        dve.tensor_tensor(x_tm, x_tm, u_g, ALU.add).then_inc(tick(own, "x3_ready"), 1)
        dve.wait_ge(*last(own))
        rms_norm(8, x_tm, tm)
        from_banks([(fm, lambda k: ("ffn_pre_g_2", k))])
        ffn("f2", 2 * FT)
        product_out("f2_out0", f"f2_out{FT // 2 - 1}")
        rms_gain(9, u_g, u_g, "ffn_post_g_2").then_inc(tick(own), 1)
        dve.wait_ge(*last(own))
        dve.tensor_tensor(tm, u_g, x_tm, ALU.add).then_inc(tick(own, "y_done"), 1)


INPUTS = [
    "x", "mem", "norm1", "norm_mem", "w_mem_kv", "w_o", "norm2", "w_ffn_in", "w_ffn_out", "nsa_w_in", "nsa_gate_b",
    "nsa_cmp_pos", "nsa_cmp_w1", "nsa_cmp_w2", "rw_w_in", "rw_mu", "rw_w0", "rw_w2", "rw_a0", "rw_a2", "rw_g2",
    "rw_k_k", "rw_k_a", "rw_r_k", "rw_lnx_w", "rw_lnx_b", "final_norm", "mix_pre_g_2", "w_in_2", "b_forget_2",
    "sgu_norm_g_2", "w_spatial_2", "b_spatial_2", "w_out_2", "mix_post_g_2", "ffn_pre_g_2", "w_gate_2", "w_up_2",
    "w_down_2", "ffn_post_g_2"]


def kernel(**inputs):
    import numpy as _np
    import concourse.bacc as _bacc
    from concourse import mybir as _mybir
    from concourse.bass_utils import run_bass_kernel_spmd as _run

    nc = _bacc.Bacc("TRN2", target_bir_lowering=False, num_devices=1)
    arrays, tensors = {}, {}
    for name in INPUTS:
        a = _np.ascontiguousarray(inputs[name])
        arrays[f"in_{name}"] = a
        tensors[name] = nc.dram_tensor(f"in_{name}", a.shape, _mybir.dt.from_np(a.dtype), kind="ExternalInput").ap()
    constants = shape_constants()[1]
    arrays["shape_constants"] = constants
    tensors["shape_constants"] = nc.dram_tensor("shape_constants", constants.shape, F32, kind="ExternalInput").ap()
    out = nc.dram_tensor("out_0", (1, S, D), F32, kind="ExternalOutput").ap()
    kernel_program(nc, tensors, out)
    r = _run(nc, [arrays], core_ids=[0])
    return r.results[0]["out_0"]
```

```python
import math
from contextlib import ExitStack

import numpy as np

import concourse.bass as bass
from concourse import mybir

F32 = mybir.dt.float32
F32R = mybir.dt.float32r
ALU = mybir.AluOpType
ACT = mybir.ActivationFunctionType
AX = mybir.AxisListType

P = 128
D = 1024
S = 256
QT = S // P
KT = D // P
DH = 64
H = 12
G = 4
R = H // G
MH = 4
FFN = 2816
FT = FFN // P
CMP_BLOCK, CMP_STRIDE = 32, 16
NCMP = (S - CMP_BLOCK) // CMP_STRIDE + 1
CH = 64
NT = H * DH // P
EPS = 1e-6
GN_EPS = 64e-5
MERGES = (2, 4, 8, 16, 32)
NEG = -1e30
C0 = math.exp(-0.5)
NFH = 8
RING = 3
SPLITS = 2
PIECES = 2
SLOT = 2048


def alibi_slopes(n):
    def pow2(m):
        start = 2.0 ** (-8.0 / m)
        return [start ** (i + 1) for i in range(m)]
    c = 2 ** int(math.floor(math.log2(n)))
    s = pow2(c)
    if c < n:
        s = s + pow2(2 * c)[0::2][: n - c]
    return [float(np.float32(v)) for v in s]


SLOPES = alibi_slopes(H)


def head_of(p, i):
    gp, r = divmod(i, R)
    return (2 * gp + p) * R + r


def shape_constants():
    i = np.arange(P)[:, None]
    t = np.arange(P)[None, :]
    parts = {}
    parts["ident"] = (i == t)
    same = (i // CH) == (t // CH)
    parts["wkv_mask"] = np.concatenate([same & (i < t), same & (i <= t)], 1)
    for s in (1, 2, 4, 8, 16, 32):
        parts[f"merge{s}"] = (i // (2 * s) == t // (2 * s)) & (i % (2 * s) < s) & (t % (2 * s) >= s)
    parts["head_ones"] = (i // DH) == (t // DH)
    heads_of = 2 * np.arange(NT)[None, :, None] + i[:, :, None] // DH
    parts["head_sel"] = (heads_of == np.arange(H)[None, None, :]).reshape(P, -1)
    parts["tri"] = i <= t
    parts["ones"] = np.ones((P, P))
    dist, causal = [], []
    for qt in range(QT):
        k = np.arange((qt + 1) * P)[None, :]
        d = (qt * P + i) - k
        dist.append(np.where(d >= 0, -d, NEG))
        causal.append(np.where(d >= 0, 0.0, NEG))
    parts["dist"] = np.concatenate(dist, 1)
    parts["causal"] = np.concatenate(causal, 1)
    parts["chunk_keep"] = np.broadcast_to((np.arange(S)[None, :] % CH) != 0, (P, S))
    end = np.arange(16)[None, :] * CMP_STRIDE + CMP_BLOCK - 1
    dist, mask = np.zeros((P, QT, 16)), np.zeros((P, QT, 16))
    for qt in range(QT):
        d = qt * P + i - end
        dist[:, qt] = np.where(d >= 0, -d, NEG)
        mask[:, qt] = (d >= 0) & (np.arange(16)[None, :] < NCMP)
    parts["cmp_dist"] = dist.reshape(P, -1)
    parts["cmp_mask"] = mask.reshape(P, -1)
    slopes = np.array([[[SLOPES[head_of(p, j)] for j in range(NT)]] * QT for p in range(2)])
    parts["slopes"] = np.broadcast_to(slopes.reshape(1, -1), (P, 2 * QT * NT))
    parts["q_scale"] = np.concatenate([np.repeat(DH ** -0.5 / slopes[p, 0:1], DH, 0) for p in range(2)], 0)
    parts["dup"] = np.concatenate([i == p * DH + t % DH for p in range(2)], 1)
    parts["head_back"] = (2 * np.arange(NT)[None, :, None] + t[:, None, :] // DH == i[:, :, None]).reshape(P, -1)
    at, cols = {}, 0
    for name, a in parts.items():
        at[name] = (cols, a.shape[1])
        cols += a.shape[1]
    return at, np.ascontiguousarray(np.concatenate([np.asarray(a, np.float32) for a in parts.values()], 1))


VEC = {}
for _n, _k in (("norm1", 16), ("norm_mem", 16), ("norm2", 16), ("mix_pre_g_2", 8), ("ffn_pre_g_2", 8),
               ("rw_w0", 6), ("rw_a0", 6), ("rw_k_k", 6), ("rw_k_a", 6), ("rw_r_k", 6),
               ("rw_lnx_w", 6), ("rw_lnx_b", 6), ("rw_mu", 20)):
    VEC[_n] = (sum(k for _, k in VEC.values()), _k)
MU_LAST = sum(k for _, k in VEC.values())
MU_TAIL = 32


def kernel_program(nc, T, out):
    ctx = ExitStack()
    with ctx:
        build(nc, T, out, ctx)


def build(nc, T, out, ctx):
    def sb(name, n):
        return ctx.enter_context(nc.sbuf_tensor(name, [P, n], F32))

    sems = {}

    def sem(name):
        if name not in sems:
            sems[name] = ctx.enter_context(nc.semaphore(name))
        return sems[name]

    CAT, cst_np = shape_constants()

    base = (nc.sbuf_base + 63) // 64 * 64
    fixed_at = [0]

    def place(name, n, at=None, dtype=F32):
        if at is None:
            column = fixed_at[0]
            fixed_at[0] += (n + 7) // 8 * 8
        else:
            column = SHARED + at
        assert base + 4 * (column + n) <= nc.sbuf_usable_end
        return nc.alloc_sbuf_tensor_at(name, [P, n], dtype, offset=base + 4 * column)[:, :]

    ring = place("ring", RING * SLOT)
    x_res = place("x_res", QT * D)
    act_hi = place("act_hi", KT * S, dtype=F32R)
    act_lo = place("act_lo", KT * S, dtype=F32R)
    rows_tm = place("rows_tm", QT * D)
    CONSTANTS = CAT["head_back"][0]
    cst = place("cst", CONSTANTS)
    vec = place("vec", P)
    cmp_w2 = place("cmp_w2", 2 * DH)
    kmem1 = place("kmem1", 2 * S)
    vmem1 = place("vmem1", QT * 256)
    qmem = place("qmem", 2 * S)
    sbuf_s = place("sbuf_s", 2 * 512)
    sbuf_p = place("sbuf_p", 2 * 512)
    sbuf_pt = place("sbuf_pt", 2 * 512)
    zshift = place("zshift", 2 * 2 * (S + 1))
    zdelta = place("zdelta", 2 * S)
    small = place("small", 512)
    SHARED = fixed_at[0]
    ARENA = 28672
    arena = place("arena", ARENA, 0)
    W_HI, W_LO = 0, SPLITS * SLOT
    w_hi = place("w_hi", SPLITS * SLOT, W_HI, F32R)
    w_lo = place("w_lo", SPLITS * SLOT, W_LO, F32R)
    FREE = 2 * SPLITS * SLOT
    hT_hi = place("hT_hi", FT * S, FREE, F32R)
    hT_lo = place("hT_lo", FT * S, FREE + FT * S, F32R)
    HT_END = FREE + 2 * FT * S

    x_tm = x_res.rearrange("p (q c) -> p q c", q=QT)
    tm = rows_tm.rearrange("p (q c) -> p q c", q=QT)

    def tiles(a):
        return a.rearrange("p (k t) -> p k t", t=S)

    fm = (tiles(act_hi), tiles(act_lo))
    hT = (tiles(hT_hi), tiles(hT_lo))

    def C(name, rows=P):
        o, n = CAT[name]
        return cst[0:rows, o:o + n]

    ident = C("ident")

    def V(name, i):
        o, _ = VEC[name]
        return vec[:, o + i:o + i + 1]

    arena_at = [0]

    def take(n):
        a = arena[:, arena_at[0]:arena_at[0] + n]
        arena_at[0] += n
        assert arena_at[0] <= ARENA
        return a

    small_at = [0]

    def tiny(n):
        a = small[:, small_at[0]:small_at[0] + n]
        small_at[0] += n
        assert small_at[0] <= 512
        return a

    arena_at[0] = HT_END
    silu = take(2 * S).rearrange("p (b t) -> p b t", b=2)
    hidden = take(2 * S).rearrange("p (b t) -> p b t", b=2)
    L2_START = arena_at[0]
    arena_at[0] = FREE
    qT = take(NT * S).rearrange("p (i t) -> p i t", i=NT)
    kcvT = take(2 * 2 * S).rearrange("p (v g t) -> p v g t", v=2, g=2)
    kselT = take(2 * S).rearrange("p (g t) -> p g t", g=2)
    kwinT = take(2 * S).rearrange("p (g t) -> p g t", g=2)
    vsel = take(QT * 256).rearrange("p (q c) -> p q c", q=QT)
    vwin = take(QT * 256).rearrange("p (q c) -> p q c", q=QT)
    kmem0 = take(2 * S)
    vmem0 = take(QT * 256)
    blocks = take(2 * CMP_BLOCK // 2 * 4 * NCMP).rearrange("p (v l g n) -> p v l g n", v=2, l=CMP_BLOCK // 2, g=4)
    hid = take(2 * 4 * NCMP).rearrange("p (v n) -> p v n", v=2)
    kcb = take(2 * NCMP)
    vcb = take(256)
    s_cmp = take(2 * QT * NT * 16).rearrange("p (h q i n) -> p h q i n", h=2, q=QT, i=NT)
    p_cmpT = take(8 * 384).rearrange("p (u c) -> p u c", u=8)
    posT = take(64)
    pos_rows = take(P)
    vec_rows = take(P)
    gate_b = take(3 * H)
    arena_at[0] = MEM = (arena_at[0] + 7) // 8 * 8
    memory = take(2 * KT * S), take(2 * KT * S)
    cmp_w1 = memory[1].rearrange("p (v l e) -> p v l e", v=2, l=CMP_BLOCK // 2)
    gates = tiny(QT * 3 * H).rearrange("p (q c) -> p q c", q=QT)
    rsum = tiny(2 * 40).rearrange("p (u q) -> p u q", q=QT)
    nmax = tiny(2 * 40).rearrange("p (u q) -> p u q", q=QT)
    coef = tiny(2 * 40).rearrange("p (u q) -> p u q", q=QT)
    ssq = tiny(2 * 10).rearrange("p (r q) -> p r q", q=QT)
    rms = tiny(2 * 10).rearrange("p (r q) -> p r q", q=QT)
    c_cmp = tiny(24)
    m_cmp = tiny(24)
    vecs2 = tiny(8)
    mem_fm = [tuple(tiles(place(f"mem{l}_{part}", KT * S, MEM + (2 * l + m) * KT * S, F32R))
                    for m, part in enumerate(("hi", "lo"))) for l in range(2)]

    arena_at[0] = 0
    ar = take(NT * 2 * 2 * P).rearrange("p (i c b t) -> p i c b t", i=NT, c=2, b=2)
    b_fm = take(NT * S).rearrange("p (i t) -> p i t", i=NT)
    k_fm = take(NT * S).rearrange("p (i t) -> p i t", i=NT)
    tmat = take(2 * 512).rearrange("p (b u t) -> p b u t", b=2, u=4)
    emat = take(2 * 512).rearrange("p (b u t) -> p b u t", b=2, u=4)
    assert arena_at[0] == FREE
    g_fm = take(NT * S).rearrange("p (i t) -> p i t", i=NT)
    bonus = take(NT * S).rearrange("p (i t) -> p i t", i=NT)
    v_fm = take(NT * S).rearrange("p (i t) -> p i t", i=NT)
    AFTER = arena_at[0]
    r_fm = take(NT * S).rearrange("p (i t) -> p i t", i=NT)
    kraw = take(NT * S).rearrange("p (i t) -> p i t", i=NT)
    lora = take(3 * S).rearrange("p (i t) -> p i t", i=3)
    iclr = take(NT * S).rearrange("p (i t) -> p i t", i=NT)
    sg = take(NT * S).rearrange("p (i t) -> p i t", i=NT)
    csum = take(NT * S).rearrange("p (i t) -> p i t", i=NT)
    e_in = take(NT * S).rearrange("p (i t) -> p i t", i=NT)
    kk = take(NT * S).rearrange("p (i t) -> p i t", i=NT)
    e_neg = rows_tm[:, 0:NT * S].rearrange("p (i t) -> p i t", i=NT)
    arena_at[0] = AFTER
    sc = take(H * 512).rearrange("p (u b t) -> p u b t", u=H, b=4)
    tt = take(H * P).rearrange("p (u t) -> p u t", u=H)
    cmat = take(2 * 512).rearrange("p (b u t) -> p b u t", b=2, u=4)
    cmat3 = take(512)
    kbv_tm = take(3 * H * DH).rearrange("p (w c) -> p w c", w=3)
    p_end = tiny(NT * 4).rearrange("p (i c) -> p i c", i=NT)
    y_fm = rows_tm[:, 0:NT * S].rearrange("p (i t) -> p i t", i=NT)
    y0 = sbuf_s[:, 0:H * DH]
    u_tm = sbuf_p[:, 0:H * DH]
    state = sbuf_pt[:, 0:2 * NT * DH].rearrange("p (b i v) -> p b i v", b=2, i=NT)
    cross = zdelta.rearrange("p (q c) -> p q c", q=QT)
    zt = arena[:, AFTER:AFTER + NT * S].rearrange("p (i t) -> p i t", i=NT)
    kk_sq = b_fm
    mix_fm = zt
    assert arena_at[0] <= ARENA - 4 * H * DH
    arena_at[0] = ARENA - 4 * H * DH
    head_back = take(H * DH)
    rw_wa2 = take(H * DH)
    rw_g2 = take(2 * H * DH)
    tms = [tmat[:, 0], tmat[:, 1], zshift[:, 0:512].rearrange("p (u t) -> p u t", u=4)]
    ems = [emat[:, 0], emat[:, 1], zshift[:, 512:1024].rearrange("p (u t) -> p u t", u=4)]
    cms = [cmat[:, 0], cmat[:, 1], cmat3.rearrange("p (u t) -> p u t", u=4)]
    VEC_DMAS, SMALL_DMAS = len(VEC) + 1, 4

    arena_at[0] = L2_START
    gains = take(4 * D).rearrange("p (g c) -> p g c", g=4)
    GAIN = {"final_norm": 0, "sgu_norm_g_2": 1, "mix_post_g_2": 2, "ffn_post_g_2": 3}
    u_g = take(QT * D).rearrange("p (q c) -> p q c", q=QT)
    v_a = take(QT * D)
    ws_raw = v_a[:, 0:NFH * P].rearrange("p (g t) -> p g t", g=NFH)
    v_a = v_a.rearrange("p (q c) -> p q c", q=QT)
    arena_at[0] = FREE
    q2, k2 = tiles(take(KT * S)), tiles(take(KT * S))
    logf = take(16).rearrange("p (q h) -> p q h", q=QT)
    tmpf = take(48).rearrange("p (a q h) -> p a q h", a=3, q=QT)
    ccum = take(S)
    sel = take(NFH * P).rearrange("p (h t) -> p h t", h=NFH)
    sga = take(QT * D).rearrange("p (q c) -> p q c", q=QT)
    sgb = take(QT * D).rearrange("p (q c) -> p q c", q=QT)
    v_n = take(QT * D).rearrange("p (q c) -> p q c", q=QT)
    assert arena_at[0] <= L2_START
    wsT = zshift[:, 0:NFH * P].rearrange("p (g t) -> p g t", g=NFH)
    narrow = zdelta[:, 0:S]
    bn = tiny(24)
    mv = tiny(8)
    b_forget = tiny(8)

    bank = [ctx.enter_context(nc.psum_tensor(f"bank{i}", [P, 512], F32)) for i in range(8)]

    number, uses, slots = {}, {}, []
    turn_of, fills = [0, 0], [0] * 8

    def unit(name, banks=1, slot=None, upper=False):
        number[name] = len(number)
        uses[name] = []
        for _ in range(banks):
            b = 4 + turn_of[1] % 4 if upper else turn_of[0] % 4
            turn_of[upper] += 1
            uses[name].append((b, fills[b]))
            fills[b] += 1
        if slot:
            slots.append((name, slot))

    def align():
        turn_of[0] += -turn_of[0] % 4


    def cols(w, a, b):
        return w[:, a:b].rearrange("(k p) n -> p k n", p=P)

    def slot_cols(w, a, b):
        return lambda dst: [(dst[:, 0:KT * (b - a)].rearrange("p (k n) -> p k n", k=KT), cols(w, a, b))]

    def slot_rows(w, j):
        return lambda dst: [(dst.rearrange("p (k n) -> p k n", k=2),
                             w[2 * j * P:(2 * j + 2) * P, :].rearrange("(k p) n -> p k n", p=P))]

    def slot_pair(wa, a, wb, b):
        return lambda dst: [
            (dst.rearrange("p (k n) -> p k n", k=KT)[:, :, 0:P], cols(wa, a, a + P)),
            (dst.rearrange("p (k n) -> p k n", k=KT)[:, :, P:2 * P], cols(wb, b, b + P))]

    def slot_q(w, j):
        def loads(dst):
            d = dst.rearrange("p (k n) -> p k n", k=KT)
            for a in range(2):
                for p in range(2):
                    h = head_of(p, 2 * j + a)
                    yield (d[:, :, a * P + p * DH:a * P + (p + 1) * DH], cols(w, h * DH, (h + 1) * DH))
        return loads

    def ffn_units(tag, wa, a0, wb, b0, wo):
        for j in range(FT):
            unit(f"{tag}_in{j}", 1, slot_pair(wa, a0 + j * P, wb, b0 + j * P))
        align()
        for j in range(FT // 2):
            unit(f"{tag}_out{j}", 4 if j == 0 else 0, slot_rows(wo, j))

    nsa = T["nsa_w_in"][0]
    MW = H * DH
    GL = MW + 6 * 256
    proj = {name: slot_cols(nsa, MW + j * 256, MW + (j + 1) * 256)
            for j, name in enumerate(("kc", "vc", "ks", "vs", "kw", "vw"))}
    proj |= {f"q{j}": slot_q(nsa, j) for j in range(3)}
    proj |= {"gl": slot_cols(nsa, GL, GL + 3 * H), "qm0": slot_cols(nsa, GL + 3 * H, GL + 3 * H + 256)}
    mem_w = {f"{n}mem{l}": slot_cols(T["w_mem_kv"][l], o, o + 256) for l in range(2) for n, o in (("k", 0), ("v", 256))}
    proj |= mem_w
    align()
    for name in ("kc", "vc", "q0", "dup0", "q1", "dup1", "q2", "ks", "hid0", "vs", "hid1", "kw", "kcb", "vcb", "vw",
                 "gl", "cs0", "cs1", "glT", "qm0"):
        unit(name, 2 if name.startswith("dup") else 1, proj.get(name))
    for j in range(8):
        unit(f"pct{j}")
    for j in range(4):
        unit(f"oc{j}")
    align()
    MEM_UNITS = ("kmem0", "vmem0", "kmem1", "vmem1")
    for name in MEM_UNITS:
        if name == "vmem1":
            turn_of[0] += 1
        unit(name, 1, proj[name])
    align()
    for j in range(4):
        unit(f"wo0_{j}", 4 if j == 0 else 0, slot_rows(T["w_o"][0], j))
    ffn_units("f0", T["w_ffn_in"][0], 0, T["w_ffn_in"][0], FFN, T["w_ffn_out"][0])
    rw = T["rw_w_in"][0]
    for j in range(10):
        unit(f"z{j}", 1, slot_cols(rw, j * 256, (j + 1) * 256))
    unit("z10", 1, slot_cols(rw, 2560, 2560 + P))
    unit("qm1", 1, slot_cols(rw, 2592, 2848))
    for n in ("w2", "a2", "g2", "kn", "kb", "bs"):
        for j in range(3 if n != "kn" else 1):
            unit(f"{n}_{j}" if n != "kn" else n)
    unit("crT")
    for pr in range(2):
        for w in range(3):
            for h in range(2):
                unit(f"tr{pr}_{w}_{h}", 1, upper=True)
        for u in range(H):
            unit(f"sc{pr}_{u}", 1, upper=True)
        for p in range(2):
            unit(f"y0{pr}_{p}", 1)
        for gi in range(3):
            unit(f"ti{pr}_{gi}", 1)
        for s in MERGES:
            for gi in range(3):
                unit(f"e{pr}_{s}_{gi}", 1, upper=True)
            for gi in range(3):
                unit(f"t{pr}_{s}_{gi}", 1 if s == 32 else 2)
        for c in (2 * pr, 2 * pr + 1):
            if c:
                unit(f"z{c}c", 2, upper=True)
            unit(f"u{c}c", 2)
            if c < 3:
                unit(f"h{c}c", 1, upper=True)
            if c:
                unit(f"oi{c}c", 2, upper=True)
        unit(f"oo{pr}", 2)
    for n in ("gm", "gv", "gr"):
        for j in range(3 if n != "gv" else 1):
            unit(f"{n}_{j}" if n != "gv" else n)
    align()
    for j in range(4):
        unit(f"wo1_{j}", 4 if j == 0 else 0, slot_rows(T["w_o"][1], j))
    ffn_units("f1", T["w_ffn_in"][1], 0, T["w_ffn_in"][1], FFN, T["w_ffn_out"][1])
    w2in = T["w_in_2"][0]
    unit("wsT0"), unit("wsT1")
    for name, base2 in (("sv", 1024), ("su", 0)):
        for j in range(4):
            unit(f"{name}{j}", 1, slot_cols(w2in, base2 + j * 256, base2 + (j + 1) * 256))
    unit("sf", 1, slot_cols(w2in, 7168, 7176))
    for name, base2 in (("fq", 2048), ("fk", 3072), ("fv", 4096)):
        for j in range(4):
            unit(f"{name}{j}", 1, slot_cols(w2in, base2 + j * 256, base2 + (j + 1) * 256))
            if name == "fq" and j == 0:
                unit("sfT")
    unit("cc")
    for j in range(4):
        unit(f"sgu{j}")
    GATE_UNITS = []
    for name, base2 in (("ga", 5120), ("gb", 6144)):
        for j in range(4):
            GATE_UNITS.append(f"{name}{j}")
            unit(f"{name}{j}", 1, slot_cols(w2in, base2 + j * 256, base2 + (j + 1) * 256))
    align()
    for j in range(4):
        unit(f"wo2_{j}", 4 if j == 0 else 0, slot_rows(T["w_out_2"][0], j))
    ffn_units("f2", T["w_gate_2"][0], 0, T["w_up_2"][0], 0, T["w_down_2"][0])

    ROW_PRODUCTS = ["wo0_3", "f0_out10", "wo1_3", "f1_out10", "wo2_3", "f2_out10"]

    slot_no = {name: n for n, (name, _) in enumerate(slots)}
    landed, total = {}, [0] * RING
    for n, (name, loads) in enumerate(slots):
        k = len(list(loads(ring[:, 0:SLOT])))
        total[n % RING] += 16 * k
        landed[name] = (n % RING, total[n % RING])

    split_names = [name for name, _ in slots]
    split_no = {name: m for m, name in enumerate(split_names)}
    width = {name: SLOT for name in split_names}
    width |= {"gl": KT * 3 * H, "sf": KT * NFH, "z10": KT * P}

    HOLD = {"z10": "qm1"}

    def split_end(name):
        if name in HOLD:
            return split_no[HOLD[name]] + 1
        return min(split_no[name] + SPLITS + 1, len(split_names))

    def pieces(name):
        w = width[name] // PIECES
        return [(i * w, (i + 1) * w) for i in range(PIECES)]

    unit_done = sem("unit_done")
    slot_landed = [sem(f"slot_landed{r}") for r in range(RING)]
    bank_free = [sem(f"bank_free{b}") for b in range(8)]

    def bank_of(name, i=0):
        return bank[uses[name][i][0]]

    def filled(name):
        return unit_done, number[name] + 1

    def evacuated(name, i=0):
        b, before = uses[name][i]
        return bank_free[b], before + 1

    def counter(name):
        return {"step": name, "counts": {}, "last": None}

    def tick(own, name=None):
        name = name or own["step"]
        own["counts"][name] = own["counts"].get(name, 0) + 1
        own["last"] = (sem(name), own["counts"][name])
        return sem(name)

    def freed(own, name, i=0):
        b, before = uses[name][i]
        own["last"] = (bank_free[b], before + 1)
        return bank_free[b]

    def last(own):
        return own["last"]

    hid_base = {"f0": 0, "f1": FT, "f2": 2 * FT}

    heads = []
    for h in range(H):
        heads += [("sel", h), ("win", h)]
    heads += [("mem0", i) for i in range(MH)]
    heads += [("mem1", i) for i in range(MH)]
    heads += [("fox", i) for i in range(NFH)]
    first = {}
    for n, (kind, _) in enumerate(heads):
        first.setdefault(kind, n)
    AFTER_STAGE = {"nsa": "wo0_0", "mem1": "crT"}
    LAG = {"nsa": 2, "mem1": 2, "fox": 1}
    STAGES = {"nsa": range(0, 28), "mem1": range(28, 32), "fox": range(32, 40)}

    def head_parts(n):
        kind, i = heads[n]
        if kind in ("mem0", "mem1"):
            k = (kmem0 if kind == "mem0" else kmem1[:, :]).rearrange("p (g t) -> p g t", g=2)
            v = (vmem0 if kind == "mem0" else vmem1[:, :]).rearrange("p (q c) -> p q c", q=QT)
            q = qmem[:, :].rearrange("p (g t) -> p g t", g=2)
            r = slice((i % 2) * DH, (i % 2) * DH + DH)
            return q[r, i // 2, :], k[r, i // 2, :], v[:, :, i * DH:(i + 1) * DH], DH, [(0, 0, S), (1, S, S)]
        causal = [(0, 0, P), (1, P, S)]
        if kind == "fox":
            return q2[:, i, :], k2[:, i, :], v_a[:, :, i * P:(i + 1) * P], P, causal
        g, r = divmod(i, R)
        p, gp = g % 2, g // 2
        rows = slice(p * DH, (p + 1) * DH)
        k = kselT if kind == "sel" else kwinT
        v = vsel if kind == "sel" else vwin
        return qT[rows, gp * R + r, :], k[rows, gp, :], v[:, :, g * DH:(g + 1) * DH], DH, causal

    def blocks_of(n):
        *_, segs = head_parts(n)
        return [(qt, kt, c + kt * P) for qt, c, nk in segs for kt in range(nk // P)]

    score_bank = lambda n: bank[4 + n % 2]
    pt_bank = bank[6]
    o_bank = lambda n: bank[3 if n % 2 and heads[n][0] != "fox" else 7]

    cst_d = T["shape_constants"]
    vec_loads = []
    for name, (row, k) in VEC.items():
        src = T[name]
        if name == "rw_mu":
            src = src[0:1, 0:k * P].rearrange("a (k c) -> (a k) c", c=P)
        elif name == "rw_r_k":
            src = src.rearrange("a (i h) d -> (a i) (h d)", h=2)
        else:
            src = src.rearrange("a (k c) -> (a k) c", c=P)
        vec_loads.append((vec_rows[row:row + k, :], src))
    vec_loads.append((vec_rows[MU_LAST:MU_LAST + 1, 0:MU_TAIL], T["rw_mu"][0:1, 20 * P:]))
    block = ctx.enter_context(nc.Block())

    @block.sync
    def _(sp):
        sp.dma_start(x_tm, T["x"][0].rearrange("(q p) c -> p q c", p=P)).then_inc(sem("x_in"), 16)
        sp.wait_ge(sem("vec_zero"), 1)
        for dst, src in vec_loads[1::2]:
            sp.dma_start(dst, src).then_inc(sem("vec_in"), 16)
        for n, (name, loads) in enumerate(slots):
            if n >= RING:
                sp.wait_ge(sem("lo_ready"), PIECES * (n - RING + 1))
            if name == "f0_in4":
                sp.wait_ge(*filled("f0_in0"))
                for dst, src in ((head_back[0:H, :], cst_d[0:H, CONSTANTS:]), (rw_wa2[0:DH, :], T["rw_w2"][0]), (rw_wa2[DH:P, :], T["rw_a2"][0]),
                                 (rw_g2[:, 0:MW], T["rw_g2"][0, 0:P]),
                                 (rw_g2[0:32, MW:2 * MW], T["rw_g2"][0, P:P + 32])):
                    sp.dma_start(dst, src).then_inc(sem("lora_in"), 16)
            if name == "f1_in4":
                sp.wait_ge(unit_done, number["f1_in0"] + 1)
                for gn, g in GAIN.items():
                    src = T[gn].rearrange("(a c) -> a c", a=1) if gn == "final_norm" else T[gn]
                    sp.dma_start(gains[:, g, :], src.to_broadcast((P, D))).then_inc(sem("gains_in"), 16)
                sp.dma_start(ws_raw, T["w_spatial_2"][0].rearrange("g t s -> t g s")).then_inc(sem("ws_in"), 16)
            r = n % RING
            for dst, src in loads(ring[:, r * SLOT:(r + 1) * SLOT]):
                sp.dma_start(dst, src).then_inc(slot_landed[r], 16)
            if name == "q0":
                for v in range(2):
                    sp.dma_start(cmp_w1[:, v], T["nsa_cmp_w1"][0, v].rearrange("(a b) d e -> (b d) a e", b=2)).then_inc(sem("cmp_in"), 16)
            if name == "q2":
                sp.wait_ge(sem("fm_full"), 4)
                sp.dma_start(tm, T["mem"][0].rearrange("(q p) c -> p q c", p=P)).then_inc(sem("mem_in"), 16)
        sp.wait_ge(sem("y_done"), 1)
        sp.dma_start(out[0].rearrange("(q p) c -> p q c", p=P), tm).then_inc(sem("y_out"), 16)
        sp.wait_ge(sem("y_out"), 16)

    @block.gpsimd
    def _(pool):
        own = counter("pool_step")
        pool.memset(vec_rows, 0.0).then_inc(tick(own, "vec_zero"), 1)
        pool.wait_ge(sem("csum_ready"), 1)
        pool.tensor_tensor(sg, csum, sg, ALU.subtract).then_inc(tick(own, "cexc_ready"), 1)
        pool.wait_ge(*evacuated("bs_2"))
        for i in range(NT):
            ins = pool.tensor_scalar(bonus[:, i, :], bonus[:, i, :], V("rw_lnx_b", i), None, ALU.add)
        ins.then_inc(tick(own, "bonus_ready"), 1)
        for pr in range(2):
            pool.wait_ge(*evacuated(f"sc{pr}_{H - 1}"))
            for s in MERGES:
                for gi in range(3):
                    if pr or s > 2:
                        prev = (pr, MERGES[MERGES.index(s) - 1]) if s > 2 else (0, 32)
                        pool.wait_ge(*filled(f"e{prev[0]}_{prev[1]}_{gi}"))
                    pool.tensor_tensor(
                        cms[gi], sc[:, gi * 4:(gi + 1) * 4, 0, :],
                        C(f"merge{s}").unsqueeze(1).to_broadcast((P, 4, P)), ALU.mult).then_inc(tick(own, "merge_part"), 1)

    @block.tensor
    def _(pe):
        def begin(name):
            for b, before in uses.get(name, ()):
                if before:
                    pe.wait_ge(bank_free[b], before)

        def split(name, k):
            b, n = split_no[name] % SPLITS, width[name]
            return [w[:, b * SLOT:b * SLOT + n].rearrange("p (k n) -> p k n", k=k) for w in (w_hi, w_lo)]

        def piece(name, i):
            pe.wait_ge(sem("lo_ready"), PIECES * split_no[name] + i + 1)

        def product(o, ahl, bhl, first, final):
            pe.matmul(o, ahl[0], bhl[0], start=first, stop=False)
            pe.matmul(o, ahl[0], bhl[1], start=False, stop=False)
            return pe.matmul(o, ahl[1], bhl[0], start=False, stop=final)

        def fm_unit(name, act):
            begin(name)
            n = width[name] // KT
            w = split(name, KT)
            for c in range(0, n, P):
                for k in range(KT):
                    if c == 0:
                        tile_ready(k)
                        if k % (KT // PIECES) == 0:
                            piece(name, k // (KT // PIECES))
                    ins = product(bank_of(name)[0:min(n, P), c * 2:c * 2 + S], [a[:, k, c:min(c + P, n)] for a in w],
                                  [a[:, k, :] for a in act], k == 0, k == KT - 1)
            ins.then_inc(unit_done, 1)

        def tm_unit(name, act):
            begin(name)
            n = width[name] // KT
            w = split(name, KT)
            for qt in range(QT):
                for k in range(KT):
                    if qt == 0:
                        tile_ready(k)
                        if k % (KT // PIECES) == 0:
                            piece(name, k // (KT // PIECES))
                    ins = product(bank_of(name)[:, qt * 256:qt * 256 + n],
                                  [a[:, k, qt * P:(qt + 1) * P] for a in act], [a[:, k, :] for a in w],
                                  k == 0, k == KT - 1)
            ins.then_inc(unit_done, 1)

        def turn_narrow(name, n):
            begin(f"{name}T")
            pe.wait_ge(*evacuated(name))
            for qt in range(QT):
                ins = pe.transpose(bank_of(f"{name}T")[:, qt * 256:qt * 256 + n], narrow[0:n, qt * P:(qt + 1) * P],
                                   ident[0:n, 0:n])
            ins.then_inc(unit_done, 1)

        def row_unit(tag, j, n, act):
            name = f"{tag}{j}"
            begin(name)
            w = split(name, 2)
            tile_ready(2 * j)

            def tile_product(a, qt):
                k = 2 * j + a
                for half in range(2):
                    ins = product(bank_of(f"{tag}0", 2 * qt + half)[:, :], [v[:, k, qt * P:(qt + 1) * P] for v in act],
                                  [v[:, a, half * 512:(half + 1) * 512] for v in w], k == 0, k == 2 * n - 1)
                return ins

            if j < n - 1:
                for a in range(2):
                    piece(name, a)
                    for qt in range(QT):
                        ins = tile_product(a, qt)
            else:
                piece(name, 1)
                for qt in range(QT):
                    for a in range(2):
                        ins = tile_product(a, qt)
                    if qt == 0:
                        ins.then_inc(sem("tile0_done"), 1)
            ins.then_inc(unit_done, 1)

        fm_event = [0]

        def to_fm(ready, value):
            e = fm_event[0]
            fm_event[0] += 1
            pe.wait_ge(sem(ready), value)
            for j in range(4):
                for a in range(2):
                    for qt in range(QT):
                        k = 2 * j + a
                        src = tm[:, qt, k * P:(k + 1) * P]
                        ins = pe.transpose(bank[4 + j][:, a * S + qt * P:a * S + (qt + 1) * P], src, ident)
                ins.then_inc(sem("fm_full"), 1)

        expected = [None]

        def fm_ready():
            expected[0] = 4 * (fm_event[0] - 1)

        def tile_ready(k):
            if expected[0] is not None and k % 2 == 0:
                pe.wait_ge(sem("fm_lo"), expected[0] + k // 2 + 1)
                if k == KT - 2:
                    expected[0] = None

        def all_ready():
            for k in range(0, KT, 2):
                tile_ready(k)

        def scores(n):
            q, k, _, _, segs = head_parts(n)
            kind, i = heads[n]
            if n >= 2 and n - 2 in stage:
                pe.wait_ge(sem("exp_done" if heads[n - 2][0].startswith("mem") else "nmax_ready"), n - 1)
            for qt, c, nk in segs:
                ins = pe.matmul(score_bank(n)[:, c:c + nk], q[:, qt * P:(qt + 1) * P], k[:, 0:nk],
                                start=True, stop=(kind != "fox"))
                if kind == "fox":
                    ins = pe.matmul(score_bank(n)[:, c:c + nk], sel[0:NFH, i, :], ccum[0:NFH, 0:nk],
                                    start=False, stop=True)
            ins.then_inc(sem("scores_full"), 1)

        def turn(n):
            pe.wait_ge(sem("exp_done"), n + 1)
            if n >= 1:
                pe.wait_ge(sem("pt_copied"), n)
            for qt, kt, c in blocks_of(n):
                ins = pe.transpose(pt_bank[:, c:c + P], sbuf_p[:, (n % 2) * 512 + c:(n % 2) * 512 + c + P], ident)
            ins.then_inc(sem("pt_full"), 1)

        def values(n):
            _, _, v, w, _ = head_parts(n)
            pe.wait_ge(sem("pt_copied"), n + 1)
            if n >= 2:
                pe.wait_ge(sem("o_read"), n if heads[n][0] == "fox" else n - 1)
            bl = blocks_of(n)
            for qt in range(QT):
                mine = [(kt, c) for q, kt, c in bl if q == qt]
                for m, (kt, c) in enumerate(mine):
                    o = qt * P
                    ins = pe.matmul(o_bank(n)[:, o:o + w], sbuf_pt[:, (n % 2) * 512 + c:(n % 2) * 512 + c + P],
                                    v[:, kt, :], start=(m == 0), stop=(m == len(mine) - 1))
            ins.then_inc(sem("o_full"), 1)

        stage = ()

        def attention(which, between=None):
            nonlocal stage
            stage = STAGES[which]
            if which != "fox":
                pe.wait_ge(bank_free[3], min(before for name, u in uses.items() for b, before in u
                                             if b == 3 and number[name] >= number[AFTER_STAGE[which]]))
            lag = LAG[which]
            for n in range(stage[0], stage[-1] + lag + 2):
                if n in stage:
                    scores(n)
                if between:
                    between(n - stage[0])
                if n - lag in stage:
                    turn(n - lag)
                if n - lag - 1 in stage:
                    values(n - lag - 1)

        def ffn(tag):
            for j in range(FT):
                fm_unit(f"{tag}_in{j}", fm)
            pe.wait_ge(sem("hidden_lo"), hid_base[tag] + FT)
            for j in range(FT // 2):
                row_unit(f"{tag}_out", j, FT // 2, hT)

        def wkv():
            pe.wait_ge(sem("wkv_ready"), 1)
            for pr in range(2):
                tok = slice(pr * P, (pr + 1) * P)
                for w, src in enumerate((b_fm, k_fm, v_fm)):
                    for h in range(2):
                        name = f"tr{pr}_{w}_{h}"
                        begin(name)
                        for a in range(3):
                            ins = pe.transpose(bank_of(name)[:, a * P:(a + 1) * P], src[:, 3 * h + a, tok], ident)
                        ins.then_inc(unit_done, 1)
                for u in range(H):
                    p, i = divmod(u, NT)
                    r = slice(p * DH, (p + 1) * DH)
                    name = f"sc{pr}_{u}"
                    begin(name)
                    both = ar[r, i, pr, :, :].rearrange("p b t -> p (b t)")
                    pe.matmul(bank_of(name)[:, 0:S], b_fm[r, i, tok], both, start=True, stop=True)
                    pe.matmul(bank_of(name)[:, S:2 * S], k_fm[r, i, tok], both, start=True, stop=True).then_inc(unit_done, 1)
                pe.wait_ge(*evacuated(f"tr{pr}_2_1"))
                for p in range(2):
                    begin(f"y0{pr}_{p}")
                    pe.wait_ge(*evacuated(f"sc{pr}_{p * NT + NT - 1}"))
                    for i in range(NT):
                        ins = pe.matmul(bank_of(f"y0{pr}_{p}")[:, i * DH:(i + 1) * DH], sc[:, p * NT + i, 2, :],
                                        kbv_tm[:, 2, (2 * i + p) * DH:(2 * i + p + 1) * DH], start=True, stop=True)
                    ins.then_inc(unit_done, 1)
                for gi in range(3):
                    begin(f"ti{pr}_{gi}")
                    pe.wait_ge(sem("tt_init"), 3 * pr + gi + 1)
                    for a in range(4):
                        ins = pe.transpose(bank_of(f"ti{pr}_{gi}")[:, a * P:(a + 1) * P], tt[:, 4 * gi + a, :], ident)
                    ins.then_inc(unit_done, 1)
                for li, s in enumerate(MERGES):
                    for gi in range(3):
                        name = f"e{pr}_{s}_{gi}"
                        begin(name)
                        pe.wait_ge(sem("merge_part"), 15 * pr + 3 * li + gi + 1)
                        if li:
                            for b in range(2):
                                pe.wait_ge(*evacuated(f"t{pr}_{MERGES[li - 1]}_{gi}", b))
                        else:
                            pe.wait_ge(*evacuated(f"ti{pr}_{gi}"))
                        for a in range(4):
                            ins = pe.matmul(bank_of(name)[:, a * P:(a + 1) * P], cms[gi][:, a, :], tms[gi][:, a, :],
                                            start=True, stop=True)
                        ins.then_inc(unit_done, 1)
                    for gi in range(3):
                        name = f"t{pr}_{s}_{gi}"
                        begin(name)
                        pe.wait_ge(*evacuated(f"e{pr}_{s}_{gi}"))
                        for a in range(4):
                            ins = pe.matmul(bank_of(name, 0)[:, a * P:(a + 1) * P], ems[gi][:, a, :],
                                            tt[:, 4 * gi + a, :], start=True, stop=True)
                        if s < 32:
                            for a in range(4):
                                ins = pe.matmul(bank_of(name, 1)[:, a * P:(a + 1) * P], tt[:, 4 * gi + a, :],
                                                ems[gi][:, a, :], start=True, stop=True)
                        ins.then_inc(unit_done, 1)
                for gi in range(3):
                    pe.wait_ge(*evacuated(f"t{pr}_32_{gi}"))
                pe.wait_ge(*evacuated(f"tr{pr}_0_1")), pe.wait_ge(*evacuated(f"tr{pr}_1_1"))
                for q in range(2):
                    c = 2 * pr + q
                    rq = slice(q * CH, (q + 1) * CH)
                    if c:
                        begin(f"z{c}c")
                        if c == 1:
                            pe.wait_ge(*evacuated("h0c"))
                        else:
                            pe.wait_ge(sem("state_ready"), c - 1)
                        for p in range(2):
                            r = slice(p * DH, (p + 1) * DH)
                            for i in range(NT):
                                ins = pe.matmul(bank_of(f"z{c}c", p)[rq, i * DH:(i + 1) * DH],
                                                ar[r, i, pr, 0, q * CH:(q + 1) * CH], state[r, c % 2, i, :],
                                                start=True, stop=True)
                        ins.then_inc(unit_done, 1)
                    begin(f"u{c}c")
                    for p in range(2):
                        pe.wait_ge(*evacuated(f"z{c}c" if c else "y00_" + str(p), p if c else 0))
                    for p in range(2):
                        for i in range(NT):
                            u = p * NT + i
                            ins = pe.matmul(bank_of(f"u{c}c", p)[rq, i * DH:(i + 1) * DH],
                                            tt[rq, u, q * CH:(q + 1) * CH], y0[rq, u * DH:(u + 1) * DH],
                                            start=True, stop=True)
                    ins.then_inc(unit_done, 1)
                    if c < 3:
                        begin(f"h{c}c")
                        for p in range(2):
                            pe.wait_ge(*evacuated(f"u{c}c", p))
                        for p in range(2):
                            r = slice(p * DH, (p + 1) * DH)
                            for i in range(NT):
                                hc = slice((2 * i + p) * DH, (2 * i + p + 1) * DH)
                                o = bank_of(f"h{c}c")[r, i * DH:(i + 1) * DH]
                                pe.matmul(o, kbv_tm[rq, 0, hc], u_tm[rq, (p * NT + i) * DH:(p * NT + i + 1) * DH],
                                          start=True, stop=False)
                                ins = pe.matmul(o, kbv_tm[rq, 1, hc], kbv_tm[rq, 2, hc], start=False, stop=True)
                        ins.then_inc(unit_done, 1)
                    if c:
                        begin(f"oi{c}c")
                        for p in range(2):
                            r = slice(p * DH, (p + 1) * DH)
                            for i in range(NT):
                                ins = pe.matmul(bank_of(f"oi{c}c", p)[r, i * DH:(i + 1) * DH], state[r, c % 2, i, :],
                                                ar[r, i, pr, 1, q * CH:(q + 1) * CH], start=True, stop=True)
                        ins.then_inc(unit_done, 1)
                begin(f"oo{pr}")
                for p in range(2):
                    pe.wait_ge(*evacuated(f"u{2 * pr + 1}c", p))
                for i in range(NT):
                    for p in range(2):
                        r = slice(p * DH, (p + 1) * DH)
                        u = p * NT + i
                        o = bank_of(f"oo{pr}", i // 3)[r, (i % 3) * P:(i % 3 + 1) * P]
                        pe.matmul(o, u_tm[:, u * DH:(u + 1) * DH], sc[:, u, 1, :], start=True, stop=False)
                        ins = pe.matmul(o, kbv_tm[:, 2, (2 * i + p) * DH:(2 * i + p + 1) * DH], sc[:, u, 3, :],
                                        start=False, stop=True)
                ins.then_inc(unit_done, 1)

        pe.wait_ge(sem("ident_in"), 16)
        pe.wait_ge(sem("vec_in"), VEC_DMAS * 16)
        pe.transpose(bank[0][:, 0:P], vec_rows, ident).then_inc(sem("table_full"), 1)
        to_fm("tm_ready", 1)
        fm_ready()
        def duplicate(v):
            name = f"dup{v}"
            if v == 0:
                pe.wait_ge(sem("cst_in"), 16)
                pe.wait_ge(sem("tables"), 2)
            begin(name)
            pe.wait_ge(*evacuated(("kc", "vc")[v]))
            for gp in range(2):
                for p in range(2):
                    ins = pe.matmul(bank_of(name, gp)[:, p * S:(p + 1) * S], C("dup")[:, p * P:(p + 1) * P],
                                    kcvT[:, v, gp, :], start=True, stop=True)
            ins.then_inc(unit_done, 1)

        def hidden_layer(v):
            name = f"hid{v}"
            begin(name)
            if v == 0:
                pe.wait_ge(sem("cmp_in"), 32)
            pe.wait_ge(*evacuated(f"dup{v}", 1))
            for l in range(CMP_BLOCK // 2):
                ins = pe.matmul(bank_of(name)[:, 0:4 * NCMP], cmp_w1[:, v, l, :],
                                blocks[:, v, l].rearrange("p g n -> p (g n)"),
                                start=(l == 0), stop=(l == CMP_BLOCK // 2 - 1))
            ins.then_inc(unit_done, 1)

        fm_unit("kc", fm), fm_unit("vc", fm)
        pe.wait_ge(sem("pos_in"), 48)
        pe.transpose(bank[3][:, 0:72], pos_rows[0:72, :], ident[0:72, 0:72]).then_inc(sem("table_full"), 1)
        fm_unit("q0", fm)
        duplicate(0)
        fm_unit("q1", fm)
        duplicate(1)
        fm_unit("q2", fm), fm_unit("ks", fm)
        hidden_layer(0)
        tm_unit("vs", fm)
        hidden_layer(1)
        fm_unit("kw", fm)
        pe.wait_ge(sem("small_in"), 16 * SMALL_DMAS)
        begin("kcb")
        pe.wait_ge(*evacuated("hid0"))
        for p in range(2):
            ins = pe.matmul(bank_of("kcb")[p * DH:(p + 1) * DH, 0:2 * NCMP], cmp_w2[:, 0:DH],
                            hid[:, 0, p * 30:(p + 1) * 30], start=True, stop=True)
        ins.then_inc(unit_done, 1)
        begin("vcb")
        pe.wait_ge(*evacuated("hid1"))
        for g in range(G):
            o = (g % 2) * 30 + (g // 2) * NCMP
            ins = pe.matmul(bank_of("vcb")[0:NCMP, g * DH:(g + 1) * DH], hid[:, 1, o:o + NCMP],
                            cmp_w2[:, DH:2 * DH], start=True, stop=True)
        ins.then_inc(unit_done, 1)
        tm_unit("vw", fm)
        fm_unit("gl", fm)
        pe.wait_ge(*evacuated("kcb"))
        pe.wait_ge(*evacuated("q2"))
        for p in range(2):
            begin(f"cs{p}")
            r = slice(p * DH, (p + 1) * DH)
            for qt in range(QT):
                for i in range(NT):
                    c = (qt * NT + i) * 16
                    ins = pe.matmul(bank_of(f"cs{p}")[:, c:c + NCMP], qT[r, i, qt * P:(qt + 1) * P],
                                    kcb[r, (i // R) * NCMP:(i // R + 1) * NCMP], start=True, stop=True)
            ins.then_inc(unit_done, 1)
        turn_narrow("gl", 3 * H)
        fm_unit("qm0", fm)
        to_fm("tm_ready", 2)
        pe.wait_ge(sem("pcmp_ready"), 1)
        for j in range(8):
            begin(f"pct{j}")
            p, qt, hf = j // 4, (j // 2) % 2, j % 2
            for a in range(3):
                ins = pe.transpose(bank_of(f"pct{j}")[0:NCMP, a * P:(a + 1) * P],
                                   s_cmp[:, p, qt, hf * 3 + a, 0:NCMP], ident)
            ins.then_inc(unit_done, 1)
        pe.wait_ge(*evacuated("vcb"))
        for j in range(4):
            p, qt = j // 2, j % 2
            begin(f"oc{j}")
            pe.wait_ge(*evacuated(f"pct{2 * j}"))
            pe.wait_ge(*evacuated(f"pct{2 * j + 1}"))
            for i in range(NT):
                g = 2 * (i // R) + p
                ins = pe.matmul(bank_of(f"oc{j}")[:, i * DH:(i + 1) * DH],
                                p_cmpT[0:NCMP, 2 * j + i // 3, (i % 3) * P:(i % 3 + 1) * P],
                                vcb[0:NCMP, g * DH:(g + 1) * DH], start=True, stop=True)
            ins.then_inc(unit_done, 1)
        for name in ("ks", "vs", "kw", "vw", "qm0"):
            pe.wait_ge(*evacuated(name))
        fm_ready()
        all_ready()

        def memory_unit(j):
            if j < len(MEM_UNITS):
                (tm_unit if MEM_UNITS[j].startswith("v") else fm_unit)(MEM_UNITS[j], mem_fm[int(MEM_UNITS[j][-1])])
            if j == 23:
                pe.wait_ge(*evacuated("kmem0")), pe.wait_ge(*evacuated("vmem0"))

        attention("nsa", memory_unit)
        to_fm("o_read", 28)
        fm_ready()
        for j in range(4):
            row_unit("wo0_", j, 4, fm)
        to_fm("tm_ready", 3)
        fm_ready()
        ffn("f0")

        to_fm("tm_ready", 4)
        fm_ready()
        for j in range(10):
            fm_unit(f"z{j}", fm)
        fm_unit("z10", fm)
        fm_unit("qm1", fm)
        pe.wait_ge(sem("lora_in"), 80)
        pe.wait_ge(sem("lora_ready"), 3)
        for n, r in (("w2", slice(0, DH)), ("a2", slice(DH, P))):
            for j in range(3):
                begin(f"{n}_{j}")
                for a in range(2):
                    i = 2 * j + a
                    ins = pe.matmul(bank_of(f"{n}_{j}")[:, a * S:(a + 1) * S], rw_wa2[r, i * P:(i + 1) * P],
                                    lora[r, 0, :], start=True, stop=True)
                ins.then_inc(unit_done, 1)
        for j in range(3):
            begin(f"g2_{j}")
            for a in range(2):
                i = 2 * j + a
                o = bank_of(f"g2_{j}")[:, a * S:(a + 1) * S]
                pe.matmul(o, rw_g2[:, i * P:(i + 1) * P], lora[:, 1, :], start=True, stop=False)
                ins = pe.matmul(o, rw_g2[0:32, MW + i * P:MW + (i + 1) * P], lora[0:32, 2, :], start=False, stop=True)
            ins.then_inc(unit_done, 1)

        def head_sums(name, src, ready, step):
            begin(name)
            for i in range(NT):
                pe.wait_ge(sem(ready), 1 + step * (i // 2))
                ins = pe.matmul(bank_of(name)[0:H, 0:S], C("head_sel")[:, i * H:(i + 1) * H], src[:, i, :],
                                start=(i == 0), stop=(i == NT - 1))
            ins.then_inc(unit_done, 1)

        def head_spread(tag):
            for j in range(3):
                begin(f"{tag}_{j}")
                for a in range(2):
                    i = 2 * j + a
                    ins = pe.matmul(bank_of(f"{tag}_{j}")[:, a * S:(a + 1) * S],
                                    head_back[0:H, i * P:(i + 1) * P], narrow[0:H, :], start=True, stop=True)
                ins.then_inc(unit_done, 1)

        head_sums("kn", kk_sq, "sumsrc_ready", 0)
        pe.wait_ge(sem("knorm_ready"), 1)
        head_spread("kb")
        pe.wait_ge(sem("sumsrc_ready"), 2)
        for j in range(3):
            begin(f"bs_{j}")
            pe.matmul(bank_of(f"bs_{j}")[:, :], C("head_ones"),
                      bonus[:, 2 * j:2 * j + 2, :].rearrange("p a t -> p (a t)"), start=True, stop=True).then_inc(unit_done, 1)
        pe.wait_ge(*evacuated("qm1"))
        attention("mem1")
        begin("crT")
        pe.wait_ge(sem("o_read"), 32)
        for a in range(2):
            for qt in range(QT):
                ins = pe.transpose(bank_of("crT")[:, a * S + qt * P:a * S + (qt + 1) * P],
                                   cross[:, qt, a * P:(a + 1) * P], ident)
        ins.then_inc(unit_done, 1)
        wkv()
        for a in range(2):
            pe.wait_ge(*evacuated("oo1", a))
        for j in range(3):
            begin(f"gm_{j}")
            pe.matmul(bank_of(f"gm_{j}")[:, :], C("head_ones"),
                      y_fm[:, 2 * j:2 * j + 2, :].rearrange("p a t -> p (a t)"), start=True, stop=True).then_inc(unit_done, 1)
        head_sums("gv", zt, "squares_ready", 1)
        pe.wait_ge(sem("rstd_ready"), 1)
        head_spread("gr")
        pe.wait_ge(*evacuated("crT"))
        for j in range(4):
            if j < 3:
                pe.wait_ge(sem("mix1_lo"), j + 1)
            row_unit("wo1_", j, 4, fm)
        to_fm("tm_ready", 5)
        fm_ready()
        ffn("f1")

        for j in range(2):
            begin(f"wsT{j}")
            pe.wait_ge(sem("ws_in"), 16)
            for a in range(4):
                ins = pe.transpose(bank_of(f"wsT{j}")[:, a * P:(a + 1) * P], ws_raw[:, 4 * j + a, :], ident)
            ins.then_inc(unit_done, 1)
        to_fm("tm_ready", 6)
        fm_ready()
        for name in ("sv", "su"):
            for j in range(4):
                tm_unit(f"{name}{j}", fm)
        fm_unit("sf", fm)
        for name in ("fq", "fk"):
            for j in range(4):
                fm_unit(f"{name}{j}", fm)
                if name == "fq" and j == 0:
                    turn_narrow("sf", NFH)
        for j in range(4):
            tm_unit(f"fv{j}", fm)
        begin("cc")
        pe.wait_ge(sem("logf_ready"), 1)
        o = bank_of("cc")
        pe.matmul(o[0:NFH, 0:P], logf[:, 0, :], C("tri"), start=True, stop=True)
        pe.matmul(o[0:NFH, P:S], logf[:, 0, :], C("ones"), start=True, stop=False)
        pe.matmul(o[0:NFH, P:S], logf[:, 1, :], C("tri"), start=False, stop=True).then_inc(unit_done, 1)
        pe.wait_ge(sem("vn_ready"), 1)
        for j in range(2):
            pe.wait_ge(*evacuated(f"wsT{j}"))
        for j in range(4):
            begin(f"sgu{j}")
            qt, half = j // 2, j % 2
            for a in range(4):
                g = 4 * half + a
                ins = pe.matmul(bank_of(f"sgu{j}")[:, a * P:(a + 1) * P], wsT[:, g, :],
                                v_n[:, qt, g * P:(g + 1) * P], start=True, stop=True)
            ins.then_inc(unit_done, 1)
        pe.wait_ge(*evacuated("cc"))
        for j in range(4):
            for name in ("fq", "fk", "fv"):
                pe.wait_ge(*evacuated(f"{name}{j}"))

        def gate_unit(j):
            if j < len(GATE_UNITS):
                tm_unit(GATE_UNITS[j], fm)

        attention("fox", gate_unit)
        to_fm("tm_ready", 7)
        fm_ready()
        for j in range(4):
            row_unit("wo2_", j, 4, fm)
        to_fm("tm_ready", 8)
        fm_ready()
        ffn("f2")

    @block.scalar
    def _(act):
        own = counter("act_step")
        tiles2 = lambda a: a.rearrange("p i t -> p (i t)")
        copy = ACT.Identity

        o, n = CAT["ident"]
        act.dma_start(cst[:, o:o + n], cst_d[:, o:o + n]).then_inc(sem("ident_in"), 16)
        act.wait_ge(sem("vec_zero"), 1)
        for dst, src in vec_loads[0::2]:
            act.dma_start(dst, src).then_inc(sem("vec_in"), 16)

        def squares(r, src):
            if last(own):
                act.wait_ge(*last(own))
            act.activation(sbuf_p, src[:, 0, :], ACT.Square, accum_out=ssq[:, r, 0:1]).then_inc(tick(own, "sq_act"), 1)

        def root(r):
            act.wait_ge(sem("ms_ready"), r + 1)
            act.activation(rms[:, r, :], ssq[:, r, :], ACT.Sqrt).then_inc(tick(own, "rt_ready"), 1)

        act.wait_ge(sem("x_in"), 16)
        squares(0, x_tm)
        root(0)
        for p in range(2):
            act.dma_start(pos_rows[0:2 * CMP_BLOCK, p * DH:(p + 1) * DH],
                          T["nsa_cmp_pos"][0].rearrange("v l d -> (v l) d")).then_inc(sem("pos_in"), 16)
        act.dma_start(pos_rows[64:72, :], T["b_spatial_2"][0]).then_inc(sem("pos_in"), 16)
        smalls = [
            (cmp_w2[:, 0:DH], T["nsa_cmp_w2"][0, 0]), (cmp_w2[:, DH:2 * DH], T["nsa_cmp_w2"][0, 1]),
            (gate_b, T["nsa_gate_b"].to_broadcast((P, 3 * H))),
            (b_forget, T["b_forget_2"].to_broadcast((P, NFH)))]
        for dst, src in smalls:
            act.dma_start(dst, src).then_inc(sem("small_in"), 16)
        assert o == 0
        act.dma_start(cst[:, n:], cst_d[:, n:CONSTANTS]).then_inc(sem("cst_in"), 16)

        fm_event = [0]

        def from_banks(outs):
            e = fm_event[0]
            fm_event[0] += 1
            for j in range(4):
                act.wait_ge(sem("fm_full"), 4 * e + j + 1)
                for k in (2 * j, 2 * j + 1):
                    for dst, gain in outs:
                        b = bank[4 + j][:, (k % 2) * S:(k % 2 + 1) * S]
                        if gain is None:
                            ins = act.activation(dst[0][:, k, :], b, copy)
                        else:
                            ins = act.activation(dst[0][:, k, :], b, copy, scale=V(*gain(k)))
                ins.then_inc(tick(own, "fm_hi"), 1)

        split_at = [0]

        def ahead(name):
            split_to(split_end(name))

        def split_to(end):
            while split_at[0] < end:
                m = split_at[0]
                split_at[0] += 1
                new = split_names[m]
                r, v = landed[new]
                act.wait_ge(slot_landed[r], v)
                if m >= SPLITS:
                    act.wait_ge(*filled(split_names[m - SPLITS]))
                for lo, hi in pieces(new):
                    act.activation(w_hi[:, (m % SPLITS) * SLOT + lo:(m % SPLITS) * SLOT + hi],
                                   ring[:, r * SLOT + lo:r * SLOT + hi], copy).then_inc(tick(own, "hi_ready"), 1)

        def evac(name, dst, func=copy, scale=1.0, src=None):
            act.wait_ge(*filled(name))
            act.activation(dst, bank_of(name)[:, :] if src is None else src, func, scale=scale).then_inc(freed(own, name), 1)

        def two(name):
            return bank_of(name)[:, :].rearrange("p (q c) -> p q c", q=2)

        def exps(n):
            kind, i = heads[n]
            act.wait_ge(sem("nmax_ready"), n + 1)
            if n >= 2:
                act.wait_ge(sem("pt_full"), n - 1)
            slope = SLOPES[i] if kind in ("sel", "win") else 1.0
            for qt, c, nk in head_parts(n)[4]:
                src = score_bank(n) if kind in ("mem0", "mem1") else sbuf_s[:, (n % 2) * 512:]
                o = (n % 2) * 512 + c
                ins = act.activation(sbuf_p[:, o:o + nk], src[:, c:c + nk], ACT.Exp, bias=nmax[:, n, qt:qt + 1],
                                     scale=slope,
                                     accum_out=rsum[:, n, qt:qt + 1])
            ins.then_inc(tick(own, "exp_done"), 1)

        def copy_pt(n):
            act.wait_ge(sem("pt_full"), n + 1)
            if n >= 2:
                act.wait_ge(sem("o_full"), n - 1)
            w = P * len(blocks_of(n))
            act.activation(sbuf_pt[:, (n % 2) * 512:(n % 2) * 512 + w], pt_bank[:, 0:w], copy).then_inc(tick(own, "pt_copied"), 1)

        def attention(which, between=None):
            st = STAGES[which]
            for n in range(st[0], st[-1] + 2):
                if n in st:
                    exps(n)
                if n - 1 in st:
                    copy_pt(n - 1)
                if between and n in st:
                    between(n - st[0])

        def high_hidden(tag, j):
            act.wait_ge(*evacuated(f"{tag}_in{j}"))
            act.activation(hT[0][:, j, :], hidden[:, j % 2, :], copy).then_inc(tick(own, "hidden_hi"), 1)

        def linear(names, outs):
            for name in names:
                ahead(name)
                if name in outs:
                    evac(name, *outs[name])

        def rows_ahead(tag):
            for j in range(3):
                ahead(f"{tag}_{j}")

        def ffn(tag, base):
            for j in range(FT):
                ahead(f"{tag}_in{j}")
                act.wait_ge(*filled(f"{tag}_in{j}"))
                if j >= 2:
                    act.wait_ge(*evacuated(f"{tag}_in{j - 2}"))
                act.activation(silu[:, j % 2, :], bank_of(f"{tag}_in{j}")[:, 0:S], ACT.Silu).then_inc(tick(own, "silu_ready"), 1)
                if j:
                    high_hidden(tag, j - 1)
            high_hidden(tag, FT - 1)
            for j in range(FT // 2 - 1):
                ahead(f"{tag}_out{j}")

        act.wait_ge(sem("tables"), 1)
        from_banks([(fm, lambda k: ("norm1", k))])

        def queries(j):
            ahead(f"q{j}")
            act.wait_ge(*filled(f"q{j}"))
            for a in range(2):
                i = 2 * j + a
                ins = act.activation(qT[:, i, :], bank_of(f"q{j}")[:, a * S:(a + 1) * S], copy,
                                     scale=C("q_scale")[:, i:i + 1])
            ins.then_inc(freed(own, f"q{j}"), 1)

        ahead("kc"), ahead("vc")
        act.wait_ge(sem("cst_in"), 16)
        for j in range(3):
            queries(j)
        linear(("ks",), {"ks": (tiles2(kselT),)})
        act.wait_ge(sem("mem_in"), 16)
        squares(1, tm)
        root(1)
        for v in range(2):
            if v:
                ahead("vs")
            act.wait_ge(*filled(f"hid{v}"))
            act.activation(hid[:, v, :], bank_of(f"hid{v}")[:, 0:4 * NCMP],
                           ACT.Gelu_apprx_tanh).then_inc(freed(own, f"hid{v}"), 1)
        ahead("kw")
        evac("kw", tiles2(kwinT))
        ahead("vw"), ahead("gl")
        evac("gl", narrow[0:3 * H], src=bank_of("gl")[0:3 * H, 0:S])
        act.wait_ge(sem("scmp_ready"), 1)
        sall = s_cmp.rearrange("p h q i n -> p (h q i) n")[:, :, 0:NCMP]
        act.activation(sall, sall, ACT.Exp).then_inc(tick(own, "ecmp_ready"), 1)
        ahead("qm0")
        evac("qm0", qmem, scale=DH ** -0.5)
        act.wait_ge(*evacuated("glT"))
        act.activation(gates, gates, ACT.Sigmoid).then_inc(tick(own, "gates_ready"), 1)
        for j in range(8):
            evac(f"pct{j}", p_cmpT[0:NCMP, j, :], src=bank_of(f"pct{j}")[0:NCMP, 0:384])
        from_banks([(mem_fm[l], lambda k, l=l: ("norm_mem", 8 * l + k)) for l in range(2)])

        def memory_unit(j):
            if j < len(MEM_UNITS):
                ahead(MEM_UNITS[j])
                if MEM_UNITS[j] == "kmem0":
                    evac("kmem0", kmem0)
                if MEM_UNITS[j] == "kmem1":
                    evac("kmem1", kmem1)

        attention("nsa", memory_unit)
        from_banks([(fm, None)])
        rows_ahead("wo0")
        act.wait_ge(*evacuated("wo0_0", 1))
        squares(2, x_tm)
        root(2)
        ahead("wo0_3")
        from_banks([(fm, lambda k: ("norm2", k))])
        ffn("f0", 0)
        act.wait_ge(*evacuated("f0_out0", 1))
        squares(3, x_tm)
        root(3)
        ahead("f0_out10")

        from_banks([(fm, lambda k: ("norm1", 8 + k))])
        zs = zshift[:, :].rearrange("p (b a t) -> p b a t", b=2, a=2)
        act.wait_ge(sem("zcol_ready"), 1)
        for j in range(11):
            ahead(f"z{j}")
            if j >= 2:
                act.wait_ge(sem("zmix_ready"), j - 1)
            if j < 10:
                evac(f"z{j}", zs[:, j % 2, :, 1:S + 1], src=two(f"z{j}"))
            else:
                evac("z10", zs[0:32, 0, 0, 1:S + 1], src=bank_of("z10")[0:32, 0:S])
        evac("qm1", qmem, scale=DH ** -0.5)
        act.wait_ge(sem("zmix_ready"), 11)
        act.activation(lora[0:DH, 0, :], lora[0:DH, 0, :], ACT.Tanh).then_inc(tick(own, "lora_ready"), 1)
        act.activation(lora[:, 1, :], lora[:, 1, :], ACT.Sigmoid).then_inc(tick(own, "lora_ready"), 1)
        act.activation(lora[0:32, 2, :], lora[0:32, 2, :], ACT.Sigmoid).then_inc(tick(own, "lora_ready"), 1)
        for n, dst, b0 in (("w2", sg, "rw_w0"), ("a2", iclr, "rw_a0")):
            for j in range(3):
                act.wait_ge(*filled(f"{n}_{j}"))
                act.activation(dst[:, 2 * j, :], bank_of(f"{n}_{j}")[:, 0:S], ACT.Sigmoid, bias=V(b0, 2 * j))
                act.activation(dst[:, 2 * j + 1, :], bank_of(f"{n}_{j}")[:, S:2 * S], ACT.Sigmoid,
                                        bias=V(b0, 2 * j + 1)).then_inc(freed(own, f"{n}_{j}"), 1)
        evac("kn", narrow[0:H, :], ACT.Sqrt, src=bank_of("kn")[0:H, 0:S])
        act.wait_ge(sem("csum_ready"), 1)
        flat = lambda a: a.rearrange("p i t -> p (i t)")
        act.activation(flat(e_in), flat(csum), ACT.Exp, scale=-C0).then_inc(tick(own, "exps_ready"), 1)
        act.activation(flat(e_neg), flat(csum), ACT.Exp, scale=C0).then_inc(tick(own, "exps_ready"), 1)
        act.wait_ge(sem("cexc_ready"), 1)
        act.activation(flat(sg), flat(sg), ACT.Exp, scale=-C0).then_inc(tick(own, "exps_ready"), 1)
        attention("mem1")
        act.wait_ge(*filled("crT"))
        act.activation(fm[0][:, 6:8, :], two("crT"), copy).then_inc(tick(own, "cross_hi"), 1)
        for pr in range(2):
            for w in range(3):
                evac(f"tr{pr}_{w}_1", kbv_tm[:, w, 384:768], src=bank_of(f"tr{pr}_{w}_1")[:, 0:384])
            for gi in range(3):
                evac(f"ti{pr}_{gi}", tms[gi].rearrange("p u t -> p (u t)"))
            for s in MERGES:
                for gi in range(3):
                    evac(f"e{pr}_{s}_{gi}", ems[gi].rearrange("p u t -> p (u t)"))
            for q in range(2):
                c = 2 * pr + q
                rq = slice(q * CH, (q + 1) * CH)
                act.wait_ge(*filled(f"u{c}c"))
                for p in range(2):
                    act.activation(u_tm[rq, p * 384:(p + 1) * 384], bank_of(f"u{c}c", p)[rq, 0:384], copy).then_inc(freed(own, f"u{c}c", p), 1)
                if c:
                    act.wait_ge(*filled(f"oi{c}c"))
                    act.wait_ge(sem("yzero_ready"), 1)
                    for p in range(2):
                        r = slice(p * DH, (p + 1) * DH)
                        act.activation(
                            y_fm[r, :, c * CH:(c + 1) * CH],
                            bank_of(f"oi{c}c", p)[r, 0:384].rearrange("p (i t) -> p i t", i=NT), copy).then_inc(freed(own, f"oi{c}c", p), 1)
        act.wait_ge(*filled("oo1"))
        split_to(split_no["wo1_0"] + 1)
        for j in range(3):
            act.wait_ge(*evacuated(f"gm_{j}"))
            act.activation(flat(zt[:, 2 * j:2 * j + 2, :]), flat(y_fm[:, 2 * j:2 * j + 2, :]),
                           ACT.Square).then_inc(tick(own, "squares_ready"), 1)
        split_to(split_no["wo1_1"] + 1)
        act.wait_ge(*evacuated("gv"))
        act.activation(narrow[0:H, :], narrow[0:H, :], ACT.Sqrt).then_inc(tick(own, "gstd_ready"), 1)
        for j in range(3):
            act.wait_ge(sem("mix1_ready"), j + 1)
            act.activation(fm[0][:, 2 * j:2 * j + 2, :], mix_fm[:, 2 * j:2 * j + 2, :], copy).then_inc(tick(own, "mix1_hi"), 1)
        rows_ahead("wo1")
        act.wait_ge(*evacuated("wo1_0", 1))
        squares(4, x_tm)
        root(4)
        ahead("wo1_3")
        from_banks([(fm, lambda k: ("norm2", 8 + k))])
        ffn("f1", FT)
        act.wait_ge(*evacuated("f1_out0", 1))
        squares(5, x_tm)
        root(5)

        act.wait_ge(sem("x2_ready"), 1)
        squares(6, x_tm)
        root(6)
        ahead("f1_out10")
        from_banks([(fm, lambda k: ("mix_pre_g_2", k))])
        part = lambda dst, j: dst[:, :, j * 256:(j + 1) * 256]
        for name, dst in (("sv", v_n), ("su", u_g)):
            for j in range(4):
                linear((f"{name}{j}",), {f"{name}{j}": (part(dst, j), ACT.Gelu_apprx_tanh, 1.0, two(f"{name}{j}"))})
                if name == "su" and j == 0:
                    act.wait_ge(sem("lnvar_ready"), 1)
                    act.activation(mv[:, 4:6], mv[:, 4:6], ACT.Sqrt).then_inc(tick(own, "lnstd_ready"), 1)
        ahead("sf")
        evac("sf", narrow[0:NFH], src=bank_of("sf")[0:NFH, 0:S])
        linear(("fq0",), {"fq0": (tiles2(q2[:, 0:2, :]), copy, P ** -0.5)})
        act.wait_ge(sem("fabs_ready"), 1)
        act.activation(tmpf[:, 1], tmpf[:, 1], ACT.Exp, scale=-1.0).then_inc(tick(own), 1)
        act.wait_ge(*last(own))
        act.activation(tmpf[:, 1], tmpf[:, 1], ACT.Ln, bias=1.0).then_inc(tick(own, "fln_ready"), 1)
        for j in range(1, 4):
            linear((f"fq{j}",), {f"fq{j}": (tiles2(q2[:, 2 * j:2 * j + 2, :]), copy, P ** -0.5)})
        for name in ("fk", "fv"):
            for j in range(4):
                ahead(f"{name}{j}")

        def gate(j):
            name = GATE_UNITS[j]
            dst = sga if name.startswith("ga") else sgb
            ahead(name)
            evac(name, part(dst, j % 4), ACT.Sigmoid, 1.0, two(name))

        attention("fox", gate)
        from_banks([(fm, None)])
        rows_ahead("wo2")
        act.wait_ge(*evacuated("wo2_0", 1))
        squares(7, u_g)
        root(7)
        act.wait_ge(sem("x3_ready"), 1)
        squares(8, x_tm)
        root(8)
        ahead("wo2_3")
        from_banks([(fm, lambda k: ("ffn_pre_g_2", k))])
        ffn("f2", 2 * FT)
        act.wait_ge(*evacuated("f2_out0", 1))
        squares(9, u_g)
        root(9)

    @block.vector
    def _(dve):
        own = counter("dve_step")
        flat = lambda a: a.rearrange("p i t -> p (i t)")

        def mean_square(r, src):
            dve.tensor_tensor_reduce(out=sbuf_s[:, :], in0=src[:, 1, :], in1=src[:, 1, :], scale=1.0, scalar=0.0,
                                              op0=ALU.mult, op1=ALU.add, accum_out=ssq[:, r, 1:2]).then_inc(tick(own), 1)
            dve.wait_ge(*last(own))
            dve.wait_ge(sem("sq_act"), r + 1)
            dve.tensor_scalar(ssq[:, r, :], ssq[:, r, :], 1.0 / D, EPS, ALU.mult, ALU.add).then_inc(tick(own, "ms_ready"), 1)

        def inverse(r):
            dve.wait_ge(sem("rt_ready"), r + 1)
            dve.reciprocal(rms[:, r, :], rms[:, r, :]).then_inc(tick(own), 1)
            dve.wait_ge(*last(own))

        def rms_norm(r, src, dst):
            mean_square(r, src)
            scale_rows(r, src, dst)

        def scale_rows(r, src, dst):
            inverse(r)
            for qt in range(QT):
                ins = dve.tensor_scalar(dst[:, qt, :], src[:, qt, :], rms[:, r, qt:qt + 1], None, ALU.mult)
            ins.then_inc(tick(own, "tm_ready"), 1)

        def rms_gain(r, src, dst, gain):
            mean_square(r, src)
            inverse(r)
            for qt in range(QT):
                ins = dve.scalar_tensor_tensor(out=dst[:, qt, :], in0=src[:, qt, :], scalar=rms[:, r, qt:qt + 1],
                                               in1=gains[:, GAIN[gain], :], op0=ALU.mult, op1=ALU.mult)
            return ins

        fm_event = [0]

        def from_banks(outs):
            e = fm_event[0]
            fm_event[0] += 1
            for j in range(4):
                dve.wait_ge(sem("fm_hi"), 4 * e + j + 1)
                for k in (2 * j, 2 * j + 1):
                    for dst, gain in outs:
                        b = bank[4 + j][:, (k % 2) * S:(k % 2 + 1) * S]
                        hi = dst[0][:, k, :].bitcast(F32)
                        if gain is None:
                            ins = dve.tensor_tensor(dst[1][:, k, :], b, hi, ALU.subtract)
                        else:
                            ins = dve.scalar_tensor_tensor(out=dst[1][:, k, :], in0=b, scalar=V(*gain(k)), in1=hi,
                                                           op0=ALU.mult, op1=ALU.subtract)
                ins.then_inc(tick(own, "fm_lo"), 1)

        split_at = [0]

        def ahead(name):
            split_to(split_end(name))

        def split_to(end):
            while split_at[0] < end:
                m = split_at[0]
                split_at[0] += 1
                new = split_names[m]
                r, _ = landed[new]
                for i, (lo, hi) in enumerate(pieces(new)):
                    dve.wait_ge(sem("hi_ready"), PIECES * m + i + 1)
                    c = slice((m % SPLITS) * SLOT + lo, (m % SPLITS) * SLOT + hi)
                    dve.tensor_tensor(w_lo[:, c], ring[:, r * SLOT + lo:r * SLOT + hi], w_hi[:, c].bitcast(F32),
                                      ALU.subtract).then_inc(tick(own, "lo_ready"), 1)

        def linear(names, outs):
            for name in names:
                ahead(name)
                if name in outs:
                    evac(name, *outs[name])

        def rows_ahead(tag):
            for j in range(3):
                ahead(f"{tag}_{j}")

        def evac(name, dst, src=None):
            dve.wait_ge(*filled(name))
            dve.tensor_copy(dst, bank_of(name)[:, :] if src is None else src).then_inc(freed(own, name), 1)

        def two(name):
            return bank_of(name)[:, :].rearrange("p (q c) -> p q c", q=2)

        def product_tile(final, i):
            if i == 0:
                dve.wait_ge(sem("tile0_done"), ROW_PRODUCTS.index(final) + 1)
            if i == 2:
                dve.wait_ge(*filled(final))

        def residual(tag, final):
            for i in range(4):
                product_tile(final, i)
                o = x_tm[:, i // 2, (i % 2) * 512:(i % 2 + 1) * 512]
                dve.tensor_tensor(o, bank_of(tag, i)[:, :], o, ALU.add).then_inc(freed(own, tag, i), 1)
            dve.wait_ge(*last(own))

        def maxima(n):
            kind, i = heads[n]
            dve.wait_ge(sem("scores_full"), n + 1)
            if kind in ("mem0", "mem1"):
                ins = dve.tensor_reduce(nmax[:, n, :], score_bank(n)[:, :].rearrange("p (q k) -> p q k", q=2),
                                        AX.X, ALU.max, negate=True)
                ins.then_inc(tick(own, "nmax_ready"), 1)
                return
            if n >= 2:
                dve.wait_ge(sem("exp_done"), n - 1)
            table, slope = (C("causal"), 1.0) if kind == "fox" else (C("dist"), SLOPES[i])
            for qt, c, nk in head_parts(n)[4]:
                o = (n % 2) * 512 + c
                dve.tensor_tensor_reduce(
                    out=sbuf_s[:, o:o + nk], in0=score_bank(n)[:, c:c + nk], in1=table[:, c:c + nk], scale=1.0,
                    scalar=-3e38, op0=ALU.add, op1=ALU.max, accum_out=nmax[:, n, qt:qt + 1]).then_inc(tick(own), 1)
            dve.wait_ge(*last(own))
            dve.tensor_scalar(nmax[:, n, :], nmax[:, n, :], -slope, None, ALU.mult).then_inc(tick(own, "nmax_ready"), 1)

        def finish(n):
            kind, i = heads[n]
            dve.wait_ge(sem("o_full"), n + 1)
            dve.reciprocal(coef[:, n, :], rsum[:, n, :]).then_inc(tick(own), 1)
            dve.wait_ge(*last(own))
            if kind in ("sel", "win"):
                br = 1 if kind == "sel" else 2
                dve.tensor_tensor(coef[:, n, :], coef[:, n, :], gates[:, :, br * H + i], ALU.mult).then_inc(tick(own), 1)
                dve.wait_ge(*last(own))
            for qt in range(QT):
                o = qt * P
                if kind in ("sel", "win"):
                    dst = tm[:, qt, i * DH:(i + 1) * DH]
                    ins = dve.scalar_tensor_tensor(out=dst, in0=o_bank(n)[:, o:o + DH], scalar=coef[:, n, qt:qt + 1],
                                                   in1=dst, op0=ALU.mult, op1=ALU.add)
                else:
                    w = P if kind == "fox" else DH
                    dst = {"mem0": tm[:, :, MW:], "mem1": cross, "fox": tm}[kind][:, qt, i * w:(i + 1) * w]
                    ins = dve.tensor_scalar(dst, o_bank(n)[:, o:o + w], coef[:, n, qt:qt + 1], None, ALU.mult)
            ins.then_inc(tick(own, "o_read"), 1)

        def attention(which, between=None):
            st = STAGES[which]
            lag = LAG[which]
            for n in range(st[0], st[-1] + lag + 2):
                if n in st:
                    maxima(n)
                if between and n in st:
                    between(n - st[0])
                if n - lag - 1 in st:
                    finish(n - lag - 1)
            dve.wait_ge(*last(own))

        def low_hidden(j, base):
            dve.wait_ge(sem("hidden_hi"), base + j + 1)
            dve.tensor_tensor(hT[1][:, j, :], hidden[:, j % 2, :], hT[0][:, j, :].bitcast(F32),
                              ALU.subtract).then_inc(tick(own, "hidden_lo"), 1)

        def ffn(tag, base):
            for j in range(FT):
                ahead(f"{tag}_in{j}")
                dve.wait_ge(sem("silu_ready"), base + j + 1)
                if last(own):
                    dve.wait_ge(*last(own))
                dve.tensor_tensor(hidden[:, j % 2, :], bank_of(f"{tag}_in{j}")[:, S:2 * S], silu[:, j % 2, :],
                                  ALU.mult).then_inc(freed(own, f"{tag}_in{j}"), 1)
                if j:
                    low_hidden(j - 1, base)
            low_hidden(FT - 1, base)
            for j in range(FT // 2 - 1):
                ahead(f"{tag}_out{j}")

        dve.wait_ge(sem("x_in"), 16)
        mean_square(0, x_tm)
        dve.wait_ge(sem("table_full"), 1)
        dve.tensor_copy(vec[:, :], bank[0][:, 0:P]).then_inc(tick(own, "tables"), 1)
        dve.wait_ge(*last(own))
        scale_rows(0, x_tm, tm)
        from_banks([(fm, lambda k: ("norm1", k))])

        def lay_blocks(v):
            for gp in range(2):
                dve.wait_ge(*filled(f"dup{v}"))
                rows16 = bank_of(f"dup{v}", gp)[:, :].rearrange("q (p m a b) -> q a p m b", p=2, a=8, b=2)
                for b in range(2):
                    r = slice(b * DH, (b + 1) * DH)
                    pos = posT[r, v * CMP_BLOCK:(v + 1) * CMP_BLOCK].rearrange("q (a b) -> q a b", b=2)[:, :, b]
                    for hf in range(2):
                        ls = slice(8 * hf, 8 * hf + 8)
                        dst = blocks[r, v, ls].rearrange("q a (p g) n -> q a p g n", p=2)[:, :, :, gp, :]
                        ins = dve.tensor_tensor(dst, rows16[r, :, :, hf:hf + NCMP, b],
                                                pos[:, ls].unsqueeze(2).unsqueeze(3).to_broadcast((DH, 8, 2, NCMP)), ALU.add)
                ins.then_inc(freed(own, f"dup{v}", gp), 1)

        linear(("kc", "vc"), {"kc": (flat(kcvT[:, 0]),), "vc": (flat(kcvT[:, 1]),)})
        dve.wait_ge(sem("table_full"), 2)
        dve.tensor_copy(posT, bank[3][:, 0:64]).then_inc(tick(own), 1)
        dve.tensor_copy(vecs2, bank[3][:, 64:72]).then_inc(tick(own, "tables"), 1)
        dve.wait_ge(*last(own))
        ahead("q0")
        lay_blocks(0)
        ahead("q1")
        lay_blocks(1)
        ahead("q2"), ahead("ks")
        dve.wait_ge(sem("mem_in"), 16)
        rms_norm(1, tm, tm)
        linear(("vs",), {"vs": (flat(vsel),)})
        ahead("kw")
        evac("kcb", kcb, bank_of("kcb")[:, 0:30])
        evac("vcb", vcb[0:NCMP, :], bank_of("vcb")[0:NCMP, 0:256])
        linear(("vw",), {"vw": (flat(vwin),)})
        ahead("gl")
        sv = s_cmp.rearrange("p h q i n -> p (h q i) n")
        for p in range(2):
            dve.wait_ge(*filled(f"cs{p}"))
            for qt in range(QT):
                ins = dve.tensor_tensor(
                    s_cmp[:, p, qt, :, 0:NCMP],
                    bank_of(f"cs{p}")[:, qt * 96:(qt + 1) * 96].rearrange("p (u n) -> p u n", n=16)[:, :, 0:NCMP],
                    C("cmp_dist")[:, qt * 16:qt * 16 + NCMP].unsqueeze(1).to_broadcast((P, NT, NCMP)), ALU.add)
            ins.then_inc(freed(own, f"cs{p}"), 1)
        dve.wait_ge(*last(own))
        dve.tensor_reduce(m_cmp, sv[:, :, 0:NCMP], AX.X, ALU.max).then_inc(tick(own), 1)
        dve.wait_ge(*last(own))
        dve.tensor_tensor(sv[:, :, 0:NCMP], sv[:, :, 0:NCMP],
                                     m_cmp.unsqueeze(2).to_broadcast((P, 24, NCMP)), ALU.subtract).then_inc(tick(own), 1)
        dve.wait_ge(*last(own))
        dve.tensor_tensor(sv[:, :, 0:NCMP], sv[:, :, 0:NCMP],
                          C("slopes").unsqueeze(2).to_broadcast((P, 24, NCMP)), ALU.mult).then_inc(tick(own, "scmp_ready"), 1)
        dve.wait_ge(*filled("glT"))
        dve.wait_ge(sem("small_in"), 16 * SMALL_DMAS)
        dve.tensor_tensor(gates, two("glT")[:, :, 0:3 * H], gate_b.unsqueeze(1).to_broadcast((P, QT, 3 * H)),
                          ALU.add).then_inc(freed(own, "glT"), 1)
        dve.wait_ge(sem("ecmp_ready"), 1)
        dve.tensor_reduce(c_cmp, sv[:, :, 0:NCMP], AX.X, ALU.add).then_inc(tick(own), 1)
        dve.wait_ge(*last(own))
        mask = C("cmp_mask").rearrange("p (q n) -> p q n", q=QT)
        for p in range(2):
            for qt in range(QT):
                v = s_cmp[:, p, qt, :, 0:NCMP]
                ins = dve.tensor_tensor(v, v, mask[:, qt, 0:NCMP].unsqueeze(1).to_broadcast((P, NT, NCMP)), ALU.mult)
        ins.then_inc(tick(own, "pcmp_ready"), 1)
        ahead("qm0")
        dve.reciprocal(c_cmp, c_cmp).then_inc(tick(own), 1)
        dve.wait_ge(*last(own))
        dve.wait_ge(sem("gates_ready"), 1)
        cc4 = c_cmp.rearrange("p (h q g r) -> p h q g r", h=2, q=QT, g=2)
        gc = gates[:, :, 0:H].rearrange("p q (g h r) -> p h q g r", g=2, h=2)
        for p in range(2):
            dve.tensor_tensor(cc4[:, p], cc4[:, p], gc[:, p], ALU.mult).then_inc(tick(own), 1)
        dve.wait_ge(*last(own))
        from_banks([(mem_fm[l], lambda k, l=l: ("norm_mem", 8 * l + k)) for l in range(2)])
        for j in range(4):
            p, qt = divmod(j, 2)
            dve.wait_ge(*filled(f"oc{j}"))
            for gp in range(2):
                base = (2 * gp + p) * R * DH
                ins = dve.tensor_tensor(
                    tm[:, qt, base:base + R * DH].rearrange("p (r d) -> p r d", r=R),
                    bank_of(f"oc{j}")[:, gp * R * DH:(gp + 1) * R * DH].rearrange("p (r d) -> p r d", r=R),
                    cc4[:, p, qt, gp].unsqueeze(2).to_broadcast((P, R, DH)), ALU.mult)
            ins.then_inc(freed(own, f"oc{j}"), 1)
        dve.wait_ge(*last(own))

        def memory_unit(j):
            if j < len(MEM_UNITS):
                linear((MEM_UNITS[j],), {"vmem0": (vmem0,), "vmem1": (vmem1,)})

        attention("nsa", memory_unit)
        from_banks([(fm, None)])
        rows_ahead("wo0")
        residual("wo0_0", "wo0_3")
        rms_norm(2, x_tm, tm)
        ahead("wo0_3")
        from_banks([(fm, lambda k: ("norm2", k))])
        ffn("f0", 0)
        residual("f0_out0", f"f0_out{FT // 2 - 1}")
        rms_norm(3, x_tm, tm)
        ahead("f0_out10")

        zs = zshift[:, :].rearrange("p (b a t) -> p b a t", b=2, a=2)
        dve.memset(zs[:, :, :, 0:1], 0.0).then_inc(tick(own, "zcol_ready"), 1)
        dve.wait_ge(*last(own))
        from_banks([(fm, lambda k: ("norm1", 8 + k))])
        zd = zdelta[:, :].rearrange("p (a t) -> p a t", a=2)
        dsts = [r_fm[:, i, :] for i in range(NT)] + [kraw[:, i, :] for i in range(NT)] + \
               [v_fm[:, i, :] for i in range(NT)] + [lora[:, i, :] for i in range(3)]
        for j in range(11):
            ahead(f"z{j}")
            dve.wait_ge(*evacuated(f"z{j}"))
            z = zs[:, j % 2]
            rows = slice(0, P) if j < 10 else slice(0, 32)
            n = 2 if j < 10 else 1
            dve.tensor_tensor(zd[rows, 0:n, :], z[rows, 0:n, 0:S], z[rows, 0:n, 1:S + 1], ALU.subtract).then_inc(tick(own), 1)
            dve.wait_ge(*last(own))
            for a in range(n):
                i = 2 * j + a
                mu = V("rw_mu", i) if j < 10 else vec[0:32, MU_LAST:MU_LAST + 1]
                ins = dve.scalar_tensor_tensor(out=dsts[i][rows], in0=zd[rows, a, :], scalar=mu,
                                               in1=z[rows, a, 1:S + 1], op0=ALU.mult, op1=ALU.add)
            ins.then_inc(tick(own, "zmix_ready"), 1)
            dve.wait_ge(*last(own))
        dve.wait_ge(*filled("qm1"))
        for i in range(NT):
            dve.tensor_scalar(kk[:, i, :], kraw[:, i, :], V("rw_k_k", i), None, ALU.mult).then_inc(tick(own), 1)
        dve.wait_ge(*last(own))
        dve.tensor_tensor(kk_sq, kk, kk, ALU.mult).then_inc(tick(own, "sumsrc_ready"), 1)
        for j in range(3):
            dve.wait_ge(*evacuated(f"w2_{j}"))
            for i in (2 * j, 2 * j + 1):
                ins = dve.tensor_tensor_scan(csum[:, i, :], C("chunk_keep"), sg[:, i, :], 0.0, ALU.mult, ALU.add)
        ins.then_inc(tick(own, "csum_ready"), 1)
        for j in range(3):
            evac(f"g2_{j}", g_fm[:, 2 * j:2 * j + 2, :].rearrange("p a t -> p (a t)"))
        dve.wait_ge(*evacuated("kn"))
        dve.tensor_scalar(narrow[0:H, :], narrow[0:H, :], 1e-12, None, ALU.max).then_inc(tick(own), 1)
        dve.wait_ge(*last(own))
        dve.reciprocal(narrow[0:H, :], narrow[0:H, :]).then_inc(tick(own, "knorm_ready"), 1)
        for j in range(3):
            dve.wait_ge(*filled(f"kb_{j}"))
            part = flat(kk[:, 2 * j:2 * j + 2, :])
            dve.scalar_tensor_tensor(out=part, in0=part, scalar=-1.0, in1=bank_of(f"kb_{j}")[:, :],
                                     op0=ALU.mult, op1=ALU.mult).then_inc(freed(own, f"kb_{j}"), 1)
        dve.wait_ge(sem("exps_ready"), 3)
        for i in range(NT):
            dve.tensor_scalar(csum[:, i, :], iclr[:, i, :], 1.0, V("rw_k_a", i), ALU.subtract, ALU.mult).then_inc(tick(own), 1)
        dve.wait_ge(*last(own))
        dve.scalar_tensor_tensor(out=flat(kraw), in0=flat(csum), scalar=1.0, in1=flat(kraw),
                                          op0=ALU.add, op1=ALU.mult).then_inc(tick(own), 1)
        dve.wait_ge(*last(own))
        for i in range(NT):
            ins = dve.scalar_tensor_tensor(out=bonus[:, i, :], in0=r_fm[:, i, :], scalar=V("rw_r_k", i),
                                           in1=kraw[:, i, :], op0=ALU.mult, op1=ALU.mult)
        ins.then_inc(tick(own, "sumsrc_ready"), 1)
        dve.scalar_tensor_tensor(out=flat(b_fm), in0=flat(kk), scalar=-1.0, in1=flat(iclr),
                                          op0=ALU.mult, op1=ALU.mult).then_inc(tick(own), 1)
        dve.wait_ge(*last(own))
        dve.tensor_tensor(flat(b_fm), flat(b_fm), flat(e_neg), ALU.mult)
        dve.tensor_tensor(flat(k_fm), flat(kraw), flat(e_neg), ALU.mult)
        by_pair = lambda a: a.rearrange("p i (c t) -> p i c t", c=2)
        dve.tensor_tensor(ar[:, :, :, 0, :], by_pair(kk), by_pair(sg), ALU.mult)
        dve.tensor_tensor(ar[:, :, :, 1, :], by_pair(r_fm), by_pair(e_in), ALU.mult).then_inc(tick(own, "wkv_ready"), 1)
        dve.tensor_copy(p_end, e_in.rearrange("p i (c t) -> p i c t", t=CH)[:, :, :, CH - 1]).then_inc(tick(own), 1)
        dve.wait_ge(*last(own))
        dve.memset(y_fm[:, :, 0:CH], 0.0).then_inc(tick(own, "yzero_ready"), 1)
        for j in range(3):
            dve.wait_ge(*filled(f"bs_{j}"))
            t = slice(2 * j, 2 * j + 2)
            dve.tensor_tensor(bonus[:, t, :], two(f"bs_{j}"), v_fm[:, t, :], ALU.mult).then_inc(freed(own, f"bs_{j}"), 1)
        attention("mem1")
        dve.wait_ge(sem("cross_hi"), 1)
        dve.tensor_tensor(fm[1][:, 6:8, :], two("crT"), fm[0][:, 6:8, :].bitcast(F32),
                          ALU.subtract).then_inc(freed(own, "crT"), 1)
        wmask = C("wkv_mask").unsqueeze(1).to_broadcast((P, 2, S))
        for pr in range(2):
            tok = slice(pr * P, (pr + 1) * P)
            for w in range(3):
                evac(f"tr{pr}_{w}_0", kbv_tm[:, w, 0:384], src=bank_of(f"tr{pr}_{w}_0")[:, 0:384])
            for u in range(H):
                dve.wait_ge(*filled(f"sc{pr}_{u}"))
                dve.tensor_tensor(sc[:, u].rearrange("p (c b) t -> p c (b t)", c=2), two(f"sc{pr}_{u}"),
                                           wmask, ALU.mult).then_inc(freed(own, f"sc{pr}_{u}"), 1)
            dve.wait_ge(*last(own))
            for gi in range(3):
                us = slice(4 * gi, 4 * gi + 4)
                dve.tensor_tensor(tt[:, us, :], sc[:, us, 0, :],
                                           C("merge1").unsqueeze(1).to_broadcast((P, 4, P)), ALU.mult).then_inc(tick(own), 1)
                dve.wait_ge(*last(own))
                dve.tensor_tensor(tt[:, us, :], tt[:, us, :],
                                             ident.unsqueeze(1).to_broadcast((P, 4, P)), ALU.add).then_inc(tick(own, "tt_init"), 1)
            for p in range(2):
                evac(f"y0{pr}_{p}", y0[:, p * 384:(p + 1) * 384], src=bank_of(f"y0{pr}_{p}")[:, 0:384])
            for s in MERGES:
                for gi in range(3):
                    name = f"t{pr}_{s}_{gi}"
                    dve.wait_ge(*filled(name))
                    us = slice(4 * gi, 4 * gi + 4)
                    v4 = lambda b: b[:, :].rearrange("p (u t) -> p u t", u=4)
                    dve.tensor_tensor(tt[:, us, :], v4(bank_of(name, 0)), tt[:, us, :], ALU.add).then_inc(freed(own, name, 0), 1)
                    if s < 32:
                        dve.tensor_tensor(tms[gi], v4(bank_of(name, 1)), tms[gi], ALU.add).then_inc(freed(own, name, 1), 1)
                dve.wait_ge(*last(own))
            for q in range(2):
                c = 2 * pr + q
                rq = slice(q * CH, (q + 1) * CH)
                if c:
                    dve.wait_ge(*filled(f"z{c}c"))
                    for p in range(2):
                        y = y0[rq, p * 384:(p + 1) * 384]
                        dve.tensor_tensor(y, bank_of(f"z{c}c", p)[rq, 0:384], y, ALU.add).then_inc(freed(own, f"z{c}c", p), 1)
                if c < 3:
                    dve.wait_ge(*filled(f"h{c}c"))
                    new = state[:, (c + 1) % 2]
                    h = bank_of(f"h{c}c")[:, 0:384].rearrange("p (i v) -> p i v", i=NT)
                    decay = p_end[:, :, c].unsqueeze(2).to_broadcast((P, NT, DH))
                    if c:
                        dve.tensor_tensor(new, h, state[:, c % 2], ALU.add).then_inc(freed(own, f"h{c}c"), 1)
                        dve.wait_ge(*last(own))
                        dve.tensor_tensor(new, new, decay, ALU.mult).then_inc(tick(own, "state_ready"), 1)
                    else:
                        dve.tensor_tensor(new, h, decay, ALU.mult).then_inc(freed(own, f"h{c}c"), 1)
            dve.wait_ge(*filled(f"oo{pr}"))
            for c in (2 * pr, 2 * pr + 1):
                if c:
                    for p in range(2):
                        dve.wait_ge(*evacuated(f"oi{c}c", p))
            for a in range(2):
                y = y_fm[:, 3 * a:3 * a + 3, tok]
                dve.tensor_tensor(y, bank_of(f"oo{pr}", a)[:, 0:384].rearrange("p (i t) -> p i t", i=3), y,
                                           ALU.add).then_inc(freed(own, f"oo{pr}", a), 1)
        dve.wait_ge(*last(own))
        for j in range(3):
            dve.wait_ge(*filled(f"gm_{j}"))
            t = slice(2 * j, 2 * j + 2)
            dve.scalar_tensor_tensor(out=flat(y_fm[:, t, :]), in0=bank_of(f"gm_{j}")[:, :],
                                              scalar=-1.0 / DH, in1=flat(y_fm[:, t, :]), op0=ALU.mult, op1=ALU.add).then_inc(freed(own, f"gm_{j}"), 1)
        split_to(split_no["wo1_0"] + 1)
        dve.wait_ge(*filled("gv"))
        dve.tensor_scalar(narrow[0:H, :], bank_of("gv")[0:H, 0:S], 1.0 / DH, GN_EPS,
                          ALU.mult, ALU.add).then_inc(freed(own, "gv"), 1)
        dve.wait_ge(sem("gstd_ready"), 1)
        dve.reciprocal(narrow[0:H, :], narrow[0:H, :]).then_inc(tick(own, "rstd_ready"), 1)
        dve.wait_ge(sem("bonus_ready"), 1)
        for j in range(3):
            dve.wait_ge(*filled(f"gr_{j}"))
            for i in (2 * j, 2 * j + 1):
                ins = dve.scalar_tensor_tensor(out=y_fm[:, i, :], in0=bank_of(f"gr_{j}")[:, (i % 2) * S:(i % 2 + 1) * S],
                                               scalar=V("rw_lnx_w", i), in1=y_fm[:, i, :], op0=ALU.mult, op1=ALU.mult)
            ins.then_inc(freed(own, f"gr_{j}"), 1)
            dve.wait_ge(*last(own))
            ts = slice(2 * j, 2 * j + 2)
            dve.tensor_tensor(y_fm[:, ts, :], y_fm[:, ts, :], bonus[:, ts, :], ALU.add).then_inc(tick(own), 1)
            dve.wait_ge(*last(own))
            dve.tensor_tensor(mix_fm[:, ts, :], y_fm[:, ts, :], g_fm[:, ts, :], ALU.mult).then_inc(tick(own, "mix1_ready"), 1)
        for j in range(3):
            dve.wait_ge(sem("mix1_hi"), j + 1)
            ts = slice(2 * j, 2 * j + 2)
            dve.tensor_tensor(fm[1][:, ts, :], mix_fm[:, ts, :], fm[0][:, ts, :].bitcast(F32),
                              ALU.subtract).then_inc(tick(own, "mix1_lo"), 1)
        split_to(split_no["wo1_1"] + 1)
        rows_ahead("wo1")
        residual("wo1_0", "wo1_3")
        rms_norm(4, x_tm, tm)
        ahead("wo1_3")
        from_banks([(fm, lambda k: ("norm2", 8 + k))])
        ffn("f1", FT)
        residual("f1_out0", f"f1_out{FT // 2 - 1}")

        dve.wait_ge(sem("gains_in"), 16 * len(GAIN))
        rms_gain(5, x_tm, x_tm, "final_norm").then_inc(tick(own, "x2_ready"), 1)
        dve.wait_ge(*last(own))
        for j in range(2):
            dve.wait_ge(*filled(f"wsT{j}"))
            dve.tensor_tensor(wsT[:, 4 * j:4 * j + 4, :],
                                       bank_of(f"wsT{j}")[:, :].rearrange("p (g t) -> p g t", g=4),
                                       C("tri").unsqueeze(1).to_broadcast((P, 4, P)), ALU.mult).then_inc(freed(own, f"wsT{j}"), 1)
        rms_norm(6, x_tm, tm)
        ahead("f1_out10")
        from_banks([(fm, lambda k: ("mix_pre_g_2", k))])
        for j in range(4):
            ahead(f"sv{j}")
            dve.wait_ge(*evacuated(f"sv{j}"))
        ahead("su0")
        bnv = bn.rearrange("p (q a s) -> p q a s", q=2, a=2)
        mvv = mv[:, 0:4].rearrange("p (q s) -> p q s", q=2)
        for qt in range(QT):
            for a in range(2):
                dve.bn_stats(bnv[:, qt, a, :], v_n[:, qt, a * 512:(a + 1) * 512]).then_inc(tick(own), 1)
        dve.wait_ge(*last(own))
        for qt in range(QT):
            dve.bn_aggr(mvv[:, qt, :], bnv[:, qt].rearrange("p a s -> p (a s)")).then_inc(tick(own), 1)
        dve.wait_ge(*last(own))
        dve.tensor_scalar(mv[:, 4:6], mvv[:, :, 1], EPS, None, ALU.add).then_inc(tick(own, "lnvar_ready"), 1)
        dve.wait_ge(sem("lnstd_ready"), 1)
        dve.reciprocal(mv[:, 4:6], mv[:, 4:6]).then_inc(tick(own), 1)
        dve.wait_ge(*last(own))
        for qt in range(QT):
            dve.tensor_scalar(v_n[:, qt, :], v_n[:, qt, :], mvv[:, qt, 0:1], mv[:, 4 + qt:5 + qt],
                                       ALU.subtract, ALU.mult).then_inc(tick(own), 1)
        dve.wait_ge(*last(own))
        gsg = gains[:, GAIN["sgu_norm_g_2"], :].unsqueeze(1).to_broadcast((P, QT, D))
        dve.tensor_tensor(v_n, v_n, gsg, ALU.mult).then_inc(tick(own, "vn_ready"), 1)
        for j in range(1, 4):
            ahead(f"su{j}")
        ahead("sf")
        ahead("fq0")
        dve.wait_ge(*filled("sfT"))
        dve.tensor_tensor(tmpf[:, 0], two("sfT")[:, :, 0:NFH],
                                   b_forget.unsqueeze(1).to_broadcast((P, QT, NFH)), ALU.add).then_inc(freed(own, "sfT"), 1)
        dve.wait_ge(*last(own))
        dve.tensor_scalar(tmpf[:, 2], tmpf[:, 0], -1.0, None, ALU.mult).then_inc(tick(own), 1)
        dve.wait_ge(*last(own))
        dve.tensor_tensor(tmpf[:, 1], tmpf[:, 0], tmpf[:, 2], ALU.max).then_inc(tick(own, "fabs_ready"), 1)
        dve.tensor_scalar(tmpf[:, 0], tmpf[:, 0], 0.0, None, ALU.min).then_inc(tick(own), 1)
        dve.wait_ge(sem("fln_ready"), 1)
        dve.wait_ge(*last(own))
        dve.tensor_tensor(logf, tmpf[:, 0], tmpf[:, 1], ALU.subtract).then_inc(tick(own, "logf_ready"), 1)
        dve.tensor_copy(sel[0:NFH], ident[0:NFH, 0:NFH].unsqueeze(2).to_broadcast((NFH, NFH, P))).then_inc(tick(own), 1)
        for j in range(1, 4):
            ahead(f"fq{j}")
        for j in range(4):
            linear((f"fk{j}",), {f"fk{j}": (flat(k2[:, 2 * j:2 * j + 2, :]),)})
        for j in range(4):
            linear((f"fv{j}",), {f"fv{j}": (v_a[:, :, j * 256:(j + 1) * 256], two(f"fv{j}"))})
        dve.wait_ge(*filled("cc"))
        dve.tensor_scalar(ccum[0:NFH, :], bank_of("cc")[0:NFH, 0:S], -1.0, None, ALU.mult).then_inc(freed(own, "cc"), 1)
        for j in range(4):
            dve.wait_ge(*evacuated(f"su{j}"))
        for j in range(4):
            dve.wait_ge(*filled(f"sgu{j}"))
            qt, half = divmod(j, 2)
            for a in range(4):
                g = 4 * half + a
                u = u_g[:, qt, g * P:(g + 1) * P]
                ins = dve.scalar_tensor_tensor(out=u, in0=bank_of(f"sgu{j}")[:, a * P:(a + 1) * P],
                                               scalar=vecs2[:, g:g + 1], in1=u, op0=ALU.add, op1=ALU.mult)
            ins.then_inc(freed(own, f"sgu{j}"), 1)
        attention("fox", lambda j: ahead(GATE_UNITS[j]))
        for j in range(8):
            dve.wait_ge(*evacuated(GATE_UNITS[j]))
        dve.tensor_tensor(u_g, u_g, sga, ALU.mult).then_inc(tick(own), 1)
        dve.tensor_tensor(tm, tm, sgb, ALU.mult).then_inc(tick(own), 1)
        dve.wait_ge(*last(own))
        dve.tensor_tensor(tm, tm, u_g, ALU.add).then_inc(tick(own, "tm_ready"), 1)
        from_banks([(fm, None)])

        def product_out(tag, final):
            for i in range(4):
                product_tile(final, i)
                dve.tensor_copy(u_g[:, i // 2, (i % 2) * 512:(i % 2 + 1) * 512], bank_of(tag, i)[:, :]).then_inc(freed(own, tag, i), 1)
            dve.wait_ge(*last(own))

        rows_ahead("wo2")
        product_out("wo2_0", "wo2_3")
        rms_gain(7, u_g, u_g, "mix_post_g_2").then_inc(tick(own), 1)
        dve.wait_ge(*last(own))
        dve.tensor_tensor(x_tm, x_tm, u_g, ALU.add).then_inc(tick(own, "x3_ready"), 1)
        dve.wait_ge(*last(own))
        rms_norm(8, x_tm, tm)
        ahead("wo2_3")
        from_banks([(fm, lambda k: ("ffn_pre_g_2", k))])
        ffn("f2", 2 * FT)
        product_out("f2_out0", f"f2_out{FT // 2 - 1}")
        rms_gain(9, u_g, u_g, "ffn_post_g_2").then_inc(tick(own), 1)
        dve.wait_ge(*last(own))
        dve.tensor_tensor(tm, u_g, x_tm, ALU.add).then_inc(tick(own, "y_done"), 1)


INPUTS = [
    "x", "mem", "norm1", "norm_mem", "w_mem_kv", "w_o", "norm2", "w_ffn_in", "w_ffn_out", "nsa_w_in", "nsa_gate_b",
    "nsa_cmp_pos", "nsa_cmp_w1", "nsa_cmp_w2", "rw_w_in", "rw_mu", "rw_w0", "rw_w2", "rw_a0", "rw_a2", "rw_g2",
    "rw_k_k", "rw_k_a", "rw_r_k", "rw_lnx_w", "rw_lnx_b", "final_norm", "mix_pre_g_2", "w_in_2", "b_forget_2",
    "sgu_norm_g_2", "w_spatial_2", "b_spatial_2", "w_out_2", "mix_post_g_2", "ffn_pre_g_2", "w_gate_2", "w_up_2",
    "w_down_2", "ffn_post_g_2"]


def kernel(**inputs):
    import numpy as _np
    import concourse.bacc as _bacc
    from concourse import mybir as _mybir
    from concourse.bass_utils import run_bass_kernel_spmd as _run

    nc = _bacc.Bacc("TRN2", target_bir_lowering=False, num_devices=1)
    arrays, tensors = {}, {}
    for name in INPUTS:
        a = _np.ascontiguousarray(inputs[name])
        arrays[f"in_{name}"] = a
        tensors[name] = nc.dram_tensor(f"in_{name}", a.shape, _mybir.dt.from_np(a.dtype), kind="ExternalInput").ap()
    constants = shape_constants()[1]
    arrays["shape_constants"] = constants
    tensors["shape_constants"] = nc.dram_tensor("shape_constants", constants.shape, F32, kind="ExternalInput").ap()
    out = nc.dram_tensor("out_0", (1, S, D), F32, kind="ExternalOutput").ap()
    kernel_program(nc, tensors, out)
    r = _run(nc, [arrays], core_ids=[0])
    return r.results[0]["out_0"]
```
